# Optimizing a Trainium2 kernel written in Bass

```python
import math
import jax
import jax.numpy as jnp
from jax import lax
import numpy as np

D_MODEL = 1024
BATCH = 1
SEQ = 256
DEPTH = 2

F32 = jnp.float32
QB = 128
NEG = -1e30
BIG = 1e9
LN_EPS = 1e-5
RMS_EPS = 1e-6

ALPHA = (2 * DEPTH) ** 0.25
BETA = (8 * DEPTH) ** -0.25

N_BUCKETS = 32
REL_MAX_DIST = 2048

H_A = 12
NOPE = 64
ROPE_DIM = 32
MLA_V = 64
Q_LORA = 256
KV_LORA = 128
ROPE_THETA = 10000.0

DIL_PAIRS = ((128, 1), (512, 4), (2048, 16))
H_B_GROUP = 4
H_B = H_B_GROUP * 3
HD_B = 64

H_C = 8
G_C = 2
R_C = 4
DK_C = 64
DV_C = 64
CMP_LEN = 32
CMP_STRIDE = 16
CMP_HID = 64
SEL_BLOCK = 64
SEL_TOP = 16
SEL_QB = 64
WIN = 512

H_D = 4
DD = 64

REL_B0 = 0
REL_C0 = H_B
REL_D0 = H_B + H_C
N_REL_HEADS = H_B + H_C + H_D

N_EXPERTS = 64
TOP_K = 8
N_EXPERT_GROUPS = 8
TOPK_GROUPS = 4
D_EXPERT = 256
D_SHARED = 256
ROUTED_SCALE = 2.5
EBLK = 128

AB_SIZES = (Q_LORA, KV_LORA, ROPE_DIM, H_B * HD_B, H_B * HD_B, H_B * HD_B)
AB_IN = sum(AB_SIZES)
AB_OUT = H_A * MLA_V + H_B_GROUP * HD_B
CD_SIZES = (H_C * DK_C,) + (G_C * DK_C, G_C * DV_C) * 3 + (3 * H_C, H_D * 2 * DD, H_D * 2 * DD, H_D * 2 * DD)
CD_IN = sum(CD_SIZES)
CD_OUT = H_C * DV_C + H_D * 2 * DD

kernel_name = 'hybrid_mla_dilated_nsa_diff_moe_deepnorm'

def split_cols(h, sizes):
    out, start = [], 0
    for n in sizes:
        out.append(h[..., start:start + n])
        start += n
    return out

def layer_norm(x, g, b):
    xf = x.astype(F32)
    mu = xf.mean(-1, keepdims=True)
    var = jnp.square(xf - mu).mean(-1, keepdims=True)
    return ((xf - mu) * lax.rsqrt(var + LN_EPS) * g + b).astype(x.dtype)

def rms_norm(x, g):
    xf = x.astype(F32)
    return (xf * lax.rsqrt(jnp.square(xf).mean(-1, keepdims=True) + RMS_EPS) * g).astype(x.dtype)

def rope(t, pos):
    half = t.shape[-1] // 2
    freqs = ROPE_THETA ** (-jnp.arange(half, dtype=F32) / half)
    ang = pos.astype(F32)[:, None] * freqs
    cos = jnp.cos(ang)[:, None, :]
    sin = jnp.sin(ang)[:, None, :]
    t1 = t[..., :half].astype(F32)
    t2 = t[..., half:].astype(F32)
    return jnp.concatenate([t1 * cos - t2 * sin, t1 * sin + t2 * cos], -1).astype(t.dtype)

def rel_bucket(dist):
    n = jnp.maximum(dist, 0)
    exact = N_BUCKETS // 2
    log_ratio = jnp.log(jnp.maximum(n, 1).astype(F32) / exact) / math.log(REL_MAX_DIST / exact)
    large = exact + (log_ratio * (N_BUCKETS - exact)).astype(jnp.int32)
    return jnp.where(n < exact, n, jnp.minimum(large, N_BUCKETS - 1))

def rel_bias_lookup(tab, dist):
    return tab[rel_bucket(dist)].astype(F32)

def banded_attention(q, k, v, max_dist, bias_tab, dist_scale):
    N, G, R, L, dk = q.shape
    dv = v.shape[-1]
    nb = L // QB
    nback = -(-max_dist // QB)
    kw = (nback + 1) * QB

    def windows(t):
        tp = jnp.pad(t, ((0, 0), (0, 0), (nback * QB, 0), (0, 0))).reshape(N, G, nb + nback, QB, t.shape[-1])
        return jnp.concatenate([tp[:, :, j:j + nb] for j in range(nback + 1)], axis=3)

    kwin, vwin = windows(k), windows(v)
    a = jnp.arange(QB)
    c = jnp.arange(kw)
    dist = a[:, None] + nback * QB - c[None, :]
    kpos = (jnp.arange(nb)[:, None] - nback) * QB + c[None, :]
    mask = ((dist >= 0) & (dist <= max_dist))[None] & (kpos >= 0)[:, None, :]
    bias = rel_bias_lookup(bias_tab, dist * dist_scale).transpose(2, 0, 1).reshape(G, R, 1, QB, kw)
    qb = q.reshape(N, G, R, nb, QB, dk)
    s = jnp.einsum('ngrbqd,ngbkd->ngrbqk', qb, kwin).astype(F32) * dk ** -0.5 + bias
    s = jnp.where(mask, s, NEG)
    m = s.max(-1, keepdims=True)
    p = jnp.exp(s - m)
    l = p.sum(-1)
    o = jnp.einsum('ngrbqk,ngbkd->ngrbqd', p.astype(v.dtype), vwin).astype(F32) / l[..., None]
    lse = m[..., 0] + jnp.log(l)
    return o.reshape(N, G, R, L, dv).astype(v.dtype), lse.reshape(N, G, R, L)

def to_strided(t, dil, lp):
    B, H, S, d = t.shape
    L = S // dil
    t = t.reshape(B, H, L, dil, d).transpose(0, 3, 1, 2, 4).reshape(B * dil, H, L, d)
    return jnp.pad(t, ((0, 0), (0, 0), (0, lp - L), (0, 0)))

def from_strided(t, B, S, dil):
    L = S // dil
    t = t[:, :, :L]
    rest = t.shape[3:]
    t = jnp.moveaxis(t.reshape((B, dil) + t.shape[1:]), 1, 3)
    return t.reshape((B, t.shape[1], S) + rest)

def dilated_attention(q, k, v, tab):
    B, _, H, S, hd = q.shape
    outs, lses = [], []
    for g, (window, dil) in enumerate(DIL_PAIRS):
        L = S // dil
        lp = -(-L // QB) * QB
        o, lse = banded_attention(to_strided(q[:, g], dil, lp)[:, :, None], to_strided(k[:, g], dil, lp),
                                  to_strided(v[:, g], dil, lp), window // dil,
                                  tab[:, g * H:(g + 1) * H], dil)
        outs.append(from_strided(o[:, :, 0], B, S, dil).astype(F32))
        lses.append(from_strided(lse[:, :, 0], B, S, dil))
    w = jax.nn.softmax(jnp.stack(lses), axis=0)
    return jnp.sum(w[..., None] * jnp.stack(outs), axis=0).astype(v.dtype)

def mla_attention(q, k, v):
    B, H, S, dqk = q.shape
    nb = S // QB
    qb = q.reshape(B, H, nb, QB, dqk).transpose(2, 0, 1, 3, 4)
    kpos = jnp.arange(S)

    def body(args):
        qq, i = args
        causal = kpos[None, :] <= (i * QB + jnp.arange(QB))[:, None]
        s = jnp.einsum('bhqd,bhkd->bhqk', qq, k).astype(F32) * dqk ** -0.5
        p = jax.nn.softmax(jnp.where(causal, s, NEG), axis=-1)
        return jnp.einsum('bhqk,bhkd->bhqd', p.astype(v.dtype), v)

    o = lax.map(body, (qb, jnp.arange(nb)))
    return o.transpose(1, 2, 0, 3, 4).reshape(B, H, S, -1)

def mixer_ab(x, w_in, q_norm, w_uq, kv_norm, w_ukv, w_out, tab_b):
    B, S, _ = x.shape
    pos = jnp.arange(S)
    c_q, c_kv, k_r, q_b, k_b, v_b = split_cols(x @ w_in, AB_SIZES)
    q = (rms_norm(c_q, q_norm) @ w_uq).reshape(B, S, H_A, NOPE + ROPE_DIM)
    kv = (rms_norm(c_kv, kv_norm) @ w_ukv).reshape(B, S, H_A, NOPE + MLA_V)
    k_r = jnp.broadcast_to(rope(k_r.reshape(B, S, 1, ROPE_DIM), pos), (B, S, H_A, ROPE_DIM))
    q_a = jnp.concatenate([q[..., :NOPE], rope(q[..., NOPE:], pos)], -1).transpose(0, 2, 1, 3)
    k_a = jnp.concatenate([kv[..., :NOPE], k_r], -1).transpose(0, 2, 1, 3)
    v_a = kv[..., NOPE:].transpose(0, 2, 1, 3)
    o_a = mla_attention(q_a, k_a, v_a).transpose(0, 2, 1, 3).reshape(B, S, H_A * MLA_V)

    def heads_b(t):
        return t.reshape(B, S, len(DIL_PAIRS), H_B_GROUP, HD_B).transpose(0, 2, 3, 1, 4)

    o_b = dilated_attention(heads_b(q_b), heads_b(k_b), heads_b(v_b), tab_b)
    o_b = o_b.transpose(0, 2, 1, 3).reshape(B, S, H_B_GROUP * HD_B)
    return jnp.concatenate([o_a, o_b], -1) @ w_out

def compress_blocks(t, pos_emb, w1, w2):
    B, G, S, d = t.shape
    nc = (S - CMP_LEN) // CMP_STRIDE + 1
    idx = jnp.arange(nc)[:, None] * CMP_STRIDE + jnp.arange(CMP_LEN)[None, :]
    blk = (t[:, :, idx] + pos_emb).reshape(B, G, nc, CMP_LEN * d)
    return jax.nn.gelu(blk @ w1) @ w2

def nsa_attention(q, k_cmp, v_cmp, k_slc, v_slc, k_win, v_win, gates, pos_k, k_w1, k_w2, pos_v, v_w1, v_w2, tab):
    B, G, R, S, dk = q.shape
    scale = dk ** -0.5
    pos = jnp.arange(S)
    kc = compress_blocks(k_cmp, pos_k, k_w1, k_w2)
    vc = compress_blocks(v_cmp, pos_v, v_w1, v_w2)
    nc = kc.shape[2]
    blk_end = jnp.arange(nc) * CMP_STRIDE + CMP_LEN - 1
    dist_c = pos[:, None] - blk_end[None, :]
    valid_c = dist_c >= 0
    bias_c = rel_bias_lookup(tab, dist_c).transpose(2, 0, 1).reshape(G, R, S, nc)
    s_c = jnp.einsum('bgrsd,bgcd->bgrsc', q, kc).astype(F32) * scale + bias_c
    s_c = jnp.where(valid_c, s_c, NEG)
    e_c = jnp.exp(s_c - s_c.max(-1, keepdims=True)) * valid_c
    p_c = e_c / jnp.maximum(e_c.sum(-1, keepdims=True), 1e-30)
    o_cmp = jnp.einsum('bgrsc,bgcd->bgrsd', p_c.astype(vc.dtype), vc)
    n_sel = S // SEL_BLOCK
    c0 = jnp.arange(nc) * CMP_STRIDE
    s0 = jnp.arange(n_sel) * SEL_BLOCK
    overlap = jnp.maximum(jnp.minimum(c0[:, None] + CMP_LEN, s0[None, :] + SEL_BLOCK)
                          - jnp.maximum(c0[:, None], s0[None, :]), 0).astype(F32) / CMP_LEN
    imp = jnp.einsum('bgrsc,cj->bgsj', p_c, overlap)
    forced = (s0[None, :] == (pos // SEL_BLOCK * SEL_BLOCK)[:, None]) | (s0[None, :] == 0)
    imp = jnp.where(forced, BIG, jnp.where(s0[None, :] <= pos[:, None], imp, -BIG))
    n_top = min(SEL_TOP, n_sel)
    _, sel_idx = lax.top_k(imp, n_top)
    kblk = k_slc.reshape(B, G, n_sel, SEL_BLOCK, dk)
    vblk = v_slc.reshape(B, G, n_sel, SEL_BLOCK, -1)
    nq = S // SEL_QB
    tk = n_top * SEL_BLOCK
    b_ix = jnp.arange(B)[:, None, None]
    g_ix = jnp.arange(G)[None, :, None]
    tab_g = tab.reshape(N_BUCKETS, G, R).transpose(1, 0, 2)

    def sel_block(args):
        qq, ii, bi = args
        flat = ii.reshape(B, G, SEL_QB * n_top)
        kk = kblk[b_ix, g_ix, flat].reshape(B, G, SEL_QB, tk, dk)
        vv = vblk[b_ix, g_ix, flat].reshape(B, G, SEL_QB, tk, -1)
        kpos = (ii[..., None] * SEL_BLOCK + jnp.arange(SEL_BLOCK)).reshape(B, G, SEL_QB, tk)
        dist = (bi * SEL_QB + jnp.arange(SEL_QB))[:, None] - kpos
        bias = tab_g[g_ix[..., None], rel_bucket(dist)].astype(F32).transpose(0, 1, 4, 2, 3)
        s = jnp.einsum('bgrqd,bgqkd->bgrqk', qq, kk).astype(F32) * scale + bias
        p = jax.nn.softmax(jnp.where((dist >= 0)[:, :, None], s, NEG), axis=-1)
        return jnp.einsum('bgrqk,bgqkd->bgrqd', p.astype(vv.dtype), vv)

    q_b = q.reshape(B, G, R, nq, SEL_QB, dk).transpose(3, 0, 1, 2, 4, 5)
    i_b = sel_idx.reshape(B, G, nq, SEL_QB, n_top).transpose(2, 0, 1, 3, 4)
    o_sel = lax.map(sel_block, (q_b, i_b, jnp.arange(nq)))
    o_sel = o_sel.transpose(1, 2, 3, 0, 4, 5).reshape(B, G, R, S, -1)
    o_win, _ = banded_attention(q, k_win, v_win, WIN - 1, tab, 1)
    return gates[0] * o_cmp + gates[1] * o_sel + gates[2] * o_win

def diff_attention(q, k, v, lam, tab):
    B, H, _, S, dd = q.shape
    nb = S // QB
    kpos = jnp.arange(S)
    q_b = q.reshape(B, H, 2, nb, QB, dd).transpose(3, 0, 1, 2, 4, 5)

    def body(args):
        qq, i = args
        dist = (i * QB + jnp.arange(QB))[:, None] - kpos[None, :]
        bias = rel_bias_lookup(tab, dist).transpose(2, 0, 1)[:, None]
        s = jnp.einsum('bhmqd,bhmkd->bhmqk', qq, k).astype(F32) * dd ** -0.5 + bias
        p = jax.nn.softmax(jnp.where(dist >= 0, s, NEG), axis=-1)
        a = p[:, :, 0] - lam * p[:, :, 1]
        return jnp.einsum('bhqk,bhkd->bhqd', a.astype(v.dtype), v)

    o = lax.map(body, (q_b, jnp.arange(nb)))
    return o.transpose(1, 2, 0, 3, 4).reshape(B, H, S, -1)

def mixer_cd(x, w_in, pos_k, k_w1, k_w2, pos_v, v_w1, v_w2, lq1, lk1, lq2, lk2, d_norm, w_out,
             tab_c, tab_d, lam_init):
    B, S, _ = x.shape
    (q_c, k_cmp, v_cmp, k_slc, v_slc, k_win, v_win, g_c, q_d, k_d, v_d) = split_cols(x @ w_in, CD_SIZES)

    def heads_q(t):
        return t.reshape(B, S, G_C, R_C, DK_C).transpose(0, 2, 3, 1, 4)

    def heads_kv(t):
        return t.reshape(B, S, G_C, -1).transpose(0, 2, 1, 3)

    gates = jax.nn.sigmoid(g_c).reshape(B, S, 3, G_C, R_C).transpose(2, 0, 3, 4, 1)[..., None]
    o_c = nsa_attention(heads_q(q_c), heads_kv(k_cmp), heads_kv(v_cmp), heads_kv(k_slc), heads_kv(v_slc),
                        heads_kv(k_win), heads_kv(v_win), gates, pos_k, k_w1, k_w2, pos_v, v_w1, v_w2, tab_c)
    o_c = o_c.transpose(0, 3, 1, 2, 4).reshape(B, S, H_C * DV_C)
    lam = (jnp.exp(jnp.sum(lq1.astype(F32) * lk1.astype(F32)))
           - jnp.exp(jnp.sum(lq2.astype(F32) * lk2.astype(F32))) + lam_init)
    qd = q_d.reshape(B, S, H_D, 2, DD).transpose(0, 2, 3, 1, 4)
    kd = k_d.reshape(B, S, H_D, 2, DD).transpose(0, 2, 3, 1, 4)
    vd = v_d.reshape(B, S, H_D, 2 * DD).transpose(0, 2, 1, 3)
    o_d = diff_attention(qd, kd, vd, lam, tab_d)
    o_d = (rms_norm(o_d, d_norm) * (1.0 - lam_init)).transpose(0, 2, 1, 3).reshape(B, S, H_D * 2 * DD)
    return jnp.concatenate([o_c, o_d], -1) @ w_out

def swiglu(x, wg, wu, wd):
    return (jax.nn.silu(x @ wg) * (x @ wu)) @ wd

def routed_experts(xf, e_idx, gate, w_gate, w_up, w_down):
    N, D = xf.shape
    E = w_gate.shape[0]
    A = N * TOP_K
    flat_e = e_idx.reshape(A)
    order = jnp.argsort(flat_e)
    e_sorted = flat_e[order]
    tok_sorted = (order // TOP_K).astype(jnp.int32)
    w_sorted = gate.reshape(A)[order]
    counts = jnp.bincount(flat_e, length=E)
    padded = (counts + EBLK - 1) // EBLK * EBLK
    pad_end = jnp.cumsum(padded)
    pad_start = pad_end - padded
    start = jnp.cumsum(counts) - counts
    dest = pad_start[e_sorted] + jnp.arange(A) - start[e_sorted]
    n_blocks = (A + E * (EBLK - 1) + EBLK - 1) // EBLK
    P = n_blocks * EBLK
    rows = jnp.full((P,), N, jnp.int32).at[dest].set(tok_sorted)
    row_w = jnp.zeros((P,), F32).at[dest].set(w_sorted)
    blk_e = jnp.minimum(jnp.searchsorted(pad_end, jnp.arange(n_blocks) * EBLK, side='right'), E - 1)
    xpad = jnp.concatenate([xf, jnp.zeros((1, D), xf.dtype)], 0)

    def body(args):
        r, w, e = args
        xb = xpad[r]
        hb = jax.nn.silu(xb @ w_gate[e]) * (xb @ w_up[e])
        return (hb @ w_down[e]) * w[:, None].astype(xb.dtype)

    yb = lax.map(body, (rows.reshape(n_blocks, EBLK), row_w.reshape(n_blocks, EBLK), blk_e))
    return jax.ops.segment_sum(yb.reshape(P, D), rows, num_segments=N + 1)[:N]

def moe(x, router_w, router_b, w_gate, w_up, w_down, sh_gate, sh_up, sh_down):
    B, S, D = x.shape
    xf = x.reshape(B * S, D)
    scores = jax.nn.sigmoid(xf.astype(F32) @ router_w.astype(F32))
    sel = scores + router_b.astype(F32)
    per_grp = N_EXPERTS // N_EXPERT_GROUPS
    grp_score = lax.top_k(sel.reshape(-1, N_EXPERT_GROUPS, per_grp), 2)[0].sum(-1)
    _, grp_idx = lax.top_k(grp_score, TOPK_GROUPS)
    grp_mask = jax.nn.one_hot(grp_idx, N_EXPERT_GROUPS, dtype=F32).sum(-2) > 0
    sel = jnp.where(jnp.repeat(grp_mask, per_grp, axis=-1), sel, NEG)
    _, e_idx = lax.top_k(sel, TOP_K)
    gate = jnp.take_along_axis(scores, e_idx, axis=-1)
    gate = gate / gate.sum(-1, keepdims=True) * ROUTED_SCALE
    y = routed_experts(xf, e_idx, gate, w_gate, w_up, w_down) + swiglu(xf, sh_gate, sh_up, sh_down)
    return y.reshape(B, S, D)

def setup_inputs(seed: int = 0) -> dict:
    key = jax.random.key(seed)
    ks = iter(jax.random.split(key, 48))
    NE = (DEPTH + 1) // 2
    NO = DEPTH // 2

    def nrm(shape, scale):
        return jax.random.normal(next(ks), shape, F32) * scale

    def gain(shape):
        return 1.0 + nrm(shape, 0.02)

    return {
        'x': nrm((BATCH, SEQ, D_MODEL), 1.0),
        'rel_bias': nrm((N_BUCKETS, N_REL_HEADS), 0.1),
        'ab_w_in': nrm((NE, D_MODEL, AB_IN), D_MODEL ** -0.5),
        'mla_q_norm': gain((NE, Q_LORA)),
        'mla_w_uq': nrm((NE, Q_LORA, H_A * (NOPE + ROPE_DIM)), Q_LORA ** -0.5),
        'mla_kv_norm': gain((NE, KV_LORA)),
        'mla_w_ukv': nrm((NE, KV_LORA, H_A * (NOPE + MLA_V)), KV_LORA ** -0.5),
        'ab_w_out': nrm((NE, AB_OUT, D_MODEL), AB_OUT ** -0.5 * BETA),
        'cd_w_in': nrm((NO, D_MODEL, CD_IN), D_MODEL ** -0.5),
        'nsa_cmp_pos_k': nrm((NO, CMP_LEN, DK_C), 0.1),
        'nsa_cmp_k_w1': nrm((NO, CMP_LEN * DK_C, CMP_HID), (CMP_LEN * DK_C) ** -0.5),
        'nsa_cmp_k_w2': nrm((NO, CMP_HID, DK_C), CMP_HID ** -0.5),
        'nsa_cmp_pos_v': nrm((NO, CMP_LEN, DV_C), 0.1),
        'nsa_cmp_v_w1': nrm((NO, CMP_LEN * DV_C, CMP_HID), (CMP_LEN * DV_C) ** -0.5),
        'nsa_cmp_v_w2': nrm((NO, CMP_HID, DV_C), CMP_HID ** -0.5),
        'diff_lambda_q1': nrm((NO, DD), 0.1),
        'diff_lambda_k1': nrm((NO, DD), 0.1),
        'diff_lambda_q2': nrm((NO, DD), 0.1),
        'diff_lambda_k2': nrm((NO, DD), 0.1),
        'diff_norm': gain((NO, 2 * DD)),
        'cd_w_out': nrm((NO, CD_OUT, D_MODEL), CD_OUT ** -0.5 * BETA),
        'ln1_g': gain((DEPTH, D_MODEL)),
        'ln1_b': nrm((DEPTH, D_MODEL), 0.02),
        'ln2_g': gain((DEPTH, D_MODEL)),
        'ln2_b': nrm((DEPTH, D_MODEL), 0.02),
        'router_w': nrm((DEPTH, D_MODEL, N_EXPERTS), D_MODEL ** -0.5),
        'router_b': nrm((DEPTH, N_EXPERTS), 0.01),
        'exp_w_gate': nrm((DEPTH, N_EXPERTS, D_MODEL, D_EXPERT), D_MODEL ** -0.5),
        'exp_w_up': nrm((DEPTH, N_EXPERTS, D_MODEL, D_EXPERT), D_MODEL ** -0.5),
        'exp_w_down': nrm((DEPTH, N_EXPERTS, D_EXPERT, D_MODEL), D_EXPERT ** -0.5 * BETA),
        'sh_w_gate': nrm((DEPTH, D_MODEL, D_SHARED), D_MODEL ** -0.5),
        'sh_w_up': nrm((DEPTH, D_MODEL, D_SHARED), D_MODEL ** -0.5),
        'sh_w_down': nrm((DEPTH, D_SHARED, D_MODEL), D_SHARED ** -0.5 * BETA),
    }

def reference(x, rel_bias, ab_w_in, mla_q_norm, mla_w_uq, mla_kv_norm, mla_w_ukv, ab_w_out,
              cd_w_in, nsa_cmp_pos_k, nsa_cmp_k_w1, nsa_cmp_k_w2, nsa_cmp_pos_v, nsa_cmp_v_w1, nsa_cmp_v_w2,
              diff_lambda_q1, diff_lambda_k1, diff_lambda_q2, diff_lambda_k2, diff_norm, cd_w_out,
              ln1_g, ln1_b, ln2_g, ln2_b, router_w, router_b, exp_w_gate, exp_w_up, exp_w_down,
              sh_w_gate, sh_w_up, sh_w_down):
    tab_b = rel_bias[:, REL_B0:REL_B0 + H_B]
    tab_c = rel_bias[:, REL_C0:REL_C0 + H_C]
    tab_d = rel_bias[:, REL_D0:REL_D0 + H_D]
    for l in range(DEPTH):
        i = l // 2
        if l % 2 == 0:
            y = mixer_ab(x, ab_w_in[i], mla_q_norm[i], mla_w_uq[i], mla_kv_norm[i], mla_w_ukv[i],
                         ab_w_out[i], tab_b)
        else:
            lam_init = 0.8 - 0.6 * math.exp(-0.3 * l)
            y = mixer_cd(x, cd_w_in[i], nsa_cmp_pos_k[i], nsa_cmp_k_w1[i], nsa_cmp_k_w2[i],
                         nsa_cmp_pos_v[i], nsa_cmp_v_w1[i], nsa_cmp_v_w2[i],
                         diff_lambda_q1[i], diff_lambda_k1[i], diff_lambda_q2[i], diff_lambda_k2[i],
                         diff_norm[i], cd_w_out[i], tab_c, tab_d, lam_init)
        x = layer_norm(ALPHA * x + y, ln1_g[l], ln1_b[l])
        y = moe(x, router_w[l], router_b[l], exp_w_gate[l], exp_w_up[l], exp_w_down[l],
                sh_w_gate[l], sh_w_up[l], sh_w_down[l])
        x = layer_norm(ALPHA * x + y, ln2_g[l], ln2_b[l])
    return x


_drawn_inputs = setup_inputs


def setup_inputs(seed=0):
    import zlib

    import numpy as np

    out = dict(_drawn_inputs(seed))
    spreads = {}
    factors = {'mla_q_norm': 5.15,
     'mla_kv_norm': 2.929,
     'nsa_cmp_pos_k': 20.805,
     'nsa_cmp_pos_v': 2.831,
     'diff_lambda_k1': 2.729,
     'diff_lambda_k2': 4.389,
     'diff_norm': 4.49}
    for name, (base, spread) in spreads.items():
        noise = np.random.default_rng([zlib.crc32(name.encode()), seed]).standard_normal(out[name].shape)
        drawn = base * np.exp(spread * noise) if base else spread * noise
        out[name] = jnp.asarray(drawn.astype(out[name].dtype))
    for name, factor in factors.items():
        out[name] = (out[name] * factor).astype(out[name].dtype)
    return out
```

```python
import math
from contextlib import ExitStack

import numpy as np

import concourse.bass as bass
from concourse import mybir

P = 128
TOK = 256
TT = TOK // P
D = 1024
DC = D // P
DEPTH = 2
ALPHA = (2 * DEPTH) ** 0.25
LN_EPS, RMS_EPS = 1e-5, 1e-6
NEG = -1e30

H_A, NOPE, ROPE, MLA_V = 12, 64, 32, 64
Q_LORA, KV_LORA = 256, 128
QK_A = NOPE + ROPE
HALF = ROPE // 2
H_B, HD = 12, 64
H_C, G_C, R_C = 8, 2, 4
H_D = 4
CMP_LEN, CMP_STRIDE = 32, 16
NC_BLK = (TOK - CMP_LEN) // CMP_STRIDE + 1
LAM_INIT = 0.8 - 0.6 * math.exp(-0.3 * 1)
BUCKETS = 32

EXPERTS, TOP_K, GROUPS, TOP_GROUPS = 64, 8, 8, 4
F_EXP = 256
ROUTED_SCALE = 2.5
SLOTS = 64
PASSES = TOK // SLOTS
EXTRA = TOK * TOP_K // SLOTS
QUADS = EXPERTS // 4
MAX_QUADS = QUADS + EXTRA // 4
VISITS = 4 * (MAX_QUADS + 1)

C_IN = Q_LORA + KV_LORA + ROPE
GU = DC * 2 * F_EXP
SLOT_W = GU + 2 * D
RING = 4
MIX_BLOCKS = 8
MIX_SIZE = [[DC * C_IN, DC * 768, DC * 768, DC * 768, 2 * 1152 + 1536, DC * 512, DC * 512],
            [DC * 536, DC * 768, DC * 512 + 2048, DC * 512 + 2048, DC * 512, DC * 512, DC * 512]]

SPAN = P + TOK - 1
BIAS_ROWS = 25
BIAS_OF = [(0, 13), (13, 12)]

CONST = {}
_at = 0
for _name, _n in (("ident", P), ("tri", P), ("ones", P), ("iota", SLOTS * (PASSES + 1)),
                  ("cos", TT * HALF), ("sin", TT * HALF), ("valid", TT * 16), ("gtri", 64),
                  ("kiota", EXTRA), ("thr", 3), ("ecode", 1), ("pcode", 3), ("base", EXPERTS), ("quad4", 8)):
    CONST[_name] = (_at, _n)
    _at += _n
N_CONST = _at
SMALL = {"qn": (0, 256), "kvn": (256, 128), "dn": (384, 128), "lam": (512, 256), "rb": (768, 128)}
N_SMALL = 896


def build(nc, x, xT_in, mixw, expw, const, tab, hot, mask, small, lnp, routw, pos, w2, out):
    F32, I32 = mybir.dt.float32, mybir.dt.int32
    ALU, ACT = mybir.AluOpType, mybir.ActivationFunctionType
    X = mybir.AxisListType.X
    scratch = nc.dram_tensor("bias_rows_dram", (BIAS_ROWS, SPAN), F32, kind="Internal").ap()

    with ExitStack() as ctx:
        def sb(name, shape, dt=F32):
            return ctx.enter_context(nc.sbuf_tensor(name, shape, dt))

        def sem(name):
            return ctx.enter_context(nc.semaphore(name))

        def per_layer(name):
            return [sem(f"{name}_{l}") for l in range(DEPTH)]

        bank = [ctx.enter_context(nc.psum_tensor(f"bank{i}", [P, 512], F32)) for i in range(8)]
        Ybank = [[bank[2 * t + hh] for hh in range(2)] for t in range(TT)]
        bA, bB, bC, bH = bank[4], bank[5], bank[6], bank[7]

        ring = sb("ring", [P, RING, SLOT_W])
        x_tok = sb("x_tok", [P, TT, D])
        xT = sb("xT", [P, DC, TOK])
        zb = sb("zb", [P, TT * 1152])
        biasZ = sb("biasZ", [P, 13, TOK])
        arena = sb("arena", [P, 12288])
        probs = sb("probs", [P, 2, 3 * P])
        probsT = sb("probsT", [P, 2, 3 * P])
        ob = sb("ob", [P, TT, 512])
        tmp = sb("tmp", [P, 832])
        cst = sb("cst", [P, N_CONST])
        sml = sb("sml", [P, N_SMALL])
        rw = sb("rw", [P, DC, EXPERTS])
        posT = sb("posT", [P, 2, CMP_LEN])
        w2s = sb("w2s", [P, 2, HD])
        negmax = sb("negmax", [P, TT, 24])
        rowsum = sb("rowsum", [P, TT, 24])
        rinv = sb("rinv", [P, TT, 24])
        gates3 = sb("gates3", [P, TT, 24])
        wg = sb("wg", [P, TT, 24])
        st = sb("st", [P, 64])
        lam = sb("lam", [P, 8])
        visit = sb("visit", [1, 2, VISITS], I32)
        nquads = sb("nquads", [1, 4], I32)

        def area(at, *shape):
            n = int(np.prod(shape))
            ap = arena[:, at:at + n]
            if len(shape) > 1:
                names = "abcd"[:len(shape)]
                ap = ap.rearrange(f"p ({' '.join(names)}) -> p {' '.join(names)}",
                                  **{k: v for k, v in zip(names[1:], shape[1:])})
            return ap

        def zview(at, *shape):
            n = int(np.prod(shape))
            names = "abcd"[:len(shape)]
            return zb[:, at:at + n].rearrange(f"p ({' '.join(names)}) -> p {' '.join(names)}",
                                              **{k: v for k, v in zip(names[1:], shape[1:])})

        def c_(name, rows=P):
            at, n = CONST[name]
            return cst[0:rows, at:at + n]

        def s_(name):
            at, n = SMALL[name]
            return sml[:, at:at + n]

        ident = c_("ident")
        z = zview(0, TT, D)
        o_tok = z
        q_tok = zview(0, TT, 1152)
        ctok = zview(0, TT, C_IN)
        cn = zview(TT * C_IN, TT, 480)
        cT = probs[:, :, :].rearrange("p a b -> p (a b)").rearrange("p (c t) -> p c t", c=3)
        oT = xT
        V0 = area(0, TT, 24 * HD)
        KTm = area(3072, H_A, TOK)
        QTd = area(6144, 6, TOK)
        KTd = area(7680, 6, TOK)
        QTm = area(9216, H_A, TOK)
        QTc = area(0, R_C, TOK)
        QTf = area(1024, H_D, TOK)
        KTc = area(2048, 4, TOK)
        KTf = area(3072, H_D, TOK)
        Vs = area(4096, TT, 2 * P)
        Vf = area(4608, TT, 512)
        Xw = area(5632, 2, CMP_LEN, NC_BLK)
        hid = area(6592, 2, 16)
        hid_t = area(6624, 4, 16)
        hid4 = area(6688, 4, 32)
        kcT = area(6816, 16)
        VBD = area(6832, G_C, 4, HD)
        ec = area(7344, TT, H_C, 32)
        ecT = area(7856, TT, G_C, P)
        cs = area(8368, 6, 16)
        xg = area(0, 2, DC, P)
        yb = area(2048, 2, D)
        sgT = area(4096, 2, TT, P)
        hT = area(4608, 2, 2, P)
        sil = area(5120, 2, 2, P)
        Sel = area(5632, 2, TT, P)
        Selg = area(6144, 2, TT, P)
        sils = area(6656, 2, TOK)
        hTs = area(7168, 2, TOK)
        r_sc, r_sel, r_m8, r_selm, r_rep, r_mask, r_gate, r_pos = (
            area(7680 + 128 * i, TT, EXPERTS) for i in range(8))
        r_gs, r_rank, r_gm, r_top = (area(8704 + 16 * i, TT, GROUPS) for i in range(4))
        r_gt = area(8768, GROUPS, GROUPS)
        r_eq = area(8832, GROUPS, GROUPS)
        r_ov = area(8896, 4)
        r_ovp = area(8900, 4)
        r_idx = area(8904, 4)
        r_hot = area(8912, 3, EXTRA)
        r_list = area(9008, 2, EXTRA)
        r_den = area(9072, TT)
        r_q = area(9080, 8)
        visit_f = area(9088, 2, VISITS)
        lng = area(10240, 2, D)

        const_in, x_in, small_in, scratch_out, out_done = map(sem, (
            "const_in", "x_in", "small_in", "scratch_out", "out_done"))
        bias_ps, bias_sb = sem("bias_ps"), sem("bias_sb")
        bias_in, bias_free = sem("bias_in"), sem("bias_free")
        rw_in = sem("rw_in")
        ln_in, ln_free, ln_area_free = sem("ln_in"), sem("ln_free"), sem("ln_area_free")
        loaded = [[sem(f"ring{k}_loaded_{l}") for k in range(RING)] for l in range(DEPTH)]
        used = per_layer("ring_used")
        proj_done, proj_taken = per_layer("proj_done"), per_layer("proj_taken")
        rms_var, rms_std = sem("rms_var"), sem("rms_std")
        cn_ready, q_roped = sem("cn_ready"), sem("q_roped")
        scores_done, scores_taken = per_layer("scores_done"), per_layer("scores_taken")
        max_ready, probs_ready = per_layer("max_ready"), per_layer("probs_ready")
        pt_done, pt_taken, pv_done = per_layer("pt_done"), per_layer("pt_taken"), per_layer("pv_done")
        o_taken = per_layer("o_taken")
        comb_d, comb_w = sem("comb_d"), sem("comb_w")
        o_ready, oT_done, oT_taken = per_layer("o_ready"), per_layer("oT_done"), per_layer("oT_taken")
        y_done = per_layer("y_done")
        ln_var, ln_std, ln_norm, ln_gained, x_ready = map(sem, ("ln_var", "ln_std", "ln_norm", "ln_gained", "x_ready"))
        xT_done, xT_taken = sem("xT_done"), sem("xT_taken")
        logit_done, esig_ready = per_layer("logit_done"), per_layer("esig_ready")
        mask_ready, pos_done = per_layer("mask_ready"), per_layer("pos_done")
        over_ready, idx_done = per_layer("over_ready"), per_layer("idx_done")
        hot_ready, list_done, visits_ready = per_layer("hot_ready"), per_layer("list_done"), per_layer("visits_ready")
        sh_gu, sh_silu, sh_h = per_layer("sh_gu"), per_layer("sh_silu"), per_layer("sh_h")
        sel_ready, gath_done, xgA_ready, xgB_ready = (per_layer(n) for n in (
            "sel_ready", "gath_done", "xgA_ready", "xgB_ready"))
        gu_done, silu_ready, h_ready = per_layer("gu_done"), per_layer("silu_ready"), per_layer("h_ready")
        sgT_done, sgT_ready = per_layer("sgT_done"), per_layer("sgT_ready")
        down_done, ybA_ready, ybB_ready = per_layer("down_done"), per_layer("ybA_ready"), per_layer("ybB_ready")
        scat_done = per_layer("scat_done")
        moe_done = per_layer("moe_done")
        gate_logit, gate_exp = sem("gate_logit"), sem("gate_exp")
        win_ready, hid_done, hid_z, hid_e, hid_ready = map(sem, ("win_ready", "hid_done", "hid_z", "hid_e", "hid_ready"))
        kv_done, kv_taken = sem("kv_done"), sem("kv_taken")
        cmp_s, cmp_c, cmp_e, cmp_p = map(sem, ("cmp_s", "cmp_c", "cmp_e", "cmp_p"))
        cmpT_done, cmpT_taken, cmp_o = sem("cmpT_done"), sem("cmpT_taken"), sem("cmp_o")
        lam_s, lam_e = sem("lam_s"), sem("lam_e")
        dn_var, dn_std = sem("dn_var"), sem("dn_std")
        dve_step, act_step = sem("dve_step"), sem("act_step")

        def mm_group(pe, outap, pairs):
            for k, (l, r) in enumerate(pairs):
                last = pe.matmul(outap, l, r, start=(k == 0), stop=(k == len(pairs) - 1))
            return last

        def slot(block, at, chunks, cols):
            return ring[:, block % RING, at:at + chunks * cols].rearrange("p (c n) -> p c n", c=chunks)

        def tokens_out(w, t, lo, n, src=xT, chunks=DC):
            return lambda pe, b: mm_group(pe, b[:, 0:n], [(src[:, c, t * P:(t + 1) * P], w[:, c, lo:lo + n])
                                                          for c in range(chunks)])

        def two_T(w, cols):
            def go(pe, b):
                for k, lhs in enumerate(cols):
                    m = mm_group(pe, b[:, k * TOK:(k + 1) * TOK], [(lhs(w, c), xT[:, c, :]) for c in range(DC)])
                return m
            return go

        def jobs0():
            wA, wq, wk, wv = (slot(k, 0, DC, n) for k, n in ((0, C_IN), (1, 768), (2, 768), (3, 768)))
            wuq = slot(4, 0, 2, 1152)
            wukv = ring[:, 0, 2304:2304 + 1536].rearrange("p (h a d) -> p h a d", h=H_A, a=2)
            jobs = []
            for t in range(TT):
                jobs.append((0, t == 1, [], tokens_out(wA, t, 0, C_IN), [(ctok[:, t, :], (P, 0, C_IN))]))
            for blk, w, dst in ((1, wq, QTd), (2, wk, KTd)):
                for k in range(3):
                    cols = [lambda w, c, i=i: w[:, c, i * P:(i + 1) * P] for i in (2 * k, 2 * k + 1)]
                    jobs.append((blk, k == 2, [], two_T(w, cols),
                                 [(dst[:, 2 * k:2 * k + 2, :].rearrange("p a t -> p (a t)"), (P, 0, 512))]))
            for t in range(TT):
                for lo, n in ((0, 512), (512, 256)):
                    jobs.append((3, t == 1 and lo > 0, [], tokens_out(wv, t, lo, n),
                                 [(V0[:, t, lo:lo + n], (P, 0, n))]))

            def turn_q(pe, b):
                for c in range(2):
                    for t in range(TT):
                        m = pe.transpose(b[:, c * TOK + t * P:c * TOK + (t + 1) * P], cn[:, t, c * P:(c + 1) * P], ident)
                return m

            def turn_kv(pe, b):
                for t in range(TT):
                    pe.transpose(b[:, t * P:(t + 1) * P], cn[:, t, 2 * P:3 * P], ident)
                for t in range(TT):
                    m = pe.transpose(b[0:QK_A, TOK + t * P:TOK + (t + 1) * P], cn[:, t, 384:480], ident)
                return m

            jobs.append((None, False, [(cn_ready, 1)], turn_q,
                         [(cT[:, 0:2, :].rearrange("p a t -> p (a t)"), (P, 0, 512))]))
            jobs.append((None, False, [], turn_kv,
                         [(cT[:, 2, :], (P, 0, TOK)), ("rope key", None)]))
            n_cT = len(jobs)
            for t in range(TT):
                for k, (lo, n) in enumerate(((0, 512), (512, 512), (1024, 128))):
                    jobs.append((4, False, [(proj_taken[0], n_cT)] if t == 0 and k == 0 else [],
                                 tokens_out(wuq, t, lo, n, cT, 2), [(q_tok[:, t, lo:lo + n], (P, 0, n))]))
            n_q = len(jobs)
            for k in range(6):
                def nope(pe, b, k=k):
                    for i in range(2):
                        m = pe.matmul(b[0:NOPE, i * TOK:(i + 1) * TOK], wukv[:, 2 * k + i, 0, :], cT[:, 2, :],
                                      start=True, stop=True)
                    return m
                jobs.append((4, False, [], nope,
                             [(KTm[0:NOPE, 2 * k:2 * k + 2, :].rearrange("p a t -> p (a t)"), (NOPE, 0, 512))]))
            for t in range(TT):
                for h0, n in ((0, 8), (8, 4)):
                    def vals(pe, b, t=t, h0=h0, n=n):
                        return pe.matmul(b[:, 0:n * HD].rearrange("p (h d) -> p h d", h=n),
                                         cT[:, 2, t * P:(t + 1) * P], wukv[:, h0:h0 + n, 1, :], start=True, stop=True)
                    jobs.append((4, t == 1 and h0 > 0, [], vals,
                                 [(V0[:, t, 768 + h0 * HD:768 + (h0 + n) * HD], (P, 0, n * HD))]))
            for k in range(6):
                def turn(pe, b, k=k):
                    for i in range(2):
                        for t in range(TT):
                            m = pe.transpose(b[0:QK_A, i * TOK + t * P:i * TOK + (t + 1) * P],
                                             q_tok[:, t, (2 * k + i) * QK_A:(2 * k + i + 1) * QK_A], ident)
                    return m
                jobs.append((None, False, [(q_roped, TT)] if k == 0 else [], turn,
                             [(QTm[0:QK_A, 2 * k:2 * k + 2, :].rearrange("p a t -> p (a t)"), (QK_A, 0, 512))]))
            return jobs, n_q

        def jobs1():
            wqc, wkv, wqd, wkd = slot(0, 0, DC, 536), slot(1, 0, DC, 768), slot(2, 0, DC, 512), slot(3, 0, DC, 512)
            wvd = slot(4, 0, DC, 512)
            jobs = []
            for k in range(2):
                cols = [lambda w, c, r=r: w[:, c, r * P:(r + 1) * P] for r in (2 * k, 2 * k + 1)]
                jobs.append((0, False, [], two_T(wqc, cols),
                             [(QTc[:, 2 * k:2 * k + 2, :].rearrange("p a t -> p (a t)"), (P, 0, 512))]))

            def gate_cols(pe, b):
                for t in range(TT):
                    m = mm_group(pe, b[:, t * 24:(t + 1) * 24],
                                 [(xT[:, c, t * P:(t + 1) * P], wqc[:, c, 512:536]) for c in range(DC)])
                return m
            jobs.append((0, True, [], gate_cols, [("gates", None)]))
            for k in range(2):
                cols = [lambda w, c, i=i: w[:, c, i * P:(i + 1) * P] for i in (2 * k, 2 * k + 1)]
                jobs.append((1, False, [], two_T(wkv, cols),
                             [(KTc[:, 2 * k:2 * k + 2, :].rearrange("p a t -> p (a t)"), (P, 0, 512))]))

            def vals(pe, b):
                for t in range(TT):
                    m = mm_group(pe, b[:, t * TOK:(t + 1) * TOK],
                                 [(xT[:, c, t * P:(t + 1) * P], wkv[:, c, 512:768]) for c in range(DC)])
                return m
            jobs.append((1, True, [], vals, [(Vs[:, :, :].rearrange("p a t -> p (a t)"), (P, 0, 512))]))
            for blk, w, dst in ((2, wqd, QTf), (3, wkd, KTf)):
                for k in range(2):
                    cols = [lambda w, c, i=i: w[:, c, i * P:(i + 1) * P] for i in (2 * k, 2 * k + 1)]
                    jobs.append((blk, False, [], two_T(w, cols),
                                 [(dst[:, 2 * k:2 * k + 2, :].rearrange("p a t -> p (a t)"), (P, 0, 512))]))
            return jobs, wvd

        JOBS0, N_Q = jobs0()
        JOBS1, w_vd = jobs1()
        JOBS = [JOBS0, JOBS1]
        for t in range(TT):
            JOBS1.append((4, t == 1, [], tokens_out(w_vd, t, 0, 512), [(Vf[:, t, :], (P, 0, 512))]))
        KCMP_JOB = 4
        HID_AFTER = 10

        def item(l, n):
            if l == 0:
                if n < 12:
                    r = slice(64 * (n % 2), 64 * (n % 2) + 64)
                    return dict(q=QTd[r, n // 2, :], k=KTd[r, n // 2, :], v=lambda j, n=n: V0[:, j, n * HD:(n + 1) * HD],
                                bias=n, scale=HD ** -0.5, col=(n % 8) * HD, width=HD, stat=n)
                h = n - 12
                return dict(q=QTm[0:QK_A, h, :], k=KTm[0:QK_A, h, :], v=lambda j, n=n: V0[:, j, n * HD:(n + 1) * HD],
                            bias=12, scale=QK_A ** -0.5, col=(n % 8) * HD, width=HD, stat=n)
            if n < 16:
                b, g, r = n // 8, n % 2, (n % 8) // 2
                h = g * R_C + r
                rows = slice(64 * g, 64 * g + 64)
                return dict(q=QTc[rows, r, :], k=KTc[rows, 2 + b, :],
                            v=lambda j, b=b, g=g: Vs[:, j, b * P + g * HD:b * P + (g + 1) * HD],
                            bias=h, scale=HD ** -0.5, col=h * HD, width=HD, stat=8 * b + h)
            hd, m = (n - 16) // 2, n % 2
            rows = slice(64 * m, 64 * m + 64)
            return dict(q=QTf[rows, hd, :], k=KTf[rows, hd, :], v=lambda j, hd=hd: Vf[:, j, hd * P:(hd + 1) * P],
                        bias=8 + hd, scale=HD ** -0.5, col=(hd % 2) * 256 + m * P, width=P, stat=16 + 4 * m + hd)

        ITEMS = [[item(l, n) for n in range(24)] for l in range(DEPTH)]
        GROUP_END = [[8, 16, 24], [8, 16, 20, 24]]

        def group_of(l, n):
            return next(g for g, e in enumerate(GROUP_END[l]) if n < e)

        def o_bank(l, g, t):
            return bank[4 + 2 * (g % 2) + t]

        block = ctx.enter_context(nc.Block())

        @block.sync
        def _(sp):
            def ring_load(l, k, src, n):
                sp.dma_start(ring[:, k % RING, 0:n], src[:, 0:n]).then_inc(loaded[l][k % RING], 16)

            sp.dma_start(xT[:, :, :], xT_in.rearrange("(c p) t -> p c t", p=P)).then_inc(x_in, 16)
            n = None
            for l in range(DEPTH):
                for k in range(MIX_BLOCKS):
                    if k >= RING:
                        sp.wait_ge(used[l], k - RING + 1)
                    elif l:
                        sp.wait_ge(used[l - 1], n * RING + (MIX_BLOCKS - RING + k + 1))
                    if k < MIX_BLOCKS - 1:
                        ring_load(l, k, mixw[l, k], MIX_SIZE[l][k])
                    else:
                        ring_load(l, k, expw[l, EXPERTS], SLOT_W)
                    if l == 0 and k == 0:
                        sp.dma_start(x_tok[:, :, :], x.rearrange("(t p) d -> p t d", p=P)).then_inc(x_in, 16)
                sp.wait_ge(visits_ready[l], 1)
                n = sp.value_load(nquads[0:1, 0:1], min_val=QUADS, max_val=MAX_QUADS)
                with sp.Fori(0, n) as i:
                    for j in range(4):
                        e = sp.value_load(visit[0:1, 0, bass.ds(i * 4 + j, 1)], min_val=0, max_val=EXPERTS - 1)
                        sp.wait_ge(used[l], i * 4 + (MIX_BLOCKS - RING + j + 1))
                        sp.dma_start(ring[:, j, :], expw[l, bass.ds(e, 1), :, :].rearrange("o p n -> (o p) n"))\
                          .then_inc(loaded[l][j], 16)
            for t in range(TT):
                sp.wait_ge(x_ready, 2 * TT * DEPTH - TT + t + 1)
                sp.dma_start(out[t * P:(t + 1) * P, :], x_tok[:, t, :]).then_inc(out_done, 16)
            sp.wait_ge(out_done, 16 * TT)

        @block.gpsimd
        def _(pool):
            pool.dma_start(cst[:, :], const).then_inc(const_in, 16)
            pool.dma_start(tmp[0:BUCKETS, 0:BIAS_ROWS], tab).then_inc(const_in, 16)
            pool.dma_start(tmp[0:BUCKETS, 32:32 + SPAN], hot).then_inc(const_in, 16)
            pool.dma_start(tmp[0:BIAS_ROWS, 448:448 + SPAN], mask).then_inc(const_in, 16)
            pool.dma_start(sml[:, :], small.to_broadcast([P, N_SMALL])).then_inc(small_in, 16)
            pool.dma_start(posT[:, :, :], pos).then_inc(small_in, 16)
            pool.dma_start(w2s[:, :, :], w2).then_inc(small_in, 16)
            pool.dma_start(rw[:, :, :], routw[0]).then_inc(rw_in, 16)
            pool.wait_ge(bias_sb, 1)
            pool.dma_start(scratch, tmp[0:BIAS_ROWS, 448:448 + SPAN]).then_inc(scratch_out, 16)
            pool.wait_ge(scratch_out, 16)

            def bias_load(l):
                r0, n = BIAS_OF[l]
                src = bass.AP(scratch.tensor, r0 * SPAN, [(1, P), (SPAN, n), (1, TOK)])
                pool.dma_start(biasZ[:, 0:n, :], src).then_inc(bias_in, 16)

            bias_load(0)
            for l in range(DEPTH):
                for half in range(2):
                    k = 2 * l + half
                    if half == 0:
                        pool.wait_ge(ln_area_free, l + 1)
                    else:
                        pool.wait_ge(ln_gained, TT * k)
                        pool.wait_ge(ln_free, k)
                    pool.dma_start(lng[:, :, :].rearrange("p a d -> p (a d)"),
                                   lnp[k:k + 1, :].to_broadcast([P, 2 * D])).then_inc(ln_in, 16)
                    if k == 0:
                        pool.wait_ge(bias_free, 1)
                        bias_load(1)
                    if k == 1:
                        pool.wait_ge(logit_done[0], 1)
                        pool.dma_start(rw[:, :, :], routw[1]).then_inc(rw_in, 16)
                    pool.wait_ge(ln_in, 16 * (k + 1))
                    for t in range(TT):
                        pool.wait_ge(ln_gained, TT * k + t + 1)
                        pool.tensor_tensor(x_tok[:, t, :], z[:, t, :], lng[:, 1, :], ALU.add).then_inc(x_ready, 1)
                    pool.wait_ge(x_ready, TT * (k + 1))
                    pool.nop().then_inc(ln_free, 1)

        @block.tensor
        def _(pe):
            pe.wait_ge(const_in, 64)
            pe.matmul(bank[7][0:BIAS_ROWS, 0:SPAN], tmp[0:BUCKETS, 0:BIAS_ROWS], tmp[0:BUCKETS, 32:32 + SPAN],
                      start=True, stop=True).then_inc(bias_ps, 1)

            def ring_in(l, k):
                pe.wait_ge(loaded[l][k % RING], 16 * (k // RING + 1))

            def projections(l, lo, hi):
                for n in range(lo, hi):
                    blk, last_use, waits, go, _ = JOBS[l][n]
                    if blk is not None:
                        ring_in(l, blk)
                    for s, v in waits:
                        pe.wait_ge(s, v)
                    if n >= 4:
                        pe.wait_ge(proj_taken[l], n - 3)
                    m = go(pe, bank[n % 4])
                    m.then_inc(proj_done[l], 1)
                    if last_use:
                        pe.wait_ge(proj_done[l], n + 1)
                        pe.nop().then_inc(used[l], 1)

            def scores(l, n):
                it = ITEMS[l][n]
                b = bank[n % 2]
                if n >= 2:
                    pe.wait_ge(scores_taken[l], n - 1)
                for qt, kt, at in ((0, 0, 0), (1, 0, P)):
                    m = pe.matmul(b[:, at:at + P * (qt + 1)], it["q"][:, qt * P:(qt + 1) * P],
                                  it["k"][:, 0:P * (qt + 1)], start=True, stop=True)
                m.then_inc(scores_done[l], 1)

            def turn_probs(l, n):
                pe.wait_ge(probs_ready[l], n + 1)
                if n >= 2:
                    pe.wait_ge(pt_taken[l], n - 1)
                for j in range(3):
                    m = pe.transpose(bank[2 + n % 2][:, j * P:(j + 1) * P], probs[:, n % 2, j * P:(j + 1) * P], ident)
                m.then_inc(pt_done[l], 1)

            def values(l, n):
                it, g = ITEMS[l][n], group_of(l, n)
                pe.wait_ge(pt_taken[l], n + 1)
                if g >= 2:
                    pe.wait_ge(o_taken[l], g - 1)
                cols = slice(it["col"], it["col"] + it["width"])
                pe.matmul(o_bank(l, g, 0)[:, cols], probsT[:, n % 2, 0:P], it["v"](0), start=True, stop=True)
                pe.matmul(o_bank(l, g, 1)[:, cols], probsT[:, n % 2, P:2 * P], it["v"](0), start=True, stop=False)
                pe.matmul(o_bank(l, g, 1)[:, cols], probsT[:, n % 2, 2 * P:3 * P], it["v"](1), start=False, stop=True)\
                  .then_inc(pv_done[l], 1)

            def attention(l):
                pe.wait_ge(proj_taken[l], len(JOBS[l]))
                for n in range(26):
                    if n < 24:
                        scores(l, n)
                    if n == 24:
                        pe.wait_ge(scores_done[l], 24)
                        pe.nop().then_inc(ln_area_free, 1)
                    if 1 <= n <= 24:
                        turn_probs(l, n - 1)
                    if n >= 2:
                        values(l, n - 2)

            def output_projection(l):
                pe.wait_ge(o_ready[l], 1)
                for k in range(4):
                    for c in (2 * k, 2 * k + 1):
                        for t in range(TT):
                            m = pe.transpose(bank[k][:, (c % 2) * TOK + t * P:(c % 2) * TOK + (t + 1) * P],
                                             o_tok[:, t, c * P:(c + 1) * P], ident)
                    m.then_inc(oT_done[l], 1)
                pe.wait_ge(oT_taken[l], 4)
                for hh in range(2):
                    ring_in(l, 5 + hh)
                    w = slot(5 + hh, 0, DC, 512)
                    for t in range(TT):
                        m = mm_group(pe, Ybank[t][hh][:, :], [(oT[:, c, t * P:(t + 1) * P], w[:, c, :]) for c in range(DC)])
                        m.then_inc(y_done[l], 1)
                    pe.wait_ge(y_done[l], 2 * hh + 2)
                    pe.nop().then_inc(used[l], 1)

            def turn_x(k):
                for q in range(4):
                    for t in range(TT):
                        pe.wait_ge(x_ready, TT * k + t + 1)
                    for c in (2 * q, 2 * q + 1):
                        for t in range(TT):
                            m = pe.transpose(bank[4 + q][:, (c % 2) * TOK + t * P:(c % 2) * TOK + (t + 1) * P],
                                             x_tok[:, t, c * P:(c + 1) * P], ident)
                    m.then_inc(xT_done, 1)
                pe.wait_ge(xT_taken, 4 * (k + 1))

            def compress():
                pe.wait_ge(win_ready, 1)
                ring_in(1, 2)
                ring_in(1, 3)
                for kv in range(2):
                    w1 = ring[:, 2 + kv, 4096:6144].rearrange("p (j h) -> p j h", j=CMP_LEN)
                    for g in range(G_C):
                        r = slice(64 * g, 64 * g + 64)
                        for j in range(CMP_LEN):
                            m = pe.matmul(bank[6 + g][r, kv * 16:kv * 16 + NC_BLK], w1[r, j, :], Xw[r, kv, j, :],
                                          start=(j == 0), stop=(j == CMP_LEN - 1))
                m.then_inc(hid_done, 1)
                pe.wait_ge(hid_done, 1)
                pe.nop().then_inc(used[1], 2)
                pe.wait_ge(hid_ready, 1)
                pe.wait_ge(small_in, 48)
                for g in range(G_C):
                    r = slice(64 * g, 64 * g + 64)
                    pe.matmul(bank[6 + g][r, 64:64 + NC_BLK], w2s[r, 0, :], hid[r, 0, 0:NC_BLK], start=True, stop=True)
                    m = pe.matmul(bank[6 + g][:, 128:192], hid4[r, :, :].rearrange("p a c -> p (a c)"), w2s[r, 1, :],
                                  start=True, stop=True)
                m.then_inc(kv_done, 1)

            def compressed_attention():
                pe.wait_ge(kv_taken, 1)
                pe.wait_ge(proj_taken[1], len(JOBS1))
                for g in range(G_C):
                    for t in range(TT):
                        for r in range(R_C):
                            rows = slice(64 * g, 64 * g + 64)
                            at = (t * R_C + r) * 16
                            m = pe.matmul(bank[g][:, at:at + NC_BLK], QTc[rows, r, t * P:(t + 1) * P],
                                          kcT[rows, 0:NC_BLK], start=True, stop=True)
                m.then_inc(cmp_s, 1)
                pe.wait_ge(cmp_p, 1)
                for t in range(TT):
                    for g in range(G_C):
                        m = pe.transpose(bank[2][:, (t * G_C + g) * P:(t * G_C + g + 1) * P],
                                         ec[:, t, 4 * g:4 * g + 4, :].rearrange("p h c -> p (h c)"), ident)
                m.then_inc(cmpT_done, 1)
                pe.wait_ge(cmpT_taken, 1)
                for t in range(TT):
                    for g in range(G_C):
                        m = pe.matmul(bank[6 + t][:, g * 256:(g + 1) * 256], ecT[:, t, g, :],
                                      VBD[:, g, :, :].rearrange("p h d -> p (h d)"), start=True, stop=True)
                m.then_inc(cmp_o, 1)

            def router(l):
                pe.wait_ge(rw_in, 16 * (l + 1))
                for t in range(TT):
                    m = mm_group(pe, bC[:, t * EXPERTS:(t + 1) * EXPERTS],
                                 [(xT[:, c, t * P:(t + 1) * P], rw[:, c, :]) for c in range(DC)])
                m.then_inc(logit_done[l], 1)

            def gate_up_shared(l):
                ring_in(l, 7)
                w = slot(3, 0, DC, 2 * F_EXP)
                for b, lo in ((bA, 0), (bB, F_EXP)):
                    for f in range(2):
                        m = mm_group(pe, b[:, f * TOK:(f + 1) * TOK],
                                     [(w[:, c, lo + f * P:lo + (f + 1) * P], xT[:, c, :]) for c in range(DC)])
                m.then_inc(sh_gu[l], 1)

            def places(l):
                pe.wait_ge(mask_ready[l], 1)
                tri, ones = c_("tri"), c_("ones")
                mm_group(pe, bC[:, 0:EXPERTS], [(tri, r_mask[:, 0, :])])
                mm_group(pe, bC[:, EXPERTS:2 * EXPERTS], [(ones, r_mask[:, 0, :]), (tri, r_mask[:, 1, :])])
                mm_group(pe, bC[0:EXPERTS, 128:129], [(r_mask[:, t, :], ones[:, 0:1]) for t in range(TT)])\
                    .then_inc(pos_done[l], 1)

            def down_shared(l):
                pe.wait_ge(sh_h[l], 1)
                w = ring[:, 3, GU:SLOT_W].rearrange("p (f n) -> p f n", f=2)
                for t in range(TT):
                    for hh in range(2):
                        for f in range(2):
                            m = pe.matmul(Ybank[t][hh][:, :], hTs[:, f, t * P:(t + 1) * P],
                                          w[:, f, hh * 512:(hh + 1) * 512], start=(f == 0), stop=False,
                                          skip_group_check=True)
                m.then_inc(used[l], 1)

            def visit_list(l):
                pe.wait_ge(over_ready[l], 1)
                mm_group(pe, bC[0:64, 0:4], [(c_("tri", 64)[:, 0:64], r_ov[0:64, :]), (c_("ones", 64)[:, 0:64], r_ovp[0:64, :])])\
                    .then_inc(idx_done[l], 1)
                pe.wait_ge(hot_ready[l], 1)
                mm_group(pe, bC[0:1, 0:EXTRA], [(c_("ecode", 64), r_hot[0:64, p, :]) for p in range(3)])
                mm_group(pe, bC[0:1, EXTRA:2 * EXTRA], [(c_("pcode", 64)[:, p:p + 1], r_hot[0:64, p, :]) for p in range(3)])\
                    .then_inc(list_done[l], 1)

            def gather(l, a, pair):
                pe.wait_ge(sel_ready[l], pair + 1)
                for half, b in ((0, bA), (1, bB)):
                    for cc in range(4):
                        c = 4 * half + cc
                        m = mm_group(pe, b[:, cc * P:(cc + 1) * P],
                                     [(x_tok[:, t, c * P:(c + 1) * P], Sel[:, a, t, :]) for t in range(TT)])
                    m.then_inc(gath_done[l], 1)

            def scatter(l, a):
                for hh in range(2):
                    for t in range(TT):
                        m = pe.matmul(Ybank[t][hh][:, :], sgT[:, a, t, :], yb[:, a, hh * 512:(hh + 1) * 512],
                                      start=False, stop=False, skip_group_check=True)
                return m

            def experts(l):
                gather(l, 0, 0)
                pe.nop().then_inc(sgT_done[l], 1)
                pe.wait_ge(visits_ready[l], 1)
                n = pe.value_load(nquads[0:1, 0:1], min_val=QUADS, max_val=MAX_QUADS)
                with pe.Fori(0, n) as i:
                    for a in range(2):
                        pe.wait_ge(xgA_ready[l], i * 2 + (a + 1))
                        pe.wait_ge(xgB_ready[l], i * 2 + (a + 1))
                        pe.wait_ge(h_ready[l], i * 2 + (a + 1))
                        for s in range(2):
                            j = 2 * a + s
                            pe.wait_ge(loaded[l][j], i * 16 + 48)
                            w = slot(j, 0, DC, 2 * F_EXP)
                            for f in range(4):
                                at = (s * 4 + f) * SLOTS
                                m = mm_group(pe, bH[:, at:at + SLOTS],
                                             [(w[:, c, f * P:(f + 1) * P], xg[:, a, c, s * SLOTS:(s + 1) * SLOTS])
                                              for c in range(DC)])
                        m.then_inc(gu_done[l], 1)
                        pe.wait_ge(ybA_ready[l], i * 2 + (a + 1))
                        pe.wait_ge(ybB_ready[l], i * 2 + (a + 1))
                        gather(l, 1 - a, i * 2 + (a + 1))
                        pe.wait_ge(sgT_ready[l], i * 2 + (a + 1))
                        for t in range(TT):
                            m = pe.transpose(bC[:, t * P:(t + 1) * P], Selg[:, a, t, :], ident)
                        m.then_inc(sgT_done[l], 1)
                        scatter(l, 1 - a).then_inc(scat_done[l], 1)
                        pe.wait_ge(h_ready[l], i * 2 + (a + 2))
                        pe.wait_ge(xgA_ready[l], i * 2 + (a + 2))
                        pe.wait_ge(xgB_ready[l], i * 2 + (a + 2))
                        for hh, b in ((0, bA), (1, bB)):
                            for s in range(2):
                                w = ring[:, 2 * a + s, GU:SLOT_W].rearrange("p (f n) -> p f n", f=2)
                                m = mm_group(pe, b[s * SLOTS:(s + 1) * SLOTS, :],
                                             [(hT[:, a, f, s * SLOTS:(s + 1) * SLOTS], w[:, f, hh * 512:(hh + 1) * 512])
                                              for f in range(2)])
                            m.then_inc(down_done[l], 1)
                        pe.wait_ge(down_done[l], i * 4 + (2 * a + 2))
                        pe.nop().then_inc(used[l], 2)
                pe.wait_ge(ybA_ready[l], n * 2 + 1)
                pe.wait_ge(ybB_ready[l], n * 2 + 1)
                pe.wait_ge(sgT_ready[l], n * 2 + 1)
                scatter(l, 1).then_inc(moe_done[l], 1)

            pe.wait_ge(x_in, 32)
            for l in range(DEPTH):
                if l == 0:
                    projections(0, 0, len(JOBS0))
                else:
                    projections(1, 0, HID_AFTER)
                    compress()
                    projections(1, HID_AFTER, len(JOBS1))
                    compressed_attention()
                attention(l)
                output_projection(l)
                turn_x(2 * l)
                router(l)
                gate_up_shared(l)
                places(l)
                down_shared(l)
                visit_list(l)
                experts(l)
                if l + 1 < DEPTH:
                    turn_x(2 * l + 1)

        @block.scalar
        def _(act):
            steps = [0]

            def link(ins):
                steps[0] += 1
                ins.then_inc(act_step, 1)
                act.wait_ge(act_step, steps[0])

            def projections(l, lo, hi):
                for n in range(lo, hi):
                    b = bank[n % 4]
                    act.wait_ge(proj_done[l], n + 1)
                    for dst, src in JOBS[l][n][4]:
                        if isinstance(dst, str) and dst == "rope key":
                            m = act.copy(KTm[NOPE:QK_A, :, :],
                                         b[NOPE:QK_A, TOK:2 * TOK].unsqueeze(1).to_broadcast([ROPE, H_A, TOK]))
                        elif isinstance(dst, str):
                            m = act.activation(gates3[:, :, :].rearrange("p t k -> p (t k)"), b[:, 0:48], ACT.Exp, scale=-1.0)
                        else:
                            rows, c0, n_ = src
                            m = act.copy(dst, b[0:rows, c0:c0 + n_])
                    m.then_inc(proj_taken[l], 1)
                    if l == 0 and n == 2:
                        act.wait_ge(rms_var, 1)
                        act.activation(st[:, 0:4], st[:, 0:4], ACT.Sqrt).then_inc(rms_std, 1)

            def attention(l):
                for n in range(25):
                    if n < 24:
                        it = ITEMS[l][n]
                        act.wait_ge(max_ready[l], n + 1)
                        for t, c0, w in ((0, 0, P), (1, P, 2 * P)):
                            m = act.activation(probs[:, n % 2, c0:c0 + w], probs[:, n % 2, c0:c0 + w], ACT.Exp,
                                               bias=negmax[:, t, it["stat"]:it["stat"] + 1],
                                               accum_out=rowsum[:, t, it["stat"]:it["stat"] + 1])
                        m.then_inc(probs_ready[l], 1)
                    if n >= 1:
                        act.wait_ge(pt_done[l], n)
                        if n >= 3:
                            act.wait_ge(pv_done[l], n - 2)
                        act.copy(probsT[:, (n - 1) % 2, :], bank[2 + (n - 1) % 2][:, 0:3 * P]).then_inc(pt_taken[l], 1)
                    if l == 0 and n == 17:
                        act.wait_ge(comb_d, 1)
                        act.activation(wg[:, :, 0:12], wg[:, :, 0:12], ACT.Exp).then_inc(comb_w, 1)

            def output_projection(l):
                for k in range(4):
                    act.wait_ge(oT_done[l], k + 1)
                    act.copy(oT[:, 2 * k:2 * k + 2, :].rearrange("p a t -> p (a t)"), bank[k][:, :]).then_inc(oT_taken[l], 1)

            def norm(k):
                for t in range(TT):
                    act.wait_ge(ln_var, TT * k + t + 1)
                    act.activation(st[:, 16 + t:17 + t], st[:, 16 + t:17 + t], ACT.Sqrt).then_inc(ln_std, 1)

            def turn_x(k):
                for q in range(4):
                    act.wait_ge(xT_done, 4 * k + q + 1)
                    act.copy(xT[:, 2 * q:2 * q + 2, :].rearrange("p a t -> p (a t)"), bank[4 + q][:, :]).then_inc(xT_taken, 1)

            def experts(l):
                act.wait_ge(visits_ready[l], 1)
                n = act.value_load(nquads[0:1, 0:1], min_val=QUADS, max_val=MAX_QUADS)
                act.wait_ge(gath_done[l], 1)
                act.copy(xg[:, 0, 0:4, :].rearrange("p c s -> p (c s)"), bA[:, :]).then_inc(xgA_ready[l], 1)
                with act.Fori(0, n) as i:
                    for a in range(2):
                        act.wait_ge(gu_done[l], i * 2 + (a + 1))
                        act.activation(sil[:, a, :, :].rearrange("p f (s n) -> p s f n", s=2),
                                       bH[:, :].rearrange("p (s f n) -> p s f n", s=2, f=4)[:, :, 0:2, :],
                                       ACT.Silu).then_inc(silu_ready[l], 1)
                        act.wait_ge(gath_done[l], i * 4 + (2 * a + 3))
                        act.copy(xg[:, 1 - a, 0:4, :].rearrange("p c s -> p (c s)"), bA[:, :]).then_inc(xgA_ready[l], 1)
                        act.wait_ge(sgT_done[l], i * 2 + (a + 2))
                        act.copy(sgT[:, a, :, :].rearrange("p t s -> p (t s)"), bC[:, 0:TOK]).then_inc(sgT_ready[l], 1)
                        act.wait_ge(down_done[l], i * 4 + (2 * a + 1))
                        act.copy(yb[:, a, 0:512], bA[:, :]).then_inc(ybA_ready[l], 1)

            for l in range(DEPTH):
                if l == 0:
                    projections(0, 0, len(JOBS0))
                else:
                    act.wait_ge(lam_s, 1)
                    act.activation(lam[:, 0:2], lam[:, 0:2], ACT.Exp).then_inc(lam_e, 1)
                    projections(1, 0, HID_AFTER)
                    act.wait_ge(hid_z, 1)
                    act.activation(hid_t[:, 2:4, :], hid_t[:, 2:4, :], ACT.Exp, scale=-1.0).then_inc(hid_e, 1)
                    projections(1, HID_AFTER, len(JOBS1))
                    act.wait_ge(cmp_c, 1)
                    act.activation(ec[:, :, :, 0:NC_BLK], ec[:, :, :, 0:NC_BLK], ACT.Exp).then_inc(cmp_e, 1)
                    act.wait_ge(cmpT_done, 1)
                    act.copy(ecT[:, :, :, :].rearrange("p t g q -> p (t g q)"), bank[2][:, :]).then_inc(cmpT_taken, 1)
                attention(l)
                if l == 1:
                    act.wait_ge(dn_var, 1)
                    act.activation(st[:, 32:40], st[:, 32:40], ACT.Sqrt).then_inc(dn_std, 1)
                output_projection(l)
                norm(2 * l)
                turn_x(2 * l)
                act.wait_ge(logit_done[l], 1)
                act.activation(r_sc[:, :, :].rearrange("p t e -> p (t e)"), bC[:, 0:2 * EXPERTS], ACT.Exp, scale=-1.0)\
                   .then_inc(esig_ready[l], 1)
                act.wait_ge(sh_gu[l], 1)
                act.activation(sils[:, :, :].rearrange("p f t -> p (f t)"), bA[:, :], ACT.Silu).then_inc(sh_silu[l], 1)
                experts(l)
                norm(2 * l + 1)
                if l + 1 < DEPTH:
                    turn_x(2 * l + 1)

        @block.vector
        def _(dve):
            steps = [0]

            def link(ins):
                steps[0] += 1
                ins.then_inc(dve_step, 1)
                dve.wait_ge(dve_step, steps[0])

            TTen, TS, STT = dve.tensor_tensor, dve.tensor_scalar, dve.scalar_tensor_tensor

            def bias_rows():
                dve.wait_ge(bias_ps, 1)
                m = tmp[0:BIAS_ROWS, 448:448 + SPAN]
                TTen(m, bank[7][0:BIAS_ROWS, 0:SPAN], m, ALU.add).then_inc(bias_sb, 1)

            def latent_norms():
                dve.wait_ge(small_in, 48)
                link(dve.memset(cn[:, :, 384:448], 0.0))
                dve.wait_ge(proj_taken[0], 2)
                for t in range(TT):
                    for k, (c0, n) in enumerate(((0, Q_LORA), (Q_LORA, KV_LORA))):
                        link(dve.tensor_tensor_reduce(tmp[:, 0:n], ctok[:, t, c0:c0 + n], ctok[:, t, c0:c0 + n],
                                                      1.0 / n, RMS_EPS, ALU.mult, ALU.add, st[:, 2 * t + k:2 * t + k + 1]))
                dve.nop().then_inc(rms_var, 1)
                dve.wait_ge(rms_std, 1)
                link(dve.reciprocal(st[:, 4:8], st[:, 0:4]))
                for t in range(TT):
                    for k, (c0, n, g) in enumerate(((0, Q_LORA, "qn"), (Q_LORA, KV_LORA, "kvn"))):
                        STT(cn[:, t, c0:c0 + n], ctok[:, t, c0:c0 + n], st[:, 4 + 2 * t + k:5 + 2 * t + k],
                            s_(g), ALU.mult, ALU.mult)
                    cos, sin = (c_(k).rearrange("p (t f) -> p t f", t=TT)[:, t, :] for k in ("cos", "sin"))
                    k1, k2 = ctok[:, t, 384:400], ctok[:, t, 400:416]
                    u = tmp[:, 256 + 64 * t:320 + 64 * t].rearrange("p (a f) -> p a f", a=4)
                    TTen(u[:, 0, :], k1, cos, ALU.mult)
                    TTen(u[:, 1, :], k2, sin, ALU.mult)
                    TTen(u[:, 2, :], k1, sin, ALU.mult)
                    link(TTen(u[:, 3, :], k2, cos, ALU.mult))
                    TTen(cn[:, t, 448:464], u[:, 0, :], u[:, 1, :], ALU.subtract)
                    m = TTen(cn[:, t, 464:480], u[:, 2, :], u[:, 3, :], ALU.add)
                m.then_inc(cn_ready, 1)

            def rotate_queries():
                dve.wait_ge(scratch_out, 16)
                u = tmp[:, 0:768].rearrange("p (a h f) -> p a h f", a=4, h=H_A)
                for t in range(TT):
                    dve.wait_ge(proj_taken[0], N_Q - 3 * (1 - t))
                    cos, sin = (c_(k).rearrange("p (t f) -> p t f", t=TT)[:, t:t + 1, :].to_broadcast([P, H_A, HALF])
                                for k in ("cos", "sin"))
                    q = q_tok[:, t, :].rearrange("p (h e) -> p h e", h=H_A)
                    q1, q2 = q[:, :, NOPE:NOPE + HALF], q[:, :, NOPE + HALF:QK_A]
                    TTen(u[:, 0], q1, cos, ALU.mult)
                    TTen(u[:, 1], q2, sin, ALU.mult)
                    TTen(u[:, 2], q1, sin, ALU.mult)
                    link(TTen(u[:, 3], q2, cos, ALU.mult))
                    link(TTen(q1, u[:, 0], u[:, 1], ALU.subtract))
                    link(TTen(q2, u[:, 2], u[:, 3], ALU.add))
                    dve.nop().then_inc(q_roped, 1)

            def attention(l, first=0):
                dve.wait_ge(bias_in, 16 * (l + 1))
                for n in range(26):
                    if n < 24:
                        it, b = ITEMS[l][n], bank[n % 2]
                        dve.wait_ge(scores_done[l], n + 1)
                        if n >= 2:
                            dve.wait_ge(pt_done[l], n - 1)
                        STT(probs[:, n % 2, 0:P], b[:, 0:P], it["scale"], biasZ[:, it["bias"], 0:P][:, ::-1],
                            ALU.mult, ALU.add)
                        m = STT(probs[:, n % 2, P:3 * P], b[:, P:3 * P], it["scale"], biasZ[:, it["bias"], :][:, ::-1],
                                ALU.mult, ALU.add)
                        m.then_inc(scores_taken[l], 1)
                        dve.wait_ge(scores_taken[l], n + 1)
                        s = it["stat"]
                        dve.tensor_reduce(negmax[:, 0, s:s + 1], probs[:, n % 2, 0:P], X, ALU.max, negate=True)
                        dve.tensor_reduce(negmax[:, 1, s:s + 1], probs[:, n % 2, P:3 * P], X, ALU.max, negate=True)\
                           .then_inc(max_ready[l], 1)
                        if n == 23 and l == 0:
                            dve.nop().then_inc(bias_free, 1)
                    for g, end in enumerate(GROUP_END[l]):
                        if n == end + 1:
                            dve.wait_ge(pv_done[l], end)
                            (take0 if l == 0 else take1)(g)

            def inverse_sums(a, b):
                link(dve.reciprocal(rinv[:, :, a:b], rowsum[:, :, a:b]))

            def heads(ap, n):
                return ap.rearrange("p (h d) -> p h d", h=n)

            def spread(ap, n, w=HD):
                return ap.unsqueeze(2).to_broadcast([P, n, w])

            def take0(g):
                if g == 0:
                    for t in range(TT):
                        m = dve.tensor_copy(ob[:, t, :], o_bank(0, 0, t)[:, :])
                    m.then_inc(o_taken[0], 1)
                elif g == 1:
                    nm = negmax
                    link(TTen(wg[:, :, 12:16], nm[:, :, 0:4], nm[:, :, 4:8], ALU.min))
                    link(TTen(wg[:, :, 12:16], wg[:, :, 12:16], nm[:, :, 8:12], ALU.min))
                    for k in range(3):
                        m = TTen(wg[:, :, 4 * k:4 * k + 4], wg[:, :, 12:16], nm[:, :, 4 * k:4 * k + 4], ALU.subtract)
                    m.then_inc(comb_d, 1)
                    inverse_sums(12, 16)
                    for t in range(TT):
                        b = o_bank(0, 1, t)
                        TTen(heads(o_tok[:, t, 0:256], 4), heads(b[:, 256:512], 4), spread(rinv[:, t, 12:16], 4), ALU.mult)
                    dve.wait_ge(comb_w, 1)
                    link(TTen(tmp[:, 0:24].rearrange("p (t k) -> p t k", t=TT), wg[:, :, 0:12], rowsum[:, :, 0:12], ALU.mult))
                    u = tmp[:, 0:24].rearrange("p (t k) -> p t k", t=TT)
                    link(TTen(wg[:, :, 12:16], u[:, :, 0:4], u[:, :, 4:8], ALU.add))
                    link(TTen(wg[:, :, 12:16], wg[:, :, 12:16], u[:, :, 8:12], ALU.add))
                    link(dve.reciprocal(wg[:, :, 16:20], wg[:, :, 12:16]))
                    for k in range(3):
                        m = TTen(rinv[:, :, 4 * k:4 * k + 4], wg[:, :, 4 * k:4 * k + 4], wg[:, :, 16:20], ALU.mult)
                    link(m)
                    for t in range(TT):
                        o = heads(o_tok[:, t, 768:1024], 4)
                        link(TTen(o, heads(o_bank(0, 1, t)[:, 0:256], 4), spread(rinv[:, t, 8:12], 4), ALU.mult))
                        link(TTen(heads(ob[:, t, :], 8), heads(ob[:, t, :], 8), spread(rinv[:, t, 0:8], 8), ALU.mult))
                        link(TTen(o, o, heads(ob[:, t, 0:256], 4), ALU.add))
                        link(TTen(o, o, heads(ob[:, t, 256:512], 4), ALU.add))
                    dve.nop().then_inc(o_taken[0], 1)
                else:
                    inverse_sums(16, 24)
                    for t in range(TT):
                        m = TTen(heads(o_tok[:, t, 256:768], 8), heads(o_bank(0, 2, t)[:, :], 8),
                                 spread(rinv[:, t, 16:24], 8), ALU.mult)
                    m.then_inc(o_ready[0], 1)

            def take1(g):
                if g < 2:
                    inverse_sums(8 * g, 8 * g + 8)
                    a, b = 8 * g, 8 * g + 8
                    link(TTen(rinv[:, :, a:b], rinv[:, :, a:b], gates3[:, :, a + 8:b + 8], ALU.mult))
                    for t in range(TT):
                        link(TTen(heads(tmp[:, 0:512], 8), heads(o_bank(1, g, t)[:, :], 8), spread(rinv[:, t, a:b], 8), ALU.mult))
                        link(TTen(o_tok[:, t, 0:512], o_tok[:, t, 0:512], tmp[:, 0:512], ALU.add))
                    dve.nop().then_inc(o_taken[1], 1)
                    return
                k = 2 * (g - 2)
                inverse_sums(16 + k, 18 + k)
                inverse_sums(20 + k, 22 + k)
                link(TS(rinv[:, :, 20 + k:22 + k], rinv[:, :, 20 + k:22 + k], lam[:, 2:3], None, ALU.mult))
                for t in range(TT):
                    b = o_bank(1, g, t)[:, :].rearrange("p (h m d) -> p h m d", h=2, m=2)
                    o = heads(o_tok[:, t, 512 + k * P:512 + (k + 2) * P], 2)
                    u = heads(tmp[:, 0:256], 2)
                    TTen(o, b[:, :, 0, :], spread(rinv[:, t, 16 + k:18 + k], 2, P), ALU.mult)
                    link(TTen(u, b[:, :, 1, :], spread(rinv[:, t, 20 + k:22 + k], 2, P), ALU.mult))
                    link(TTen(o, o, u, ALU.add))
                dve.nop().then_inc(o_taken[1], 1)
                if g == 3:
                    for t in range(TT):
                        od = o_tok[:, t, 512:1024]
                        link(TTen(tmp[:, 0:512], od, od, ALU.mult))
                        link(dve.tensor_reduce(st[:, 32 + 4 * t:36 + 4 * t], heads(tmp[:, 0:512], 4), X, ALU.add))
                    link(TS(st[:, 32:40], st[:, 32:40], 1.0 / P, RMS_EPS, ALU.mult, ALU.add))
                    dve.nop().then_inc(dn_var, 1)
                    dve.wait_ge(dn_std, 1)
                    link(dve.reciprocal(st[:, 40:48], st[:, 32:40]))
                    link(TS(st[:, 40:48], st[:, 40:48], 1.0 - LAM_INIT, None, ALU.mult))
                    for t in range(TT):
                        od = heads(o_tok[:, t, 512:1024], 4)
                        link(TTen(od, od, spread(st[:, 40 + 4 * t:44 + 4 * t], 4, P), ALU.mult))
                        link(TTen(od, od, s_("dn").unsqueeze(1).to_broadcast([P, 4, P]), ALU.mult))
                    dve.nop().then_inc(o_ready[1], 1)

            def norm(k, arrived):
                for t in range(TT):
                    arrived(t)
                    if k >= 1:
                        dve.wait_ge(ln_free, k)
                    for hh in range(2):
                        cols = slice(hh * 512, (hh + 1) * 512)
                        link(STT(z[:, t, cols], x_tok[:, t, cols], ALPHA, Ybank[t][hh][:, :], ALU.mult, ALU.add))
                        link(dve.bn_stats(st[:, 48 + 6 * hh:54 + 6 * hh], z[:, t, cols]))
                    link(dve.bn_aggr(st[:, 20 + 2 * t:22 + 2 * t], st[:, 48:60]))
                    link(TS(st[:, 16 + t:17 + t], st[:, 21 + 2 * t:22 + 2 * t], LN_EPS, None, ALU.add))
                    dve.nop().then_inc(ln_var, 1)
                dve.wait_ge(ln_in, 16 * (k + 1))
                for t in range(TT):
                    dve.wait_ge(ln_std, TT * k + t + 1)
                    link(dve.reciprocal(st[:, 18 + t:19 + t], st[:, 16 + t:17 + t]))
                    link(TS(z[:, t, :], z[:, t, :], st[:, 20 + 2 * t:21 + 2 * t], st[:, 18 + t:19 + t],
                            ALU.subtract, ALU.mult))
                    TTen(z[:, t, :], z[:, t, :], lng[:, 0, :], ALU.mult).then_inc(ln_gained, 1)

            def router(l):
                dve.wait_ge(esig_ready[l], 1)
                link(TS(r_sc, r_sc, 1.0, None, ALU.add))
                link(dve.reciprocal(r_sc, r_sc))
                rb = s_("rb").rearrange("p (l e) -> p l e", l=DEPTH)[:, l:l + 1, :].to_broadcast([P, TT, EXPERTS])
                link(TTen(r_sel, r_sc, rb, ALU.add))
                for t in range(TT):
                    for g in range(GROUPS):
                        m = dve.max(r_m8[:, t, 8 * g:8 * g + 8], r_sel[:, t, 8 * g:8 * g + 8])
                link(m)
                best = r_m8.rearrange("p t (g k) -> p t g k", g=GROUPS)
                link(TTen(r_gs, best[:, :, :, 0], best[:, :, :, 1], ALU.add))
                for t in range(TT):
                    other = r_gs[:, t:t + 1, :].to_broadcast([P, GROUPS, GROUPS])
                    own = r_gs[:, t, :].unsqueeze(2).to_broadcast([P, GROUPS, GROUPS])
                    TTen(r_gt, other, own, ALU.is_gt)
                    link(TTen(r_eq, other, own, ALU.is_equal))
                    link(TTen(r_eq, r_eq, c_("gtri").rearrange("p (a b) -> p a b", a=GROUPS), ALU.mult))
                    link(TTen(r_gt, r_gt, r_eq, ALU.add))
                    link(dve.tensor_reduce(r_rank[:, t, :], r_gt, X, ALU.add))
                link(TS(r_gm, r_rank, TOP_GROUPS - 0.5, None, ALU.is_lt))
                link(TS(r_rank, r_gm, 1.0, -NEG, ALU.subtract, ALU.mult))
                for t in range(TT):
                    sel, selm = (heads(r[:, t, :], GROUPS) for r in (r_sel, r_selm))
                    link(TTen(selm, sel, spread(r_gm[:, t, :], GROUPS, 8), ALU.mult))
                    link(TTen(selm, selm, spread(r_rank[:, t, :], GROUPS, 8), ALU.add))
                    link(dve.max(r_top[:, t, :], r_selm[:, t, :]))
                    link(dve.match_replace(r_rep[:, t, :], r_top[:, t, :], r_selm[:, t, :], -3e38))
                link(TS(r_mask, r_rep, -2e38, None, ALU.is_lt))
                dve.nop().then_inc(mask_ready[l], 1)
                link(TTen(r_gate, r_sc, r_mask, ALU.mult))
                link(dve.tensor_reduce(r_den, r_gate, X, ALU.add))
                link(dve.reciprocal(r_den, r_den))
                link(TS(r_den, r_den, ROUTED_SCALE, None, ALU.mult))
                link(TTen(r_gate, r_gate, r_den.unsqueeze(2).to_broadcast([P, TT, EXPERTS]), ALU.mult))
                dve.wait_ge(pos_done[l], 1)
                link(STT(r_pos, bC[:, 0:2 * EXPERTS].rearrange("p (t e) -> p t e", t=TT), 1.0, r_mask, ALU.add, ALU.mult))
                link(TS(r_pos, r_pos, -1.0, None, ALU.add))
                dve.memset(r_ov[0:64, 3:4], 0.0)
                dve.memset(r_ovp[0:64, 0:1], 0.0)
                link(TTen(r_ov[0:64, 0:3], c_("thr", 64), bC[0:64, 128:129].to_broadcast([64, 3]), ALU.is_lt))
                link(dve.tensor_copy(r_ovp[0:64, 1:2], r_ov[0:64, 0:1]))
                link(TTen(r_ovp[0:64, 2:3], r_ovp[0:64, 1:2], r_ov[0:64, 1:2], ALU.add))
                link(TTen(r_ovp[0:64, 3:4], r_ovp[0:64, 2:3], r_ov[0:64, 2:3], ALU.add))
                dve.nop().then_inc(over_ready[l], 1)

            def shared_hidden(l):
                dve.wait_ge(sh_silu[l], 1)
                TTen(hTs[:, :, :].rearrange("p f t -> p (f t)"), sils[:, :, :].rearrange("p f t -> p (f t)"), bB[:, :],
                     ALU.mult).then_inc(sh_h[l], 1)

            def visit_list(l):
                dve.wait_ge(idx_done[l], 1)
                link(dve.tensor_copy(r_idx[0:64, :], bC[0:64, 0:4]))
                for p in range(3):
                    m = TS(r_hot[0:64, p, :], c_("kiota", 64), r_idx[0:64, p:p + 1], r_ov[0:64, p:p + 1],
                           ALU.is_equal, ALU.mult)
                m.then_inc(hot_ready[l], 1)
                link(dve.memset(visit_f[0:1, 0, :], 0.0))
                link(dve.memset(visit_f[0:1, 1, :], float(SLOTS * PASSES)))
                dve.memset(visit_f[0:1, 1, 0:EXPERTS], 0.0)
                dve.tensor_copy(visit_f[0:1, 0, 0:EXPERTS], c_("base", 1))
                link(TS(r_q[0:1, :], c_("quad4", 1), r_idx[0:1, 3:4], None, ALU.is_lt))
                link(dve.tensor_reduce(r_den[0:1, 0:1], r_q[0:1, :], X, ALU.add))
                link(TS(r_den[0:1, 0:1], r_den[0:1, 0:1], float(QUADS), None, ALU.add))
                dve.tensor_copy(nquads[0:1, 0:1], r_den[0:1, 0:1])
                dve.wait_ge(list_done[l], 1)
                link(dve.tensor_copy(r_list[0:1, :, :].rearrange("p a k -> p (a k)"), bC[0:1, 0:2 * EXTRA]))
                link(TS(r_hot[0:1, 0, :], r_list[0:1, 1, :], 0.0, float(SLOTS * PASSES), ALU.is_equal, ALU.mult))
                TTen(visit_f[0:1, 1, EXPERTS:EXPERTS + EXTRA], r_list[0:1, 1, :], r_hot[0:1, 0, :], ALU.add)
                link(dve.tensor_copy(visit_f[0:1, 0, EXPERTS:EXPERTS + EXTRA], r_list[0:1, 0, :]))
                link(dve.tensor_copy(visit[0:1, :, :], visit_f[0:1, :, :]))
                dve.nop().then_inc(visits_ready[l], 1)

            def select(l, a, first):
                for s in range(2):
                    at = first + (2 * a + s)
                    e = dve.value_load(visit[0:1, 0, bass.ds(at, 1)], min_val=0, max_val=EXPERTS - 1)
                    off = dve.value_load(visit[0:1, 1, bass.ds(at, 1)], min_val=0, max_val=SLOTS * PASSES)
                    cols = slice(s * SLOTS, (s + 1) * SLOTS)
                    base = CONST["iota"][0]
                    for t in range(TT):
                        place = r_pos[:, t, bass.ds(e, 1)]
                        slot_no = cst[:, bass.ds(off + base, SLOTS)]
                        TS(Sel[:, a, t, cols], slot_no, place, None, ALU.is_equal)
                        m = TS(Selg[:, a, t, cols], slot_no, place, r_gate[:, t, bass.ds(e, 1)], ALU.is_equal, ALU.mult)
                m.then_inc(sel_ready[l], 1)

            def experts(l):
                dve.memset(yb[:, 1, 0:512], 0.0).then_inc(ybA_ready[l], 1)
                dve.memset(yb[:, 1, 512:1024], 0.0).then_inc(ybB_ready[l], 1)
                dve.memset(sgT[:, 1, :, :], 0.0).then_inc(sgT_ready[l], 1)
                dve.nop().then_inc(h_ready[l], 1)
                select(l, 0, 0)
                n = dve.value_load(nquads[0:1, 0:1], min_val=QUADS, max_val=MAX_QUADS)
                dve.wait_ge(gath_done[l], 2)
                dve.tensor_copy(xg[:, 0, 4:8, :].rearrange("p c s -> p (c s)"), bB[:, :]).then_inc(xgB_ready[l], 1)
                with dve.Fori(0, n) as i:
                    for a in range(2):
                        dve.wait_ge(gath_done[l], i * 4 + (2 * a + 2))
                        if a:
                            dve.wait_ge(sgT_done[l], i * 2 + 2)
                            select(l, 0, i * 4 + 2 + 2)
                        else:
                            dve.wait_ge(sgT_done[l], i * 2 + 1)
                            select(l, 1, i * 4)
                        dve.wait_ge(silu_ready[l], i * 2 + (a + 1))
                        TTen(hT[:, a, :, :].rearrange("p f (s n) -> p s f n", s=2),
                             sil[:, a, :, :].rearrange("p f (s n) -> p s f n", s=2),
                             bH[:, :].rearrange("p (s f n) -> p s f n", s=2, f=4)[:, :, 2:4, :],
                             ALU.mult).then_inc(h_ready[l], 1)
                        dve.wait_ge(gath_done[l], i * 4 + (2 * a + 4))
                        dve.tensor_copy(xg[:, 1 - a, 4:8, :].rearrange("p c s -> p (c s)"), bB[:, :])\
                           .then_inc(xgB_ready[l], 1)
                        dve.wait_ge(down_done[l], i * 4 + (2 * a + 2))
                        dve.tensor_copy(yb[:, a, 512:1024], bB[:, :]).then_inc(ybB_ready[l], 1)

            def compress():
                dve.wait_ge(proj_taken[1], KCMP_JOB)
                for kv in range(2):
                    src = KTc[:, kv, :]
                    win = bass.AP(src.tensor, src.offset, [src.ap[0], (1, CMP_LEN), (CMP_STRIDE, NC_BLK)])
                    m = TTen(Xw[:, kv, :, :], win, posT[:, kv, :].unsqueeze(2).to_broadcast([P, CMP_LEN, NC_BLK]), ALU.add)
                m.then_inc(win_ready, 1)
                dve.memset(hid4[:, :, :], 0.0)
                dve.memset(VBD[:, :, :, :], 0.0)
                link(dve.memset(ec[:, :, :, :], 0.0))
                dve.wait_ge(hid_done, 1)
                for g in range(G_C):
                    r = slice(64 * g, 64 * g + 64)
                    m = dve.tensor_copy(hid_t[r, 0:2, 0:NC_BLK],
                                        bank[6 + g][r, 0:32].rearrange("p (a c) -> p a c", a=2)[:, :, 0:NC_BLK])
                link(m)
                h, u = hid_t[:, 0:2, 0:NC_BLK], hid_t[:, 2:4, 0:NC_BLK]
                link(TTen(u, h, h, ALU.mult))
                link(TS(u, u, 0.044715, 1.0, ALU.mult, ALU.add))
                link(TTen(u, u, h, ALU.mult))
                link(TS(u, u, 2.0 * math.sqrt(2.0 / math.pi), None, ALU.mult))
                dve.nop().then_inc(hid_z, 1)
                dve.wait_ge(hid_e, 1)
                link(TS(u, u, 1.0, None, ALU.add))
                link(dve.reciprocal(u, u))
                link(TTen(hid[:, :, 0:NC_BLK], h, u, ALU.mult))
                link(dve.tensor_copy(hid4[:, :, 0:NC_BLK], hid[:, 1:2, 0:NC_BLK].to_broadcast([P, 4, NC_BLK])))
                dve.nop().then_inc(hid_ready, 1)
                dve.wait_ge(kv_done, 1)
                for g in range(G_C):
                    r = slice(64 * g, 64 * g + 64)
                    dve.tensor_copy(kcT[r, 0:NC_BLK], bank[6 + g][r, 64:64 + NC_BLK])
                    for h4 in range(4):
                        q = slice(32 * h4, 32 * h4 + 32)
                        m = dve.tensor_copy(VBD[q, g, h4, :], bank[6 + g][q, 128:192])
                m.then_inc(kv_taken, 1)

            def gates_and_lambda():
                l1 = s_("lam").rearrange("p (a d) -> p a d", a=4)
                dve.tensor_tensor_reduce(tmp[:, 0:64], l1[:, 0, :], l1[:, 1, :], 1.0, 0.0, ALU.mult, ALU.add, lam[:, 0:1])
                dve.tensor_tensor_reduce(tmp[:, 64:128], l1[:, 2, :], l1[:, 3, :], 1.0, 0.0, ALU.mult, ALU.add,
                                         lam[:, 1:2]).then_inc(lam_s, 1)
                dve.wait_ge(lam_e, 1)
                link(TTen(lam[:, 2:3], lam[:, 1:2], lam[:, 0:1], ALU.subtract))
                link(TS(lam[:, 2:3], lam[:, 2:3], -LAM_INIT, None, ALU.add))
                dve.wait_ge(proj_taken[1], 3)
                link(TS(gates3[:, :, :], gates3[:, :, :], 1.0, None, ALU.add))
                link(dve.reciprocal(gates3[:, :, :], gates3[:, :, :]))

            def compressed_softmax():
                dve.wait_ge(cmp_s, 1)
                dve.wait_ge(bias_in, 32)
                seen = [7, NC_BLK]
                link(dve.memset(ec[:, 0, :, seen[0]:NC_BLK], NEG))
                for t in range(TT):
                    first = P * t + P - 1 - (CMP_LEN - 1)
                    for g in range(G_C):
                        n = seen[t]
                        zz = biasZ[:, 4 * g:4 * g + 4, :]
                        bias = bass.AP(zz.tensor, zz.offset + first, [zz.ap[0], (TOK, 4), (-CMP_STRIDE, n)])
                        s = bank[g][:, t * 64:(t + 1) * 64].rearrange("p (r c) -> p r c", r=R_C)[:, :, 0:n]
                        m = STT(ec[:, t, 4 * g:4 * g + 4, 0:n], s, HD ** -0.5, bias, ALU.mult, ALU.add)
                link(m)
                e = ec[:, :, :, 0:NC_BLK].rearrange("p t h c -> p (t h) c")
                cmax, csum = cs[:, 0, :], cs[:, 1, :]
                link(dve.tensor_reduce(cmax, e, X, ALU.max))
                link(TTen(e, e, cmax.unsqueeze(2).to_broadcast([P, 16, NC_BLK]), ALU.subtract))
                dve.nop().then_inc(cmp_c, 1)
                dve.wait_ge(cmp_e, 1)
                for t in range(TT):
                    v = c_("valid").rearrange("p (t c) -> p t c", t=TT)[:, t:t + 1, 0:NC_BLK].to_broadcast([P, H_C, NC_BLK])
                    m = TTen(ec[:, t, :, 0:NC_BLK], ec[:, t, :, 0:NC_BLK], v, ALU.mult)
                link(m)
                dve.nop().then_inc(cmp_p, 1)
                link(dve.tensor_reduce(csum, e, X, ALU.add))
                link(TS(csum, csum, 1e-30, None, ALU.max))
                link(dve.reciprocal(csum, csum))
                link(TTen(csum.rearrange("p (t h) -> p t h", t=TT), csum.rearrange("p (t h) -> p t h", t=TT),
                          gates3[:, :, 0:8], ALU.mult))
                dve.wait_ge(cmp_o, 1)
                for t in range(TT):
                    m = TTen(heads(o_tok[:, t, 0:512], 8), heads(bank[6 + t][:, :], 8),
                             spread(csum[:, 8 * t:8 * t + 8], 8), ALU.mult)
                link(m)

            bias_rows()
            for l in range(DEPTH):
                if l == 0:
                    latent_norms()
                    rotate_queries()
                else:
                    gates_and_lambda()
                    compress()
                    compressed_softmax()
                attention(l)
                norm(2 * l, lambda t, l=l: dve.wait_ge(y_done[l], 4))
                router(l)
                shared_hidden(l)
                visit_list(l)
                experts(l)
                norm(2 * l + 1, lambda t, l=l: dve.wait_ge(moe_done[l], 1))


def _constants():
    c = np.zeros((P, N_CONST), np.float32)

    def put(name, a):
        at, n = CONST[name]
        a = np.asarray(a, np.float32)
        c[:a.shape[0], at:at + n] = a.reshape(a.shape[0], n)

    p = np.arange(P)
    put("ident", np.eye(P))
    put("tri", p[:, None] < p[None, :])
    put("ones", np.ones((P, P)))
    put("iota", np.tile(np.arange(SLOTS * (PASSES + 1)), (P, 1)))
    freqs = np.float32(10000.0) ** (-np.arange(HALF, dtype=np.float32) / np.float32(HALF))
    ang = (np.arange(TOK, dtype=np.float32)[:, None] * freqs).astype(np.float32)
    for name, f in (("cos", np.cos), ("sin", np.sin)):
        put(name, f(ang).reshape(TT, P, HALF).transpose(1, 0, 2))
    tok = np.arange(TOK).reshape(TT, P).T
    put("valid", (tok[:, :, None] - (np.arange(16) * CMP_STRIDE + CMP_LEN - 1)) >= 0)
    g = np.arange(GROUPS)
    put("gtri", np.tile((g[None, :] < g[:, None]).reshape(1, -1), (P, 1)))
    put("kiota", np.tile(np.arange(EXTRA), (64, 1)))
    put("thr", np.tile(SLOTS * np.arange(1, PASSES), (64, 1)))
    put("ecode", np.arange(EXPERTS)[:, None])
    put("pcode", np.tile(SLOTS * np.arange(1, PASSES), (64, 1)))
    put("base", np.arange(EXPERTS)[None, :])
    put("quad4", 4 * np.arange(8)[None, :])

    d = np.arange(SPAN) - (P - 1)
    n = np.maximum(d, 0)
    ratio = (np.log(np.maximum(n, 1).astype(np.float32) / np.float32(16)) / np.float32(math.log(2048 / 16))).astype(np.float32)
    large = 16 + (ratio * np.float32(16)).astype(np.int32)
    bucket = np.where(n < 16, n, np.minimum(large, BUCKETS - 1))
    hot = (bucket[None, :] == np.arange(BUCKETS)[:, None]).astype(np.float32)
    mask = np.where(d < 0, NEG, 0.0)[None, :].repeat(BIAS_ROWS, 0)
    mask[0:4] = np.where((d < 0) | (d > 128), NEG, 0.0)
    mask[4:8] = np.where((d < 0) | (d % 4 != 0), NEG, 0.0)
    mask[8:12] = np.where((d < 0) | (d % 16 != 0), NEG, 0.0)
    return c, hot, mask.astype(np.float32)


def _chunks(w):
    r, n = w.shape
    return w.reshape(r // P, P, n).transpose(1, 0, 2).reshape(P, -1)


def _lay_out(a):
    f = np.float32
    mix = np.zeros((DEPTH, MIX_BLOCKS - 1, P, SLOT_W), f)

    def put(l, k, *parts):
        at = 0
        for p in parts:
            mix[l, k, :, at:at + p.shape[1]] = p
            at += p.shape[1]

    w = a["ab_w_in"][0]
    put(0, 0, _chunks(w[:, :C_IN]))
    for k in range(3):
        put(0, 1 + k, _chunks(w[:, C_IN + 768 * k:C_IN + 768 * (k + 1)]))
    put(0, 4, _chunks(a["mla_w_uq"][0]), a["mla_w_ukv"][0])
    w = a["cd_w_in"][0]
    qc = w[:, :512].reshape(D, G_C, R_C, HD).transpose(0, 2, 1, 3).reshape(D, 512)
    put(1, 0, _chunks(np.concatenate([qc, w[:, 1280:1304]], 1)))
    order = [0, 1, 2, 4, 3, 5]
    put(1, 1, _chunks(np.concatenate([w[:, 512 + P * i:512 + P * (i + 1)] for i in order], 1)))
    for k in range(2):
        w1 = a[("nsa_cmp_k_w1", "nsa_cmp_v_w1")[k]][0].reshape(CMP_LEN, HD, 64).transpose(1, 0, 2).reshape(HD, -1)
        put(1, 2 + k, _chunks(w[:, 1304 + 512 * k:1304 + 512 * (k + 1)]), np.concatenate([w1, w1], 0))
    put(1, 4, _chunks(w[:, 2328:2840]))
    for l, name in enumerate(("ab_w_out", "cd_w_out")):
        for hh in range(2):
            put(l, 5 + hh, _chunks(a[name][0][:, hh * 512:(hh + 1) * 512]))
    exp = np.empty((DEPTH, EXPERTS + 1, P, SLOT_W), f)
    gu = exp[..., :GU].reshape(DEPTH, EXPERTS + 1, P, DC, 2, F_EXP)
    dn = exp[..., GU:].reshape(DEPTH, EXPERTS + 1, P, 2, D)
    for l in range(DEPTH):
        for k, (r, s) in enumerate((("exp_w_gate", "sh_w_gate"), ("exp_w_up", "sh_w_up"))):
            gu[l, :EXPERTS, :, :, k] = a[r][l].reshape(EXPERTS, DC, P, F_EXP).transpose(0, 2, 1, 3)
            gu[l, EXPERTS, :, :, k] = a[s][l].reshape(DC, P, F_EXP).transpose(1, 0, 2)
        dn[l, :EXPERTS] = a["exp_w_down"][l].reshape(EXPERTS, 2, P, D).transpose(0, 2, 1, 3)
        dn[l, EXPERTS] = a["sh_w_down"][l].reshape(2, P, D).transpose(1, 0, 2)
    exp[..., :GU] = gu.reshape(DEPTH, EXPERTS + 1, P, GU)
    exp[..., GU:] = dn.reshape(DEPTH, EXPERTS + 1, P, 2 * D)
    const, hot, mask = _constants()
    x = a["x"][0]
    rel = a["rel_bias"]
    small = np.concatenate([a["mla_q_norm"][0], a["mla_kv_norm"][0], a["diff_norm"][0]]
                           + [a[f"diff_lambda_{n}"][0] for n in ("q1", "k1", "q2", "k2")]
                           + [a["router_b"].reshape(-1)])[None, :]
    return {
        "x": x, "xT_in": np.ascontiguousarray(x.T), "mixw": mix, "expw": exp, "const": const,
        "tab": np.concatenate([rel[:, :12], np.zeros((BUCKETS, 1), f), rel[:, 12:]], 1),
        "hot": hot, "mask": mask, "small": small,
        "lnp": np.stack([np.concatenate([a[f"ln{h}_g"][l], a[f"ln{h}_b"][l]]) for l in range(DEPTH) for h in (1, 2)]),
        "routw": a["router_w"].reshape(DEPTH, DC, P, EXPERTS).transpose(0, 2, 1, 3),
        "pos": np.tile(np.stack([a["nsa_cmp_pos_k"][0].T, a["nsa_cmp_pos_v"][0].T], 1), (2, 1, 1)),
        "w2": np.tile(np.stack([a["nsa_cmp_k_w2"][0], a["nsa_cmp_v_w2"][0]], 1), (2, 1, 1)),
    }


def kernel(**inputs):
    import concourse.bacc as _bacc
    from concourse.bass_utils import run_bass_kernel_spmd as _run

    arrays = {k: np.ascontiguousarray(v) for k, v in _lay_out({k: np.asarray(v) for k, v in inputs.items()}).items()}
    nc = _bacc.Bacc("TRN2", target_bir_lowering=False, num_devices=1)
    args = {k: nc.dram_tensor(f"in_{k}", v.shape, mybir.dt.float32, kind="ExternalInput").ap() for k, v in arrays.items()}
    out = nc.dram_tensor("out_0_dram", (TOK, D), mybir.dt.float32, kind="ExternalOutput").ap()
    build(nc, out=out, **args)
    r = _run(nc, [{f"in_{k}": v for k, v in arrays.items()}], core_ids=[0])
    return r.results[0]["out_0_dram"].reshape(1, TOK, D)
```

```python
import math
from contextlib import ExitStack

import numpy as np

import concourse.bass as bass
from concourse import mybir

P = 128
TOK = 256
TT = TOK // P
D = 1024
DC = D // P
DEPTH = 2
ALPHA = (2 * DEPTH) ** 0.25
LN_EPS, RMS_EPS = 1e-5, 1e-6
NEG = -1e30

H_A, NOPE, ROPE, MLA_V = 12, 64, 32, 64
Q_LORA, KV_LORA = 256, 128
QK_A = NOPE + ROPE
HALF = ROPE // 2
H_B, HD = 12, 64
H_C, G_C, R_C = 8, 2, 4
H_D = 4
CMP_LEN, CMP_STRIDE = 32, 16
NC_BLK = (TOK - CMP_LEN) // CMP_STRIDE + 1
LAM_INIT = 0.8 - 0.6 * math.exp(-0.3 * 1)
BUCKETS = 32

EXPERTS, TOP_K, GROUPS, TOP_GROUPS = 64, 8, 8, 4
F_EXP = 256
ROUTED_SCALE = 2.5
SLOTS = 64
PASSES = TOK // SLOTS
EXTRA = TOK * TOP_K // SLOTS
QUADS = EXPERTS // 4
MAX_QUADS = QUADS + EXTRA // 4
VISITS = 4 * (MAX_QUADS + 1)

C_IN = Q_LORA + KV_LORA + ROPE
GU = DC * 2 * F_EXP
SLOT_W = GU + 2 * D
RING = 4
MIX_BLOCKS = 8
MIX_SIZE = [[DC * C_IN, DC * 768, DC * 768, DC * 768, 2 * 1152 + 1536, DC * 512, DC * 512],
            [DC * 536, DC * 768, DC * 512 + 2048, DC * 512 + 2048, DC * 512, DC * 512, DC * 512]]

SPAN = P + TOK - 1
BIAS_ROWS = 25
BIAS_OF = [(0, 13), (13, 12)]

CONST = {}
_at = 0
for _name, _n in (("ident", P), ("tri", P), ("ones", P), ("iota", SLOTS * (PASSES + 1)),
                  ("cos", TT * HALF), ("sin", TT * HALF), ("valid", TT * 16), ("gtri", 64),
                  ("kiota", EXTRA), ("thr", 3), ("ecode", 1), ("pcode", 3), ("base", EXPERTS), ("quad4", 8)):
    CONST[_name] = (_at, _n)
    _at += _n
N_CONST = _at
SMALL = {"qn": (0, 256), "kvn": (256, 128), "dn": (384, 128), "lam": (512, 256), "rb": (768, 128)}
N_SMALL = 896


def build(nc, x, xT_in, mixw, expw, const, tab, hot, mask, small, lnp, routw, pos, w2, out):
    F32, FR, I32 = mybir.dt.float32, mybir.dt.float32r, mybir.dt.int32
    ALU, ACT = mybir.AluOpType, mybir.ActivationFunctionType
    X = mybir.AxisListType.X
    scratch = nc.dram_tensor("bias_rows_dram", (BIAS_ROWS, SPAN), F32, kind="Internal").ap()

    with ExitStack() as ctx:
        def sb(name, shape, dt=F32):
            return ctx.enter_context(nc.sbuf_tensor(name, shape, dt))

        def sem(name):
            return ctx.enter_context(nc.semaphore(name))

        def per_layer(name):
            return [sem(f"{name}_{l}") for l in range(DEPTH)]

        bank = [ctx.enter_context(nc.psum_tensor(f"bank{i}", [P, 512], F32)) for i in range(8)]
        Ybank = [[bank[2 * t + hh] for hh in range(2)] for t in range(TT)]
        bA, bB, bC, bH = bank[4], bank[5], bank[6], bank[7]

        ring = sb("ring", [P, RING, SLOT_W])
        x_tok = sb("x_tok", [P, TT, D])

        def shared_space(name, words, *views):
            offset = nc.sbuf_base
            sb(name, [P, words])
            return [nc.alloc_sbuf_tensor_at(n, shape, dt, offset=offset + 4 * at) for n, shape, dt, at in views]

        xT = sb("xT", [P, DC, TOK])
        zb, x_high = shared_space("z_space", TT * 1152, ("zb", [P, TT * 1152], F32, 0), ("x_high", [P, TT, D], FR, 0))
        biasZ, x_low = shared_space("bias_space", 13 * TOK, ("biasZ", [P, 13, TOK], F32, 0), ("x_low", [P, TT, D], FR, 0))
        arena, Sel, y_high, y_low, selT = shared_space(
            "arena_space", 12288, ("arena", [P, 12288], F32, 0), ("Sel", [P, 2, TT, P], FR, 5632),
            ("y_high", [P, D], FR, 2048), ("y_low", [P, D], FR, 3072), ("selT", [P, 2, TOK], FR, 4096))
        probs = sb("probs", [P, 3, 3 * P])
        probsT = sb("probsT", [P, 2, 3 * P])
        tmp = sb("tmp", [P, 832])
        cst = sb("cst", [P, N_CONST])
        sml = sb("sml", [P, N_SMALL])
        rw = sb("rw", [P, DC, EXPERTS])
        posT = sb("posT", [P, 2, CMP_LEN])
        w2s = sb("w2s", [P, 2, HD])
        negmax = sb("negmax", [P, TT, 24])
        rowsum = sb("rowsum", [P, TT, 24])
        rinv = sb("rinv", [P, TT, 24])
        gates3 = sb("gates3", [P, TT, 24])
        wg = sb("wg", [P, TT, 24])
        st = sb("st", [P, 64])
        lam = sb("lam", [P, 8])
        visit = sb("visit", [1, 2, VISITS], I32)
        nquads = sb("nquads", [1, 4], I32)

        def area(at, *shape):
            n = int(np.prod(shape))
            ap = arena[:, at:at + n]
            if len(shape) > 1:
                names = "abcd"[:len(shape)]
                ap = ap.rearrange(f"p ({' '.join(names)}) -> p {' '.join(names)}",
                                  **{k: v for k, v in zip(names[1:], shape[1:])})
            return ap

        def zview(at, *shape):
            n = int(np.prod(shape))
            names = "abcd"[:len(shape)]
            return zb[:, at:at + n].rearrange(f"p ({' '.join(names)}) -> p {' '.join(names)}",
                                              **{k: v for k, v in zip(names[1:], shape[1:])})

        def c_(name, rows=P):
            at, n = CONST[name]
            return cst[0:rows, at:at + n]

        def halves_of(k, t):
            return 2 * TT * k + 2 * t + 2

        def s_(name):
            at, n = SMALL[name]
            return sml[:, at:at + n]

        ident = c_("ident")
        z = zview(0, TT, D)
        o_tok = z
        q_tok = zview(0, TT, 1152)
        ctok = zview(0, TT, C_IN)
        cn = zview(TT * C_IN, TT, 480)
        cT = probs[:, 0:2, :].rearrange("p a b -> p (a b)").rearrange("p (c t) -> p c t", c=3)
        oT = xT
        ob = xT[:, 0:4, :].rearrange("p c t -> p (c t)").rearrange("p (a n) -> p a n", a=TT)
        V0 = area(0, TT, 24 * HD)
        KTm = area(3072, H_A, TOK)
        QTd = area(6144, 6, TOK)
        KTd = area(7680, 6, TOK)
        QTm = area(9216, H_A, TOK)
        QTc = area(0, R_C, TOK)
        QTf = area(1024, H_D, TOK)
        KTc = area(2048, 4, TOK)
        KTf = area(3072, H_D, TOK)
        Vs = area(4096, TT, 2 * P)
        Vf = area(4608, TT, 512)
        Xw = area(5632, 2, CMP_LEN, NC_BLK)
        hid = area(6592, 2, 16)
        hid_t = area(6624, 4, 16)
        hid4 = area(6688, 4, 32)
        kcT = area(6816, 16)
        VBD = area(6832, G_C, 4, HD)
        ec = area(7344, TT, H_C, 32)
        ecT = area(7856, TT, G_C, P)
        cs = area(8368, 6, 16)
        xg = area(0, 2, DC, P)
        hT = area(4608, TOK)
        slot_gate = area(9800, 2)
        sil = area(5120, 2, F_EXP)
        Selg = area(6144, 2, TT, P)
        sils = area(6656, 2, TOK)
        hTs = area(7168, 2, TOK)
        r_sc, r_sel, r_m8, r_selm, r_rep, r_mask, r_gate, r_pos = (
            area(7680 + 128 * i, TT, EXPERTS) for i in range(8))
        r_gs, r_rank, r_gm, r_top = (area(8704 + 16 * i, TT, GROUPS) for i in range(4))
        hid_s = area(9288, 2, F_EXP)
        r_gt = area(8768, GROUPS, GROUPS)
        r_eq = area(8832, GROUPS, GROUPS)
        r_ov = area(8896, 4)
        r_ovp = area(8900, 4)
        r_idx = area(8904, 4)
        r_hot = area(8912, 3, EXTRA)
        r_list = area(9008, 2, EXTRA)
        r_den = area(9072, TT)
        r_q = area(9080, 8)
        visit_f = area(9088, 2, VISITS)
        lng = area(10240, 2, D)

        const_in, x_in, small_in, scratch_out, out_done = map(sem, (
            "const_in", "x_in", "small_in", "scratch_out", "out_done"))
        bias_ps, bias_sb = sem("bias_ps"), sem("bias_sb")
        bias_in = sem("bias_in")
        rw_in = sem("rw_in")
        ln_in = sem("ln_in")
        dn_loaded = [[sem(f"ring{k}_down_loaded_{l}") for k in range(RING)] for l in range(DEPTH)]
        loaded = [[sem(f"ring{k}_loaded_{l}") for k in range(RING)] for l in range(DEPTH)]
        proj_done, proj_taken = per_layer("proj_done"), per_layer("proj_taken")
        rms_var, rms_std = sem("rms_var"), sem("rms_std")
        cn_ready, q_roped = sem("cn_ready"), sem("q_roped")
        scores_done, scores_taken = per_layer("scores_done"), per_layer("scores_taken")
        max_ready, probs_ready = per_layer("max_ready"), per_layer("probs_ready")
        pt_done, pt_taken, pv_done = per_layer("pt_done"), per_layer("pt_taken"), per_layer("pv_done")
        o_taken = per_layer("o_taken")
        comb_d, comb_w = sem("comb_d"), sem("comb_w")
        o_ready, oT_done, oT_taken = per_layer("o_ready"), per_layer("oT_done"), per_layer("oT_taken")
        y_done = per_layer("y_done")
        ln_var, ln_std = map(sem, ("ln_var", "ln_std"))
        x_new = sem("x_new")
        xT_done, xT_taken = sem("xT_done"), sem("xT_taken")
        logit_done, esig_ready = per_layer("logit_done"), per_layer("esig_ready")
        mask_ready, pos_done = per_layer("mask_ready"), per_layer("pos_done")
        over_ready, idx_done = per_layer("over_ready"), per_layer("idx_done")
        hot_ready, list_done, visits_ready = per_layer("hot_ready"), per_layer("list_done"), per_layer("visits_ready")
        sh_gu, sh_silu, sh_h = per_layer("sh_gu"), per_layer("sh_silu"), per_layer("sh_h")
        sh_down = per_layer("sh_down")
        sel_ready, gath_done, xgA_ready, xgB_ready = (per_layer(n) for n in (
            "sel_ready", "gath_done", "xgA_ready", "xgB_ready"))
        gu_done, silu_ready, h_ready = per_layer("gu_done"), per_layer("silu_ready"), per_layer("h_ready")
        turn_done, turn_ready = per_layer("turn_done"), per_layer("turn_ready")
        down_done, y_high_ready, y_low_ready = (per_layer(n) for n in ("down_done", "y_high_ready", "y_low_ready"))
        moe_done = per_layer("moe_done")
        gsum_done, gsum_taken = per_layer("gsum_done"), per_layer("gsum_taken")
        win_ready, hid_done, hid_z, hid_e, hid_ready = map(sem, ("win_ready", "hid_done", "hid_z", "hid_e", "hid_ready"))
        kv_done, kv_taken = sem("kv_done"), sem("kv_taken")
        cmp_s, cmp_c, cmp_e, cmp_p = map(sem, ("cmp_s", "cmp_c", "cmp_e", "cmp_p"))
        cmpT_done, cmpT_taken, cmp_o = sem("cmpT_done"), sem("cmpT_taken"), sem("cmp_o")
        high_ready, low_ready = sem("x_high_ready"), sem("x_low_ready")
        lam_s, lam_e = sem("lam_s"), sem("lam_e")
        dn_var, dn_std = sem("dn_var"), sem("dn_std")
        dve_step, act_step = sem("dve_step"), sem("act_step")

        def mm_group(pe, outap, pairs):
            for k, (l, r) in enumerate(pairs):
                last = pe.matmul(outap, l, r, start=(k == 0), stop=(k == len(pairs) - 1))
            return last

        def slot(block, at, chunks, cols):
            return ring[:, block % RING, at:at + chunks * cols].rearrange("p (c n) -> p c n", c=chunks)

        def tokens_out(w, t, lo, n, src=xT, chunks=DC):
            return lambda pe, b: mm_group(pe, b[:, 0:n], [(src[:, c, t * P:(t + 1) * P], w[:, c, lo:lo + n])
                                                          for c in range(chunks)])

        def two_T(w, cols):
            def go(pe, b):
                for k, lhs in enumerate(cols):
                    m = mm_group(pe, b[:, k * TOK:(k + 1) * TOK], [(lhs(w, c), xT[:, c, :]) for c in range(DC)])
                return m
            return go

        def jobs0():
            wA, wq, wk, wv = (slot(k, 0, DC, n) for k, n in ((0, C_IN), (1, 768), (2, 768), (3, 768)))
            wuq = slot(4, 0, 2, 1152)
            wukv = ring[:, 0, 2304:2304 + 1536].rearrange("p (h a d) -> p h a d", h=H_A, a=2)
            jobs = []
            for t in range(TT):
                jobs.append((0, t == 1, [], tokens_out(wA, t, 0, C_IN), [(ctok[:, t, :], (P, 0, C_IN))]))
            for blk, w, dst in ((1, wq, QTd), (2, wk, KTd)):
                for k in range(3):
                    cols = [lambda w, c, i=i: w[:, c, i * P:(i + 1) * P] for i in (2 * k, 2 * k + 1)]
                    jobs.append((blk, k == 2, [], two_T(w, cols),
                                 [(dst[:, 2 * k:2 * k + 2, :].rearrange("p a t -> p (a t)"), (P, 0, 512))]))
            for t in range(TT):
                for lo, n in ((0, 512), (512, 256)):
                    jobs.append((3, t == 1 and lo > 0, [], tokens_out(wv, t, lo, n),
                                 [(V0[:, t, lo:lo + n], (P, 0, n))]))

            def turn_q(pe, b):
                for c in range(2):
                    for t in range(TT):
                        m = pe.transpose(b[:, c * TOK + t * P:c * TOK + (t + 1) * P], cn[:, t, c * P:(c + 1) * P], ident)
                return m

            def turn_kv(pe, b):
                for t in range(TT):
                    pe.transpose(b[:, t * P:(t + 1) * P], cn[:, t, 2 * P:3 * P], ident)
                for t in range(TT):
                    m = pe.transpose(b[0:QK_A, TOK + t * P:TOK + (t + 1) * P], cn[:, t, 384:480], ident)
                return m

            jobs.append((None, False, [(cn_ready, 1)], turn_q,
                         [(cT[:, 0:2, :].rearrange("p a t -> p (a t)"), (P, 0, 512))]))
            jobs.append((None, False, [], turn_kv,
                         [(cT[:, 2, :], (P, 0, TOK)), ("rope key", None)]))
            n_cT = len(jobs)
            for t in range(TT):
                for k, (lo, n) in enumerate(((0, 512), (512, 512), (1024, 128))):
                    jobs.append((4, False, [(proj_taken[0], n_cT)] if t == 0 and k == 0 else [],
                                 tokens_out(wuq, t, lo, n, cT, 2), [(q_tok[:, t, lo:lo + n], (P, 0, n))]))
            n_q = len(jobs)
            for k in range(6):
                def nope(pe, b, k=k):
                    for i in range(2):
                        m = pe.matmul(b[0:NOPE, i * TOK:(i + 1) * TOK], wukv[:, 2 * k + i, 0, :], cT[:, 2, :],
                                      start=True, stop=True)
                    return m
                jobs.append((4, False, [], nope,
                             [(KTm[0:NOPE, 2 * k:2 * k + 2, :].rearrange("p a t -> p (a t)"), (NOPE, 0, 512))]))
            for t in range(TT):
                for h0, n in ((0, 8), (8, 4)):
                    def vals(pe, b, t=t, h0=h0, n=n):
                        return pe.matmul(b[:, 0:n * HD].rearrange("p (h d) -> p h d", h=n),
                                         cT[:, 2, t * P:(t + 1) * P], wukv[:, h0:h0 + n, 1, :], start=True, stop=True)
                    jobs.append((4, t == 1 and h0 > 0, [], vals,
                                 [(V0[:, t, 768 + h0 * HD:768 + (h0 + n) * HD], (P, 0, n * HD))]))
            for k in range(6):
                def turn(pe, b, k=k):
                    for i in range(2):
                        for t in range(TT):
                            m = pe.transpose(b[0:QK_A, i * TOK + t * P:i * TOK + (t + 1) * P],
                                             q_tok[:, t, (2 * k + i) * QK_A:(2 * k + i + 1) * QK_A], ident)
                    return m
                jobs.append((None, False, [(q_roped, TT)] if k == 0 else [], turn,
                             [(QTm[0:QK_A, 2 * k:2 * k + 2, :].rearrange("p a t -> p (a t)"), (QK_A, 0, 512))]))
            return jobs, n_q

        def jobs1():
            wqc, wkv, wqd, wkd = slot(0, 0, DC, 536), slot(1, 0, DC, 768), slot(2, 0, DC, 512), slot(3, 0, DC, 512)
            wvd = slot(4, 0, DC, 512)
            jobs = []
            for k in range(2):
                cols = [lambda w, c, r=r: w[:, c, r * P:(r + 1) * P] for r in (2 * k, 2 * k + 1)]
                jobs.append((0, False, [], two_T(wqc, cols),
                             [(QTc[:, 2 * k:2 * k + 2, :].rearrange("p a t -> p (a t)"), (P, 0, 512))]))

            def gate_cols(pe, b):
                for t in range(TT):
                    m = mm_group(pe, b[:, t * 24:(t + 1) * 24],
                                 [(xT[:, c, t * P:(t + 1) * P], wqc[:, c, 512:536]) for c in range(DC)])
                return m
            jobs.append((0, True, [], gate_cols, [("gates", None)]))
            for k in range(2):
                cols = [lambda w, c, i=i: w[:, c, i * P:(i + 1) * P] for i in (2 * k, 2 * k + 1)]
                jobs.append((1, False, [], two_T(wkv, cols),
                             [(KTc[:, 2 * k:2 * k + 2, :].rearrange("p a t -> p (a t)"), (P, 0, 512))]))

            def vals(pe, b):
                for t in range(TT):
                    m = mm_group(pe, b[:, t * TOK:(t + 1) * TOK],
                                 [(xT[:, c, t * P:(t + 1) * P], wkv[:, c, 512:768]) for c in range(DC)])
                return m
            jobs.append((1, True, [], vals, [(Vs[:, :, :].rearrange("p a t -> p (a t)"), (P, 0, 512))]))
            for blk, w, dst in ((2, wqd, QTf), (3, wkd, KTf)):
                for k in range(2):
                    cols = [lambda w, c, i=i: w[:, c, i * P:(i + 1) * P] for i in (2 * k, 2 * k + 1)]
                    jobs.append((blk, False, [], two_T(w, cols),
                                 [(dst[:, 2 * k:2 * k + 2, :].rearrange("p a t -> p (a t)"), (P, 0, 512))]))
            return jobs, wvd

        JOBS0, N_Q = jobs0()
        JOBS1, w_vd = jobs1()
        JOBS = [JOBS0, JOBS1]
        for t in range(TT):
            JOBS1.append((4, t == 1, [], tokens_out(w_vd, t, 0, 512), [(Vf[:, t, :], (P, 0, 512))]))
        KCMP_JOB = 4
        HID_AFTER = 10

        def freed(l, k):
            if k in (5, 6):
                return y_done[l], k - 2
            if k == 7:
                return sh_down[l], 1
            if l == 1 and k in (2, 3):
                return hid_done, 1
            return proj_done[l], 1 + next(n for n, job in enumerate(JOBS[l]) if job[0] == k and job[1])

        def item(l, n):
            if l == 0:
                if n < 12:
                    r = slice(64 * (n % 2), 64 * (n % 2) + 64)
                    return dict(q=QTd[r, n // 2, :], k=KTd[r, n // 2, :], v=lambda j, n=n: V0[:, j, n * HD:(n + 1) * HD],
                                bias=n, scale=HD ** -0.5, col=(n % 8) * HD, width=HD, stat=n)
                h = n - 12
                return dict(q=QTm[0:QK_A, h, :], k=KTm[0:QK_A, h, :], v=lambda j, n=n: V0[:, j, n * HD:(n + 1) * HD],
                            bias=12, scale=QK_A ** -0.5, col=(n % 8) * HD, width=HD, stat=n)
            if n < 16:
                b, g, r = n // 8, n % 2, (n % 8) // 2
                h = g * R_C + r
                rows = slice(64 * g, 64 * g + 64)
                return dict(q=QTc[rows, r, :], k=KTc[rows, 2 + b, :],
                            v=lambda j, b=b, g=g: Vs[:, j, b * P + g * HD:b * P + (g + 1) * HD],
                            bias=h, scale=HD ** -0.5, col=h * HD, width=HD, stat=8 * b + h)
            hd, m = (n - 16) // 2, n % 2
            rows = slice(64 * m, 64 * m + 64)
            return dict(q=QTf[rows, hd, :], k=KTf[rows, hd, :], v=lambda j, hd=hd: Vf[:, j, hd * P:(hd + 1) * P],
                        bias=8 + hd, scale=HD ** -0.5, col=(hd % 2) * 256 + m * P, width=P, stat=16 + 4 * m + hd)

        ITEMS = [[item(l, n) for n in range(24)] for l in range(DEPTH)]
        GROUP_END = [[8, 16, 24], [8, 16, 20, 24]]

        def group_of(l, n):
            return next(g for g, e in enumerate(GROUP_END[l]) if n < e)

        def o_bank(l, g, t):
            return bank[4 + 2 * (g % 2) + t]

        block = ctx.enter_context(nc.Block())

        @block.sync
        def _(sp):
            def ring_load(l, k, src, n):
                sp.dma_start(ring[:, k % RING, 0:n], src[:, 0:n]).then_inc(loaded[l][k % RING], 16)

            sp.dma_start(xT[:, :, :], xT_in.rearrange("(c p) t -> p c t", p=P)).then_inc(x_in, 16)
            n = None
            for l in range(DEPTH):
                for k in range(MIX_BLOCKS):
                    if k >= RING:
                        sp.wait_ge(*freed(l, k - RING))
                    elif l and k == 0:
                        sp.wait_ge(down_done[0], n * 4)
                    if k < MIX_BLOCKS - 1:
                        ring_load(l, k, mixw[l, k], MIX_SIZE[l][k])
                    else:
                        ring_load(l, k, expw[l, EXPERTS], SLOT_W)
                    if l == 0 and k == RING - 1:
                        sp.dma_start(x_tok[:, :, :], x.rearrange("(t p) d -> p t d", p=P)).then_inc(x_in, 16)
                def step(i, a, known):
                    pair = (2 * a, 2 * a + 1)
                    e = known or [sp.value_load(visit[0:1, 0, bass.ds(i * 4 + j, 1)], min_val=0, max_val=EXPERTS - 1)
                                  for j in pair]
                    for part, arrived, lo, hi in ((0, loaded[l], 0, GU), (1, dn_loaded[l], GU, SLOT_W)):
                        if not known:
                            sp.wait_ge(*((gu_done[l], i * 2 + (a - 1)) if part == 0 else (down_done[l], i * 4 + (2 * a - 2))))
                        for s, j in enumerate(pair):
                            if known and part == 0:
                                sp.wait_ge(*freed(l, MIX_BLOCKS - RING + j))
                            sp.dma_start(ring[:, j, lo:hi],
                                         (expw[l, e[s], :, lo:hi] if known else
                                          expw[l, bass.ds(e[s], 1), :, lo:hi].rearrange("o p n -> (o p) n")))\
                              .then_inc(arrived[j], 16)

                for a in range(2):
                    step(0, a, (2 * a, 2 * a + 1))
                sp.wait_ge(visits_ready[l], 1)
                n = sp.value_load(nquads[0:1, 0:1], min_val=QUADS, max_val=MAX_QUADS)

                with sp.Fori(1, n) as i:
                    for a in range(2):
                        step(i, a, None)
            for t in range(TT):
                sp.wait_ge(x_new, halves_of(2 * DEPTH - 1, t))
                sp.dma_start(out[t * P:(t + 1) * P, :], x_tok[:, t, :]).then_inc(out_done, 16)
            sp.wait_ge(out_done, 16 * TT)

        @block.gpsimd
        def _(pool):
            pool.dma_start(cst[:, :], const).then_inc(const_in, 16)
            pool.dma_start(tmp[0:BUCKETS, 0:BIAS_ROWS], tab).then_inc(const_in, 16)
            pool.dma_start(tmp[0:BUCKETS, 32:32 + SPAN], hot).then_inc(const_in, 16)
            pool.dma_start(tmp[0:BIAS_ROWS, 448:448 + SPAN], mask).then_inc(const_in, 16)
            pool.dma_start(sml[:, :], small.to_broadcast([P, N_SMALL])).then_inc(small_in, 16)
            pool.dma_start(posT[:, :, :], pos).then_inc(small_in, 16)
            pool.dma_start(w2s[:, :, :], w2).then_inc(small_in, 16)
            pool.dma_start(rw[:, :, :], routw[0]).then_inc(rw_in, 16)
            pool.wait_ge(bias_sb, 1)
            pool.dma_start(scratch, tmp[0:BIAS_ROWS, 448:448 + SPAN]).then_inc(scratch_out, 16)
            pool.wait_ge(scratch_out, 16)

            def bias_load(l):
                r0, n = BIAS_OF[l]
                src = bass.AP(scratch.tensor, r0 * SPAN, [(1, P), (SPAN, n), (1, TOK)])
                pool.dma_start(biasZ[:, 0:n, :], src).then_inc(bias_in, 16)

            bias_load(0)
            for l in range(DEPTH):
                for half in range(2):
                    k = 2 * l + half
                    if half == 0:
                        pool.wait_ge(scores_done[l], 24)
                    else:
                        pool.wait_ge(x_new, halves_of(k - 1, TT - 1))
                    pool.dma_start(lng[:, :, :].rearrange("p a d -> p (a d)"),
                                   lnp[k:k + 1, :].to_broadcast([P, 2 * D])).then_inc(ln_in, 16)
                    if half == 1:
                        if l == 0:
                            pool.wait_ge(logit_done[0], 1)
                            pool.dma_start(rw[:, :, :], routw[1]).then_inc(rw_in, 16)
                        pool.wait_ge(high_ready, l + 1)
                        pool.tensor_tensor(x_low[:, :, :], x_tok[:, :, :], x_high[:, :, :].bitcast(F32), ALU.subtract)\
                            .then_inc(low_ready, 1)
                        if l == 0:
                            pool.wait_ge(moe_done[0], 4)
                            bias_load(1)

        @block.tensor
        def _(pe):
            def bias_rows():
                pe.wait_ge(const_in, 64)
                pe.matmul(bank[7][0:BIAS_ROWS, 0:SPAN], tmp[0:BUCKETS, 0:BIAS_ROWS], tmp[0:BUCKETS, 32:32 + SPAN],
                          start=True, stop=True).then_inc(bias_ps, 1)

            def ring_in(l, k):
                pe.wait_ge(loaded[l][k % RING], 16 * (k // RING + 1))

            def projections(l, lo, hi):
                for n in range(lo, hi):
                    blk, _, waits, go, _ = JOBS[l][n]
                    if blk is not None:
                        ring_in(l, blk)
                    for s, v in waits:
                        pe.wait_ge(s, v)
                    if n >= 4:
                        pe.wait_ge(proj_taken[l], n - 3)
                    m = go(pe, bank[n % 4])
                    m.then_inc(proj_done[l], 1)

            def scores(l, n):
                it = ITEMS[l][n]
                b = bank[n % 3]
                if n >= 3:
                    pe.wait_ge(scores_taken[l], n - 2)
                for qt, kt, at in ((0, 0, 0), (1, 0, P)):
                    m = pe.matmul(b[:, at:at + P * (qt + 1)], it["q"][:, qt * P:(qt + 1) * P],
                                  it["k"][:, 0:P * (qt + 1)], start=True, stop=True)
                m.then_inc(scores_done[l], 1)

            def turn_probs(l, n):
                pe.wait_ge(probs_ready[l], n + 1)
                if n >= 1:
                    pe.wait_ge(pt_taken[l], n)
                for j in range(3):
                    m = pe.transpose(bank[3][:, j * P:(j + 1) * P], probs[:, n % 3, j * P:(j + 1) * P], ident)
                m.then_inc(pt_done[l], 1)

            def values(l, n):
                it, g = ITEMS[l][n], group_of(l, n)
                pe.wait_ge(pt_taken[l], n + 1)
                if g >= 2:
                    pe.wait_ge(o_taken[l], g - 1)
                cols = slice(it["col"], it["col"] + it["width"])
                pe.matmul(o_bank(l, g, 0)[:, cols], probsT[:, n % 2, 0:P], it["v"](0), start=True, stop=True)
                pe.matmul(o_bank(l, g, 1)[:, cols], probsT[:, n % 2, P:2 * P], it["v"](0), start=True, stop=False)
                pe.matmul(o_bank(l, g, 1)[:, cols], probsT[:, n % 2, 2 * P:3 * P], it["v"](1), start=False, stop=True)\
                  .then_inc(pv_done[l], 1)

            def attention(l):
                pe.wait_ge(proj_taken[l], len(JOBS[l]))
                scores(l, 0)
                scores(l, 1)
                for n in range(25):
                    if n < 22:
                        scores(l, n + 2)
                    if n < 24:
                        turn_probs(l, n)
                    if n >= 1:
                        values(l, n - 1)

            def output_projection(l):
                pe.wait_ge(o_ready[l], 1)
                for k in range(4):
                    for c in (2 * k, 2 * k + 1):
                        for t in range(TT):
                            m = pe.transpose(bank[k][:, (c % 2) * TOK + t * P:(c % 2) * TOK + (t + 1) * P],
                                             o_tok[:, t, c * P:(c + 1) * P], ident)
                    m.then_inc(oT_done[l], 1)
                pe.wait_ge(oT_taken[l], 4)
                ring_in(l, 5)
                ring_in(l, 6)
                for t in range(TT):
                    for hh in range(2):
                        if (t, hh) == (TT - 1, 1):
                            turn_x(2 * l, 0)
                        w = slot(5 + hh, 0, DC, 512)
                        m = mm_group(pe, Ybank[t][hh][:, :], [(oT[:, c, t * P:(t + 1) * P], w[:, c, :]) for c in range(DC)])
                        m.then_inc(y_done[l], 1)

            def turn_x(k, t):
                for q in range(2):
                    pe.wait_ge(x_new, halves_of(k, t) - 1 + q)
                    for cc in range(4):
                        c = 4 * q + cc
                        m = pe.transpose(bank[4 + 2 * t + q][:, cc * P:(cc + 1) * P],
                                         x_tok[:, t, c * P:(c + 1) * P], ident)
                    m.then_inc(xT_done, 1)

            def compress():
                pe.wait_ge(win_ready, 1)
                ring_in(1, 2)
                ring_in(1, 3)
                for kv in range(2):
                    w1 = ring[:, 2 + kv, 4096:6144].rearrange("p (j h) -> p j h", j=CMP_LEN)
                    for g in range(G_C):
                        r = slice(64 * g, 64 * g + 64)
                        for j in range(CMP_LEN):
                            m = pe.matmul(bank[6 + g][r, kv * 16:kv * 16 + NC_BLK], w1[r, j, :], Xw[r, kv, j, :],
                                          start=(j == 0), stop=(j == CMP_LEN - 1))
                m.then_inc(hid_done, 1)
                pe.wait_ge(hid_ready, 1)
                pe.wait_ge(small_in, 48)
                for g in range(G_C):
                    r = slice(64 * g, 64 * g + 64)
                    pe.matmul(bank[6 + g][r, 64:64 + NC_BLK], w2s[r, 0, :], hid[r, 0, 0:NC_BLK], start=True, stop=True)
                    m = pe.matmul(bank[6 + g][:, 128:192], hid4[r, :, :].rearrange("p a c -> p (a c)"), w2s[r, 1, :],
                                  start=True, stop=True)
                m.then_inc(kv_done, 1)

            def compressed_attention():
                pe.wait_ge(kv_taken, 1)
                pe.wait_ge(proj_taken[1], len(JOBS1))
                for g in range(G_C):
                    for t in range(TT):
                        for r in range(R_C):
                            rows = slice(64 * g, 64 * g + 64)
                            at = (t * R_C + r) * 16
                            m = pe.matmul(bank[g][:, at:at + NC_BLK], QTc[rows, r, t * P:(t + 1) * P],
                                          kcT[rows, 0:NC_BLK], start=True, stop=True)
                m.then_inc(cmp_s, 1)
                pe.wait_ge(cmp_p, 1)
                for t in range(TT):
                    for g in range(G_C):
                        m = pe.transpose(bank[2][:, (t * G_C + g) * P:(t * G_C + g + 1) * P],
                                         ec[:, t, 4 * g:4 * g + 4, :].rearrange("p h c -> p (h c)"), ident)
                m.then_inc(cmpT_done, 1)
                pe.wait_ge(cmpT_taken, 1)
                for t in range(TT):
                    for g in range(G_C):
                        m = pe.matmul(bank[6 + t][:, g * 256:(g + 1) * 256], ecT[:, t, g, :],
                                      VBD[:, g, :, :].rearrange("p h d -> p (h d)"), start=True, stop=True)
                m.then_inc(cmp_o, 1)

            def router(l):
                pe.wait_ge(rw_in, 16 * (l + 1))
                for t in range(TT):
                    m = mm_group(pe, bC[:, t * EXPERTS:(t + 1) * EXPERTS],
                                 [(xT[:, c, t * P:(t + 1) * P], rw[:, c, :]) for c in range(DC)])
                m.then_inc(logit_done[l], 1)

            def gate_up_shared(l, lo, hi):
                ring_in(l, 7)
                w = slot(3, 0, DC, 2 * F_EXP)
                for part in range(lo, hi):
                    b, f = (bA, bH)[part // 2], part % 2
                    m = mm_group(pe, b[:, f * TOK:(f + 1) * TOK],
                                 [(w[:, c, part * P:(part + 1) * P], xT[:, c, :]) for c in range(DC)])
                    if f:
                        m.then_inc(sh_gu[l], 1)

            def places(l):
                pe.wait_ge(mask_ready[l], 1)
                tri, ones = c_("tri"), c_("ones")
                mm_group(pe, bC[:, 0:EXPERTS], [(tri, r_mask[:, 0, :])])
                mm_group(pe, bC[:, EXPERTS:2 * EXPERTS], [(ones, r_mask[:, 0, :]), (tri, r_mask[:, 1, :])])
                mm_group(pe, bC[0:EXPERTS, 128:129], [(r_mask[:, t, :], ones[:, 0:1]) for t in range(TT)])\
                    .then_inc(pos_done[l], 1)

            def down_shared(l):
                pe.wait_ge(sh_h[l], 1)
                w = ring[:, 3, GU:SLOT_W].rearrange("p (f n) -> p f n", f=2)
                for t in range(TT):
                    for hh in range(2):
                        for f in range(2):
                            m = pe.matmul(Ybank[t][hh][:, :], hTs[:, f, t * P:(t + 1) * P],
                                          w[:, f, hh * 512:(hh + 1) * 512], start=(f == 0), stop=False,
                                          skip_group_check=True)
                m.then_inc(sh_down[l], 1)

            def keep_clock(n, b):
                for _ in range(n):
                    pe.matmul(b[:, :], ident, cst[:, 0:512], start=True, stop=True)

            def visit_places(l):
                pe.wait_ge(over_ready[l], 1)
                mm_group(pe, bC[0:64, 0:4], [(c_("tri", 64)[:, 0:64], r_ov[0:64, :]), (c_("ones", 64)[:, 0:64], r_ovp[0:64, :])])\
                    .then_inc(idx_done[l], 1)

            def visit_list(l):
                pe.wait_ge(hot_ready[l], 1)
                mm_group(pe, bC[0:1, 0:EXTRA], [(c_("ecode", 64), r_hot[0:64, p, :]) for p in range(3)])
                mm_group(pe, bC[0:1, EXTRA:2 * EXTRA], [(c_("pcode", 64)[:, p:p + 1], r_hot[0:64, p, :]) for p in range(3)])\
                    .then_inc(list_done[l], 1)

            def gather(l, a, pair):
                pe.wait_ge(sel_ready[l], pair + 1)
                for half, b in ((0, bA), (1, bB)):
                    for cc in range(4):
                        c = 4 * half + cc
                        m = mm_group(pe, b[:, cc * P:(cc + 1) * P],
                                     [(part[:, t, c * P:(c + 1) * P], Sel[:, a, t, :])
                                      for part in (x_high, x_low) for t in range(TT)])
                    m.then_inc(gath_done[l], 1)

            def scatter(l, a, done=None):
                for t in range(TT):
                    for hh in range(2):
                        for part in (y_high, y_low):
                            m = pe.matmul(Ybank[t][hh][:, :], selT[:, a, t * P:(t + 1) * P],
                                          part[:, hh * 512:(hh + 1) * 512], start=False, stop=False,
                                          skip_group_check=True)
                        if done is not None:
                            m.then_inc(done, 1)
                return m

            def experts(l):
                pe.nop().then_inc(turn_done[l], 1)
                pe.wait_ge(visits_ready[l], 1)
                n = pe.value_load(nquads[0:1, 0:1], min_val=QUADS, max_val=MAX_QUADS)
                with pe.Fori(0, n) as i:
                    for a in range(2):
                        pe.wait_ge(turn_ready[l], i * 2 + (a + 1))
                        m = mm_group(pe, bC[:, 0:1], [(Selg[:, a, t, :], c_("ones")[:, 0:1]) for t in range(TT)])
                        m.then_inc(gsum_done[l], 1)
                        pe.wait_ge(xgA_ready[l], i * 2 + (a + 1))
                        pe.wait_ge(xgB_ready[l], i * 2 + (a + 1))
                        pe.wait_ge(h_ready[l], i * 2 + (a + 1))
                        for s in range(2):
                            pe.wait_ge(loaded[l][2 * a + s], i * 16 + 48)
                        for c in range(DC):
                            for s in range(2):
                                m = pe.matmul(bH[s * SLOTS:(s + 1) * SLOTS, :], xg[:, a, c, s * SLOTS:(s + 1) * SLOTS],
                                              ring[:, 2 * a + s, c * 512:(c + 1) * 512], start=(c == 0), stop=(c == DC - 1))
                        m.then_inc(gu_done[l], 1)
                        pe.wait_ge(y_low_ready[l], i * 4 + (2 * a + 2))
                        gather(l, 1 - a, i * 2 + (a + 1))
                        pe.wait_ge(gsum_taken[l], i * 2 + (a + 1))
                        for t in range(TT):
                            pe.transpose(bC[:, t * P:(t + 1) * P], Sel[:, a, t, :].bitcast(F32), ident)
                        pe.wait_ge(h_ready[l], i * 2 + (a + 2))
                        for f in range(2):
                            m = pe.transpose(bC[:, (2 + f) * P:(3 + f) * P], hid_s[:, a, f * P:(f + 1) * P], ident)
                        m.then_inc(turn_done[l], 1)
                        scatter(l, 1 - a)
                        pe.wait_ge(turn_ready[l], i * 2 + (a + 2))
                        pe.wait_ge(xgA_ready[l], i * 2 + (a + 2))
                        pe.wait_ge(xgB_ready[l], i * 2 + (a + 2))
                        for s in range(2):
                            pe.wait_ge(dn_loaded[l][2 * a + s], i * 16 + 16)
                        for hh, b in ((0, bA), (1, bB)):
                            for f in range(2):
                                for s in range(2):
                                    at = f * P + s * SLOTS
                                    m = pe.matmul(b[s * SLOTS:(s + 1) * SLOTS, :], hT[:, at:at + SLOTS],
                                                  ring[:, 2 * a + s, GU + f * D + hh * 512:GU + f * D + (hh + 1) * 512],
                                                  start=(f == 0), stop=(f == 1))
                            m.then_inc(down_done[l], 1)
                pe.wait_ge(y_low_ready[l], n * 4 + 2)
                pe.wait_ge(turn_ready[l], n * 2 + 1)
                scatter(l, 1, moe_done[l])

            pe.wait_ge(x_in, 16)
            for l in range(DEPTH):
                if l == 0:
                    projections(0, 0, 5)
                    bias_rows()
                    projections(0, 5, len(JOBS0))
                else:
                    projections(1, 0, HID_AFTER)
                    compress()
                    projections(1, HID_AFTER, len(JOBS1))
                    compressed_attention()
                attention(l)
                keep_clock(4 + 4 * l, bank[0])
                output_projection(l)
                keep_clock(3, bank[6])
                turn_x(2 * l, 1)
                pe.wait_ge(xT_taken, 4 * (2 * l + 1))
                router(l)
                gate_up_shared(l, 0, 3)
                places(l)
                gate_up_shared(l, 3, 4)
                visit_places(l)
                pe.wait_ge(low_ready, l + 1)
                pe.wait_ge(sh_silu[l], 1)
                gather(l, 0, 0)
                visit_list(l)
                down_shared(l)
                experts(l)
                if l + 1 < DEPTH:
                    for t in range(TT):
                        keep_clock(4, bH)
                        turn_x(2 * l + 1, t)
                    pe.wait_ge(xT_taken, 4 * (2 * l + 2))

        @block.scalar
        def _(act):
            steps = [0]

            def link(ins):
                steps[0] += 1
                ins.then_inc(act_step, 1)
                act.wait_ge(act_step, steps[0])

            def projections(l, lo, hi):
                for n in range(lo, hi):
                    b = bank[n % 4]
                    act.wait_ge(proj_done[l], n + 1)
                    for dst, src in JOBS[l][n][4]:
                        if isinstance(dst, str) and dst == "rope key":
                            m = act.copy(KTm[NOPE:QK_A, :, :],
                                         b[NOPE:QK_A, TOK:2 * TOK].unsqueeze(1).to_broadcast([ROPE, H_A, TOK]))
                        elif isinstance(dst, str):
                            m = act.activation(gates3[:, :, :].rearrange("p t k -> p (t k)"), b[:, 0:48], ACT.Exp, scale=-1.0)
                        else:
                            rows, c0, n_ = src
                            m = act.copy(dst, b[0:rows, c0:c0 + n_])
                    m.then_inc(proj_taken[l], 1)
                    if l == 0 and n == 2:
                        act.wait_ge(rms_var, 1)
                        act.activation(st[:, 0:4], st[:, 0:4], ACT.Sqrt).then_inc(rms_std, 1)

            def attention(l):
                for n in range(25):
                    if n < 24:
                        it = ITEMS[l][n]
                        act.wait_ge(max_ready[l], n + 1)
                        for t, c0, w in ((0, 0, P), (1, P, 2 * P)):
                            m = act.activation(probs[:, n % 3, c0:c0 + w], probs[:, n % 3, c0:c0 + w], ACT.Exp,
                                               bias=negmax[:, t, it["stat"]:it["stat"] + 1],
                                               accum_out=rowsum[:, t, it["stat"]:it["stat"] + 1])
                        m.then_inc(probs_ready[l], 1)
                    if n >= 1:
                        act.wait_ge(pt_done[l], n)
                        if n >= 3:
                            act.wait_ge(pv_done[l], n - 2)
                        act.copy(probsT[:, (n - 1) % 2, :], bank[3][:, 0:3 * P]).then_inc(pt_taken[l], 1)
                    if l == 0 and n == 17:
                        act.wait_ge(comb_d, 1)
                        act.activation(wg[:, :, 0:12], wg[:, :, 0:12], ACT.Exp).then_inc(comb_w, 1)

            def output_projection(l):
                for k in range(4):
                    act.wait_ge(oT_done[l], k + 1)
                    act.copy(oT[:, 2 * k:2 * k + 2, :].rearrange("p a t -> p (a t)"), bank[k][:, :]).then_inc(oT_taken[l], 1)

            def norm(k):
                for t in range(TT):
                    act.wait_ge(ln_var, TT * k + t + 1)
                    act.activation(st[:, 16 + t:17 + t], st[:, 16 + t:17 + t], ACT.Sqrt).then_inc(ln_std, 1)
                    if k == 2 * DEPTH - 1:
                        continue
                    for q in range(2):
                        act.wait_ge(xT_done, 4 * k + 2 * t + q + 1)
                        act.copy(xT[:, 4 * q:4 * q + 4, t * P:(t + 1) * P],
                                 bank[4 + 2 * t + q][:, :].rearrange("p (c s) -> p c s", c=4)).then_inc(xT_taken, 1)

            def experts(l):
                act.wait_ge(gath_done[l], 1)
                act.copy(xg[:, 0, 0:4, :].rearrange("p c s -> p (c s)"), bA[:, :]).then_inc(xgA_ready[l], 1)
                act.wait_ge(visits_ready[l], 1)
                n = act.value_load(nquads[0:1, 0:1], min_val=QUADS, max_val=MAX_QUADS)
                with act.Fori(0, n) as i:
                    for a in range(2):
                        act.wait_ge(gu_done[l], i * 2 + (a + 1))
                        act.activation(sil[:, a, :], bH[:, 0:F_EXP], ACT.Silu).then_inc(silu_ready[l], 1)
                        act.wait_ge(gath_done[l], i * 4 + (2 * a + 3))
                        act.copy(xg[:, 1 - a, 0:4, :].rearrange("p c s -> p (c s)"), bA[:, :]).then_inc(xgA_ready[l], 1)
                        act.wait_ge(turn_done[l], i * 2 + (a + 2))
                        act.copy(selT[:, a, :], bC[:, 0:TOK])
                        act.copy(hT[:, :], bC[:, TOK:2 * TOK]).then_inc(turn_ready[l], 1)
                        for hh, b in ((0, bA), (1, bB)):
                            act.wait_ge(down_done[l], i * 4 + (2 * a + hh + 1))
                            act.copy(y_high[:, hh * 512:(hh + 1) * 512], b[:, :]).then_inc(y_high_ready[l], 1)

            for l in range(DEPTH):
                if l == 0:
                    projections(0, 0, len(JOBS0))
                else:
                    act.wait_ge(lam_s, 1)
                    act.activation(lam[:, 0:2], lam[:, 0:2], ACT.Exp).then_inc(lam_e, 1)
                    projections(1, 0, HID_AFTER)
                    act.wait_ge(hid_z, 1)
                    act.activation(hid_t[:, 2:4, :], hid_t[:, 2:4, :], ACT.Exp, scale=-1.0).then_inc(hid_e, 1)
                    projections(1, HID_AFTER, len(JOBS1))
                    act.wait_ge(cmp_c, 1)
                    act.activation(ec[:, :, :, 0:NC_BLK], ec[:, :, :, 0:NC_BLK], ACT.Exp).then_inc(cmp_e, 1)
                    act.wait_ge(cmpT_done, 1)
                    act.copy(ecT[:, :, :, :].rearrange("p t g q -> p (t g q)"), bank[2][:, :]).then_inc(cmpT_taken, 1)
                attention(l)
                if l == 1:
                    act.wait_ge(dn_var, 1)
                    act.activation(st[:, 32:40], st[:, 32:40], ACT.Sqrt).then_inc(dn_std, 1)
                output_projection(l)
                norm(2 * l)
                act.wait_ge(logit_done[l], 1)
                act.activation(r_sc[:, :, :].rearrange("p t e -> p (t e)"), bC[:, 0:2 * EXPERTS], ACT.Exp, scale=-1.0)\
                   .then_inc(esig_ready[l], 1)
                act.copy(x_high[:, :, :], x_tok[:, :, :]).then_inc(high_ready, 1)
                act.wait_ge(sh_gu[l], 1)
                act.activation(sils[:, :, :].rearrange("p f t -> p (f t)"), bA[:, :], ACT.Silu).then_inc(sh_silu[l], 1)
                experts(l)
                norm(2 * l + 1)

        @block.vector
        def _(dve):
            steps = [0]

            def link(ins):
                steps[0] += 1
                ins.then_inc(dve_step, 1)
                dve.wait_ge(dve_step, steps[0])

            TTen, TS, STT = dve.tensor_tensor, dve.tensor_scalar, dve.scalar_tensor_tensor

            def bias_rows():
                dve.wait_ge(bias_ps, 1)
                m = tmp[0:BIAS_ROWS, 448:448 + SPAN]
                TTen(m, bank[7][0:BIAS_ROWS, 0:SPAN], m, ALU.add).then_inc(bias_sb, 1)

            def latent_norms():
                dve.wait_ge(small_in, 48)
                link(dve.memset(cn[:, :, 384:448], 0.0))
                dve.wait_ge(proj_taken[0], 2)
                for t in range(TT):
                    for k, (c0, n) in enumerate(((0, Q_LORA), (Q_LORA, KV_LORA))):
                        link(dve.tensor_tensor_reduce(tmp[:, 0:n], ctok[:, t, c0:c0 + n], ctok[:, t, c0:c0 + n],
                                                      1.0 / n, RMS_EPS, ALU.mult, ALU.add, st[:, 2 * t + k:2 * t + k + 1]))
                dve.nop().then_inc(rms_var, 1)
                dve.wait_ge(rms_std, 1)
                link(dve.reciprocal(st[:, 4:8], st[:, 0:4]))
                for t in range(TT):
                    for k, (c0, n, g) in enumerate(((0, Q_LORA, "qn"), (Q_LORA, KV_LORA, "kvn"))):
                        STT(cn[:, t, c0:c0 + n], ctok[:, t, c0:c0 + n], st[:, 4 + 2 * t + k:5 + 2 * t + k],
                            s_(g), ALU.mult, ALU.mult)
                    cos, sin = (c_(k).rearrange("p (t f) -> p t f", t=TT)[:, t, :] for k in ("cos", "sin"))
                    k1, k2 = ctok[:, t, 384:400], ctok[:, t, 400:416]
                    u = tmp[:, 256 + 64 * t:320 + 64 * t].rearrange("p (a f) -> p a f", a=4)
                    TTen(u[:, 0, :], k1, cos, ALU.mult)
                    TTen(u[:, 1, :], k2, sin, ALU.mult)
                    TTen(u[:, 2, :], k1, sin, ALU.mult)
                    link(TTen(u[:, 3, :], k2, cos, ALU.mult))
                    TTen(cn[:, t, 448:464], u[:, 0, :], u[:, 1, :], ALU.subtract)
                    m = TTen(cn[:, t, 464:480], u[:, 2, :], u[:, 3, :], ALU.add)
                m.then_inc(cn_ready, 1)

            def rotate_queries():
                dve.wait_ge(scratch_out, 16)
                u = tmp[:, 0:768].rearrange("p (a h f) -> p a h f", a=4, h=H_A)
                for t in range(TT):
                    dve.wait_ge(proj_taken[0], N_Q - 3 * (1 - t))
                    cos, sin = (c_(k).rearrange("p (t f) -> p t f", t=TT)[:, t:t + 1, :].to_broadcast([P, H_A, HALF])
                                for k in ("cos", "sin"))
                    q = q_tok[:, t, :].rearrange("p (h e) -> p h e", h=H_A)
                    q1, q2 = q[:, :, NOPE:NOPE + HALF], q[:, :, NOPE + HALF:QK_A]
                    TTen(u[:, 0], q1, cos, ALU.mult)
                    TTen(u[:, 1], q2, sin, ALU.mult)
                    TTen(u[:, 2], q1, sin, ALU.mult)
                    link(TTen(u[:, 3], q2, cos, ALU.mult))
                    link(TTen(q1, u[:, 0], u[:, 1], ALU.subtract))
                    link(TTen(q2, u[:, 2], u[:, 3], ALU.add))
                    dve.nop().then_inc(q_roped, 1)

            def attention(l, first=0):
                dve.wait_ge(bias_in, 16 * (l + 1))
                for n in range(26):
                    if n < 24:
                        it, b = ITEMS[l][n], bank[n % 3]
                        dve.wait_ge(scores_done[l], n + 1)
                        if n >= 3:
                            dve.wait_ge(pt_done[l], n - 2)
                        STT(probs[:, n % 3, 0:P], b[:, 0:P], it["scale"], biasZ[:, it["bias"], 0:P][:, ::-1],
                            ALU.mult, ALU.add)
                        m = STT(probs[:, n % 3, P:3 * P], b[:, P:3 * P], it["scale"], biasZ[:, it["bias"], :][:, ::-1],
                                ALU.mult, ALU.add)
                        m.then_inc(scores_taken[l], 1)
                        dve.wait_ge(scores_taken[l], n + 1)
                        s = it["stat"]
                        dve.tensor_reduce(negmax[:, 0, s:s + 1], probs[:, n % 3, 0:P], X, ALU.max, negate=True)
                        dve.tensor_reduce(negmax[:, 1, s:s + 1], probs[:, n % 3, P:3 * P], X, ALU.max, negate=True)\
                           .then_inc(max_ready[l], 1)
                    for g, end in enumerate(GROUP_END[l]):
                        if n == end + 1:
                            dve.wait_ge(pv_done[l], end)
                            (take0 if l == 0 else take1)(g)

            def inverse_sums(a, b):
                link(dve.reciprocal(rinv[:, :, a:b], rowsum[:, :, a:b]))

            def heads(ap, n):
                return ap.rearrange("p (h d) -> p h d", h=n)

            def spread(ap, n, w=HD):
                return ap.unsqueeze(2).to_broadcast([P, n, w])

            def take0(g):
                if g == 0:
                    for t in range(TT):
                        m = dve.tensor_copy(ob[:, t, :], o_bank(0, 0, t)[:, :])
                    m.then_inc(o_taken[0], 1)
                elif g == 1:
                    nm = negmax
                    link(TTen(wg[:, :, 12:16], nm[:, :, 0:4], nm[:, :, 4:8], ALU.min))
                    link(TTen(wg[:, :, 12:16], wg[:, :, 12:16], nm[:, :, 8:12], ALU.min))
                    for k in range(3):
                        m = TTen(wg[:, :, 4 * k:4 * k + 4], wg[:, :, 12:16], nm[:, :, 4 * k:4 * k + 4], ALU.subtract)
                    m.then_inc(comb_d, 1)
                    inverse_sums(12, 16)
                    for t in range(TT):
                        b = o_bank(0, 1, t)
                        TTen(heads(o_tok[:, t, 0:256], 4), heads(b[:, 256:512], 4), spread(rinv[:, t, 12:16], 4), ALU.mult)
                    dve.wait_ge(comb_w, 1)
                    link(TTen(tmp[:, 0:24].rearrange("p (t k) -> p t k", t=TT), wg[:, :, 0:12], rowsum[:, :, 0:12], ALU.mult))
                    u = tmp[:, 0:24].rearrange("p (t k) -> p t k", t=TT)
                    link(TTen(wg[:, :, 12:16], u[:, :, 0:4], u[:, :, 4:8], ALU.add))
                    link(TTen(wg[:, :, 12:16], wg[:, :, 12:16], u[:, :, 8:12], ALU.add))
                    link(dve.reciprocal(wg[:, :, 16:20], wg[:, :, 12:16]))
                    for k in range(3):
                        m = TTen(rinv[:, :, 4 * k:4 * k + 4], wg[:, :, 4 * k:4 * k + 4], wg[:, :, 16:20], ALU.mult)
                    link(m)
                    for t in range(TT):
                        o = heads(o_tok[:, t, 768:1024], 4)
                        link(TTen(o, heads(o_bank(0, 1, t)[:, 0:256], 4), spread(rinv[:, t, 8:12], 4), ALU.mult))
                        link(TTen(heads(ob[:, t, :], 8), heads(ob[:, t, :], 8), spread(rinv[:, t, 0:8], 8), ALU.mult))
                        link(TTen(o, o, heads(ob[:, t, 0:256], 4), ALU.add))
                        link(TTen(o, o, heads(ob[:, t, 256:512], 4), ALU.add))
                    dve.nop().then_inc(o_taken[0], 1)
                else:
                    inverse_sums(16, 24)
                    for t in range(TT):
                        m = TTen(heads(o_tok[:, t, 256:768], 8), heads(o_bank(0, 2, t)[:, :], 8),
                                 spread(rinv[:, t, 16:24], 8), ALU.mult)
                    m.then_inc(o_ready[0], 1)

            def take1(g):
                if g < 2:
                    inverse_sums(8 * g, 8 * g + 8)
                    a, b = 8 * g, 8 * g + 8
                    link(TTen(rinv[:, :, a:b], rinv[:, :, a:b], gates3[:, :, a + 8:b + 8], ALU.mult))
                    for t in range(TT):
                        link(TTen(heads(tmp[:, 0:512], 8), heads(o_bank(1, g, t)[:, :], 8), spread(rinv[:, t, a:b], 8), ALU.mult))
                        link(TTen(o_tok[:, t, 0:512], o_tok[:, t, 0:512], tmp[:, 0:512], ALU.add))
                    dve.nop().then_inc(o_taken[1], 1)
                    return
                k = 2 * (g - 2)
                inverse_sums(16 + k, 18 + k)
                inverse_sums(20 + k, 22 + k)
                link(TS(rinv[:, :, 20 + k:22 + k], rinv[:, :, 20 + k:22 + k], lam[:, 2:3], None, ALU.mult))
                for t in range(TT):
                    b = o_bank(1, g, t)[:, :].rearrange("p (h m d) -> p h m d", h=2, m=2)
                    o = heads(o_tok[:, t, 512 + k * P:512 + (k + 2) * P], 2)
                    u = heads(tmp[:, 0:256], 2)
                    TTen(o, b[:, :, 0, :], spread(rinv[:, t, 16 + k:18 + k], 2, P), ALU.mult)
                    link(TTen(u, b[:, :, 1, :], spread(rinv[:, t, 20 + k:22 + k], 2, P), ALU.mult))
                    link(TTen(o, o, u, ALU.add))
                dve.nop().then_inc(o_taken[1], 1)
                if g == 3:
                    for t in range(TT):
                        od = o_tok[:, t, 512:1024]
                        link(TTen(tmp[:, 0:512], od, od, ALU.mult))
                        link(dve.tensor_reduce(st[:, 32 + 4 * t:36 + 4 * t], heads(tmp[:, 0:512], 4), X, ALU.add))
                    link(TS(st[:, 32:40], st[:, 32:40], 1.0 / P, RMS_EPS, ALU.mult, ALU.add))
                    dve.nop().then_inc(dn_var, 1)
                    dve.wait_ge(dn_std, 1)
                    link(dve.reciprocal(st[:, 40:48], st[:, 32:40]))
                    link(TS(st[:, 40:48], st[:, 40:48], 1.0 - LAM_INIT, None, ALU.mult))
                    for t in range(TT):
                        od = heads(o_tok[:, t, 512:1024], 4)
                        link(TTen(od, od, spread(st[:, 40 + 4 * t:44 + 4 * t], 4, P), ALU.mult))
                        link(TTen(od, od, s_("dn").unsqueeze(1).to_broadcast([P, 4, P]), ALU.mult))
                    dve.nop().then_inc(o_ready[1], 1)

            def norm(k, y_sem):
                dve.wait_ge(x_in, 32)
                for t in range(TT):
                    mean, std = st[:, 20 + 2 * t:21 + 2 * t], st[:, 16 + t:17 + t]
                    for hh in range(2):
                        dve.wait_ge(y_sem, 2 * t + hh + 1)
                        cols = slice(hh * 512, (hh + 1) * 512)
                        link(STT(z[:, t, cols], x_tok[:, t, cols], ALPHA, Ybank[t][hh][:, :], ALU.mult, ALU.add))
                        link(dve.bn_stats(st[:, 48 + 6 * hh:54 + 6 * hh], z[:, t, cols]))
                    link(dve.bn_aggr(st[:, 20 + 2 * t:22 + 2 * t], st[:, 48:60]))
                    TS(std, st[:, 21 + 2 * t:22 + 2 * t], LN_EPS, None, ALU.add).then_inc(ln_var, 1)
                    dve.wait_ge(ln_in, 16 * (k + 1))
                    STT(z[:, t, :], z[:, t, :], mean, lng[:, 0, :], ALU.subtract, ALU.mult)
                    dve.wait_ge(ln_std, TT * k + t + 1)
                    link(dve.reciprocal(st[:, 18 + t:19 + t], std))
                    for hh in range(2):
                        cols = slice(hh * 512, (hh + 1) * 512)
                        STT(x_tok[:, t, cols], z[:, t, cols], st[:, 18 + t:19 + t], lng[:, 1, cols], ALU.mult, ALU.add)\
                            .then_inc(x_new, 1)

            def router(l):
                dve.memset(y_high[:, :].bitcast(F32), 0.0)
                dve.memset(y_low[:, :].bitcast(F32), 0.0).then_inc(y_low_ready[l], 2)
                dve.memset(selT[:, 1, :].bitcast(F32), 0.0).then_inc(turn_ready[l], 1)
                dve.nop().then_inc(h_ready[l], 1)
                dve.wait_ge(esig_ready[l], 1)
                link(TS(r_sc, r_sc, 1.0, None, ALU.add))
                link(dve.reciprocal(r_sc, r_sc))
                rb = s_("rb").rearrange("p (l e) -> p l e", l=DEPTH)[:, l:l + 1, :].to_broadcast([P, TT, EXPERTS])
                link(TTen(r_sel, r_sc, rb, ALU.add))
                for t in range(TT):
                    for g in range(GROUPS):
                        m = dve.max(r_m8[:, t, 8 * g:8 * g + 8], r_sel[:, t, 8 * g:8 * g + 8])
                link(m)
                best = r_m8.rearrange("p t (g k) -> p t g k", g=GROUPS)
                link(TTen(r_gs, best[:, :, :, 0], best[:, :, :, 1], ALU.add))
                for t in range(TT):
                    other = r_gs[:, t:t + 1, :].to_broadcast([P, GROUPS, GROUPS])
                    own = r_gs[:, t, :].unsqueeze(2).to_broadcast([P, GROUPS, GROUPS])
                    TTen(r_gt, other, own, ALU.is_gt)
                    link(TTen(r_eq, other, own, ALU.is_equal))
                    link(TTen(r_eq, r_eq, c_("gtri").rearrange("p (a b) -> p a b", a=GROUPS), ALU.mult))
                    link(TTen(r_gt, r_gt, r_eq, ALU.add))
                    link(dve.tensor_reduce(r_rank[:, t, :], r_gt, X, ALU.add))
                link(TS(r_gm, r_rank, TOP_GROUPS - 0.5, None, ALU.is_lt))
                link(TS(r_rank, r_gm, 1.0, -NEG, ALU.subtract, ALU.mult))
                for t in range(TT):
                    sel, selm = (heads(r[:, t, :], GROUPS) for r in (r_sel, r_selm))
                    link(TTen(selm, sel, spread(r_gm[:, t, :], GROUPS, 8), ALU.mult))
                    link(TTen(selm, selm, spread(r_rank[:, t, :], GROUPS, 8), ALU.add))
                    link(dve.max(r_top[:, t, :], r_selm[:, t, :]))
                    link(dve.match_replace(r_rep[:, t, :], r_top[:, t, :], r_selm[:, t, :], -3e38))
                link(TS(r_mask, r_rep, -2e38, None, ALU.is_lt))
                dve.nop().then_inc(mask_ready[l], 1)
                link(TTen(r_gate, r_sc, r_mask, ALU.mult))
                link(dve.tensor_reduce(r_den, r_gate, X, ALU.add))
                link(dve.reciprocal(r_den, r_den))
                link(TS(r_den, r_den, ROUTED_SCALE, None, ALU.mult))
                link(TTen(r_gate, r_gate, r_den.unsqueeze(2).to_broadcast([P, TT, EXPERTS]), ALU.mult))
                dve.wait_ge(pos_done[l], 1)
                link(STT(r_pos, bC[:, 0:2 * EXPERTS].rearrange("p (t e) -> p t e", t=TT), 1.0, r_mask, ALU.add, ALU.mult))
                link(TS(r_pos, r_pos, -1.0, None, ALU.add))
                select(l, 0, None)
                dve.memset(r_ov[0:64, 3:4], 0.0)
                dve.memset(r_ovp[0:64, 0:1], 0.0)
                link(TTen(r_ov[0:64, 0:3], c_("thr", 64), bC[0:64, 128:129].to_broadcast([64, 3]), ALU.is_lt))
                link(dve.tensor_copy(r_ovp[0:64, 1:2], r_ov[0:64, 0:1]))
                link(TTen(r_ovp[0:64, 2:3], r_ovp[0:64, 1:2], r_ov[0:64, 1:2], ALU.add))
                link(TTen(r_ovp[0:64, 3:4], r_ovp[0:64, 2:3], r_ov[0:64, 2:3], ALU.add))
                dve.nop().then_inc(over_ready[l], 1)

            def shared_hidden(l):
                dve.wait_ge(sh_silu[l], 1)
                dve.wait_ge(sh_gu[l], 2)
                TTen(hTs[:, :, :].rearrange("p f t -> p (f t)"), sils[:, :, :].rearrange("p f t -> p (f t)"), bH[:, :],
                     ALU.mult).then_inc(sh_h[l], 1)

            def visit_list(l):
                dve.wait_ge(idx_done[l], 1)
                link(dve.tensor_copy(r_idx[0:64, :], bC[0:64, 0:4]))
                for p in range(3):
                    m = TS(r_hot[0:64, p, :], c_("kiota", 64), r_idx[0:64, p:p + 1], r_ov[0:64, p:p + 1],
                           ALU.is_equal, ALU.mult)
                m.then_inc(hot_ready[l], 1)
                shared_hidden(l)
                link(dve.memset(visit_f[0:1, 0, :], 0.0))
                link(dve.memset(visit_f[0:1, 1, :], float(SLOTS * PASSES)))
                dve.memset(visit_f[0:1, 1, 0:EXPERTS], 0.0)
                dve.tensor_copy(visit_f[0:1, 0, 0:EXPERTS], c_("base", 1))
                link(TS(r_q[0:1, :], c_("quad4", 1), r_idx[0:1, 3:4], None, ALU.is_lt))
                link(dve.tensor_reduce(r_den[0:1, 0:1], r_q[0:1, :], X, ALU.add))
                link(TS(r_den[0:1, 0:1], r_den[0:1, 0:1], float(QUADS), None, ALU.add))
                dve.tensor_copy(nquads[0:1, 0:1], r_den[0:1, 0:1])
                dve.wait_ge(gath_done[l], 2)
                dve.tensor_copy(xg[:, 0, 4:8, :].rearrange("p c s -> p (c s)"), bB[:, :]).then_inc(xgB_ready[l], 1)
                dve.wait_ge(list_done[l], 1)
                link(dve.tensor_copy(r_list[0:1, :, :].rearrange("p a k -> p (a k)"), bC[0:1, 0:2 * EXTRA]))
                link(TS(r_hot[0:1, 0, :], r_list[0:1, 1, :], 0.0, float(SLOTS * PASSES), ALU.is_equal, ALU.mult))
                TTen(visit_f[0:1, 1, EXPERTS:EXPERTS + EXTRA], r_list[0:1, 1, :], r_hot[0:1, 0, :], ALU.add)
                link(dve.tensor_copy(visit_f[0:1, 0, EXPERTS:EXPERTS + EXTRA], r_list[0:1, 0, :]))
                link(dve.tensor_copy(visit[0:1, :, :], visit_f[0:1, :, :]))
                dve.nop().then_inc(visits_ready[l], 1)

            def select(l, a, first):
                for s in range(2):
                    if first is None:
                        e, off = s, 0
                    else:
                        at = first + (2 * a + s)
                        e = dve.value_load(visit[0:1, 0, bass.ds(at, 1)], min_val=0, max_val=EXPERTS - 1)
                        off = dve.value_load(visit[0:1, 1, bass.ds(at, 1)], min_val=0, max_val=SLOTS * PASSES)
                    cols = slice(s * SLOTS, (s + 1) * SLOTS)
                    base = CONST["iota"][0]
                    for t in range(TT):
                        place = r_pos[:, t, bass.ds(e, 1)]
                        slot_no = cst[:, bass.ds(off + base, SLOTS)]
                        TS(Sel[:, a, t, cols], slot_no, place, None, ALU.is_equal)
                        m = TS(Selg[:, a, t, cols], slot_no, place, r_gate[:, t, bass.ds(e, 1)], ALU.is_equal, ALU.mult)
                m.then_inc(sel_ready[l], 1)

            def experts(l):
                n = dve.value_load(nquads[0:1, 0:1], min_val=QUADS, max_val=MAX_QUADS)
                with dve.Fori(0, n) as i:
                    for a in range(2):
                        dve.wait_ge(gsum_done[l], i * 2 + (a + 1))
                        dve.tensor_copy(slot_gate[:, a:a + 1], bC[:, 0:1]).then_inc(gsum_taken[l], 1)
                        dve.wait_ge(gath_done[l], i * 4 + (2 * a + 2))
                        if a:
                            dve.wait_ge(turn_done[l], i * 2 + 2)
                            select(l, 0, i * 4 + 2 + 2)
                        else:
                            dve.wait_ge(turn_done[l], i * 2 + 1)
                            select(l, 1, i * 4)
                        dve.wait_ge(silu_ready[l], i * 2 + (a + 1))
                        dve.wait_ge(gsum_taken[l], i * 2 + (a + 1))
                        STT(hid_s[:, a, :], sil[:, a, :], slot_gate[:, a:a + 1], bH[:, F_EXP:2 * F_EXP],
                            ALU.mult, ALU.mult).then_inc(h_ready[l], 1)
                        dve.wait_ge(gath_done[l], i * 4 + (2 * a + 4))
                        dve.tensor_copy(xg[:, 1 - a, 4:8, :].rearrange("p c s -> p (c s)"), bB[:, :])\
                           .then_inc(xgB_ready[l], 1)
                        for hh, b in ((0, bA), (1, bB)):
                            cols = slice(hh * 512, (hh + 1) * 512)
                            dve.wait_ge(y_high_ready[l], i * 4 + (2 * a + hh + 1))
                            TTen(y_low[:, cols], b[:, :], y_high[:, cols].bitcast(F32), ALU.subtract)\
                                .then_inc(y_low_ready[l], 1)

            def compress():
                dve.wait_ge(proj_taken[1], KCMP_JOB)
                for kv in range(2):
                    src = KTc[:, kv, :]
                    win = bass.AP(src.tensor, src.offset, [src.ap[0], (1, CMP_LEN), (CMP_STRIDE, NC_BLK)])
                    m = TTen(Xw[:, kv, :, :], win, posT[:, kv, :].unsqueeze(2).to_broadcast([P, CMP_LEN, NC_BLK]), ALU.add)
                m.then_inc(win_ready, 1)
                dve.memset(hid4[:, :, :], 0.0)
                dve.memset(VBD[:, :, :, :], 0.0)
                link(dve.memset(ec[:, :, :, :], 0.0))
                dve.wait_ge(hid_done, 1)
                for g in range(G_C):
                    r = slice(64 * g, 64 * g + 64)
                    m = dve.tensor_copy(hid_t[r, 0:2, 0:NC_BLK],
                                        bank[6 + g][r, 0:32].rearrange("p (a c) -> p a c", a=2)[:, :, 0:NC_BLK])
                link(m)
                h, u = hid_t[:, 0:2, 0:NC_BLK], hid_t[:, 2:4, 0:NC_BLK]
                link(TTen(u, h, h, ALU.mult))
                link(TS(u, u, 0.044715, 1.0, ALU.mult, ALU.add))
                link(TTen(u, u, h, ALU.mult))
                link(TS(u, u, 2.0 * math.sqrt(2.0 / math.pi), None, ALU.mult))
                dve.nop().then_inc(hid_z, 1)
                dve.wait_ge(hid_e, 1)
                link(TS(u, u, 1.0, None, ALU.add))
                link(dve.reciprocal(u, u))
                link(TTen(hid[:, :, 0:NC_BLK], h, u, ALU.mult))
                link(dve.tensor_copy(hid4[:, :, 0:NC_BLK], hid[:, 1:2, 0:NC_BLK].to_broadcast([P, 4, NC_BLK])))
                dve.nop().then_inc(hid_ready, 1)
                dve.wait_ge(kv_done, 1)
                for g in range(G_C):
                    r = slice(64 * g, 64 * g + 64)
                    dve.tensor_copy(kcT[r, 0:NC_BLK], bank[6 + g][r, 64:64 + NC_BLK])
                    for h4 in range(4):
                        q = slice(32 * h4, 32 * h4 + 32)
                        m = dve.tensor_copy(VBD[q, g, h4, :], bank[6 + g][q, 128:192])
                m.then_inc(kv_taken, 1)

            def gates_and_lambda():
                l1 = s_("lam").rearrange("p (a d) -> p a d", a=4)
                dve.tensor_tensor_reduce(tmp[:, 0:64], l1[:, 0, :], l1[:, 1, :], 1.0, 0.0, ALU.mult, ALU.add, lam[:, 0:1])
                dve.tensor_tensor_reduce(tmp[:, 64:128], l1[:, 2, :], l1[:, 3, :], 1.0, 0.0, ALU.mult, ALU.add,
                                         lam[:, 1:2]).then_inc(lam_s, 1)
                dve.wait_ge(lam_e, 1)
                link(TTen(lam[:, 2:3], lam[:, 1:2], lam[:, 0:1], ALU.subtract))
                link(TS(lam[:, 2:3], lam[:, 2:3], -LAM_INIT, None, ALU.add))
                dve.wait_ge(proj_taken[1], 3)
                link(TS(gates3[:, :, :], gates3[:, :, :], 1.0, None, ALU.add))
                link(dve.reciprocal(gates3[:, :, :], gates3[:, :, :]))

            def compressed_softmax():
                dve.wait_ge(cmp_s, 1)
                dve.wait_ge(bias_in, 32)
                seen = [7, NC_BLK]
                link(dve.memset(ec[:, 0, :, seen[0]:NC_BLK], NEG))
                for t in range(TT):
                    first = P * t + P - 1 - (CMP_LEN - 1)
                    for g in range(G_C):
                        n = seen[t]
                        zz = biasZ[:, 4 * g:4 * g + 4, :]
                        bias = bass.AP(zz.tensor, zz.offset + first, [zz.ap[0], (TOK, 4), (-CMP_STRIDE, n)])
                        s = bank[g][:, t * 64:(t + 1) * 64].rearrange("p (r c) -> p r c", r=R_C)[:, :, 0:n]
                        m = STT(ec[:, t, 4 * g:4 * g + 4, 0:n], s, HD ** -0.5, bias, ALU.mult, ALU.add)
                link(m)
                e = ec[:, :, :, 0:NC_BLK].rearrange("p t h c -> p (t h) c")
                cmax, csum = cs[:, 0, :], cs[:, 1, :]
                link(dve.tensor_reduce(cmax, e, X, ALU.max))
                link(TTen(e, e, cmax.unsqueeze(2).to_broadcast([P, 16, NC_BLK]), ALU.subtract))
                dve.nop().then_inc(cmp_c, 1)
                dve.wait_ge(cmp_e, 1)
                for t in range(TT):
                    v = c_("valid").rearrange("p (t c) -> p t c", t=TT)[:, t:t + 1, 0:NC_BLK].to_broadcast([P, H_C, NC_BLK])
                    m = TTen(ec[:, t, :, 0:NC_BLK], ec[:, t, :, 0:NC_BLK], v, ALU.mult)
                link(m)
                dve.nop().then_inc(cmp_p, 1)
                link(dve.tensor_reduce(csum, e, X, ALU.add))
                link(TS(csum, csum, 1e-30, None, ALU.max))
                link(dve.reciprocal(csum, csum))
                link(TTen(csum.rearrange("p (t h) -> p t h", t=TT), csum.rearrange("p (t h) -> p t h", t=TT),
                          gates3[:, :, 0:8], ALU.mult))
                dve.wait_ge(cmp_o, 1)
                for t in range(TT):
                    m = TTen(heads(o_tok[:, t, 0:512], 8), heads(bank[6 + t][:, :], 8),
                             spread(csum[:, 8 * t:8 * t + 8], 8), ALU.mult)
                link(m)

            for l in range(DEPTH):
                if l == 0:
                    bias_rows()
                    latent_norms()
                    rotate_queries()
                else:
                    gates_and_lambda()
                    compress()
                    compressed_softmax()
                attention(l)
                norm(2 * l, y_done[l])
                router(l)
                visit_list(l)
                experts(l)
                norm(2 * l + 1, moe_done[l])


def _constants():
    c = np.zeros((P, N_CONST), np.float32)

    def put(name, a):
        at, n = CONST[name]
        a = np.asarray(a, np.float32)
        c[:a.shape[0], at:at + n] = a.reshape(a.shape[0], n)

    p = np.arange(P)
    put("ident", np.eye(P))
    put("tri", p[:, None] < p[None, :])
    put("ones", np.ones((P, P)))
    put("iota", np.tile(np.arange(SLOTS * (PASSES + 1)), (P, 1)))
    freqs = np.float32(10000.0) ** (-np.arange(HALF, dtype=np.float32) / np.float32(HALF))
    ang = (np.arange(TOK, dtype=np.float32)[:, None] * freqs).astype(np.float32)
    for name, f in (("cos", np.cos), ("sin", np.sin)):
        put(name, f(ang).reshape(TT, P, HALF).transpose(1, 0, 2))
    tok = np.arange(TOK).reshape(TT, P).T
    put("valid", (tok[:, :, None] - (np.arange(16) * CMP_STRIDE + CMP_LEN - 1)) >= 0)
    g = np.arange(GROUPS)
    put("gtri", np.tile((g[None, :] < g[:, None]).reshape(1, -1), (P, 1)))
    put("kiota", np.tile(np.arange(EXTRA), (64, 1)))
    put("thr", np.tile(SLOTS * np.arange(1, PASSES), (64, 1)))
    put("ecode", np.arange(EXPERTS)[:, None])
    put("pcode", np.tile(SLOTS * np.arange(1, PASSES), (64, 1)))
    put("base", np.arange(EXPERTS)[None, :])
    put("quad4", 4 * np.arange(8)[None, :])

    d = np.arange(SPAN) - (P - 1)
    n = np.maximum(d, 0)
    ratio = (np.log(np.maximum(n, 1).astype(np.float32) / np.float32(16)) / np.float32(math.log(2048 / 16))).astype(np.float32)
    large = 16 + (ratio * np.float32(16)).astype(np.int32)
    bucket = np.where(n < 16, n, np.minimum(large, BUCKETS - 1))
    hot = (bucket[None, :] == np.arange(BUCKETS)[:, None]).astype(np.float32)
    mask = np.where(d < 0, NEG, 0.0)[None, :].repeat(BIAS_ROWS, 0)
    mask[0:4] = np.where((d < 0) | (d > 128), NEG, 0.0)
    mask[4:8] = np.where((d < 0) | (d % 4 != 0), NEG, 0.0)
    mask[8:12] = np.where((d < 0) | (d % 16 != 0), NEG, 0.0)
    return c, hot, mask.astype(np.float32)


def _chunks(w):
    r, n = w.shape
    return w.reshape(r // P, P, n).transpose(1, 0, 2).reshape(P, -1)


def _lay_out(a):
    f = np.float32
    mix = np.zeros((DEPTH, MIX_BLOCKS - 1, P, SLOT_W), f)

    def put(l, k, *parts):
        at = 0
        for p in parts:
            mix[l, k, :, at:at + p.shape[1]] = p
            at += p.shape[1]

    w = a["ab_w_in"][0]
    put(0, 0, _chunks(w[:, :C_IN]))
    for k in range(3):
        put(0, 1 + k, _chunks(w[:, C_IN + 768 * k:C_IN + 768 * (k + 1)]))
    put(0, 4, _chunks(a["mla_w_uq"][0]), a["mla_w_ukv"][0])
    w = a["cd_w_in"][0]
    qc = w[:, :512].reshape(D, G_C, R_C, HD).transpose(0, 2, 1, 3).reshape(D, 512)
    put(1, 0, _chunks(np.concatenate([qc, w[:, 1280:1304]], 1)))
    order = [0, 1, 2, 4, 3, 5]
    put(1, 1, _chunks(np.concatenate([w[:, 512 + P * i:512 + P * (i + 1)] for i in order], 1)))
    for k in range(2):
        w1 = a[("nsa_cmp_k_w1", "nsa_cmp_v_w1")[k]][0].reshape(CMP_LEN, HD, 64).transpose(1, 0, 2).reshape(HD, -1)
        put(1, 2 + k, _chunks(w[:, 1304 + 512 * k:1304 + 512 * (k + 1)]), np.concatenate([w1, w1], 0))
    put(1, 4, _chunks(w[:, 2328:2840]))
    for l, name in enumerate(("ab_w_out", "cd_w_out")):
        for hh in range(2):
            put(l, 5 + hh, _chunks(a[name][0][:, hh * 512:(hh + 1) * 512]))
    exp = np.empty((DEPTH, EXPERTS + 1, P, SLOT_W), f)
    gu = exp[..., :GU].reshape(DEPTH, EXPERTS + 1, P, DC, 2, F_EXP)
    dn = exp[..., GU:].reshape(DEPTH, EXPERTS + 1, P, 2, D)
    for l in range(DEPTH):
        for k, (r, s) in enumerate((("exp_w_gate", "sh_w_gate"), ("exp_w_up", "sh_w_up"))):
            gu[l, :EXPERTS, :, :, k] = a[r][l].reshape(EXPERTS, DC, P, F_EXP).transpose(0, 2, 1, 3)
            gu[l, EXPERTS, :, :, k] = a[s][l].reshape(DC, P, F_EXP).transpose(1, 0, 2)
        dn[l, :EXPERTS] = a["exp_w_down"][l].reshape(EXPERTS, 2, P, D).transpose(0, 2, 1, 3)
        dn[l, EXPERTS] = a["sh_w_down"][l].reshape(2, P, D).transpose(1, 0, 2)
    exp[..., :GU] = gu.reshape(DEPTH, EXPERTS + 1, P, GU)
    exp[..., GU:] = dn.reshape(DEPTH, EXPERTS + 1, P, 2 * D)
    const, hot, mask = _constants()
    x = a["x"][0]
    rel = a["rel_bias"]
    small = np.concatenate([a["mla_q_norm"][0], a["mla_kv_norm"][0], a["diff_norm"][0]]
                           + [a[f"diff_lambda_{n}"][0] for n in ("q1", "k1", "q2", "k2")]
                           + [a["router_b"].reshape(-1)])[None, :]
    return {
        "x": x, "xT_in": np.ascontiguousarray(x.T), "mixw": mix, "expw": exp, "const": const,
        "tab": np.concatenate([rel[:, :12], np.zeros((BUCKETS, 1), f), rel[:, 12:]], 1),
        "hot": hot, "mask": mask, "small": small,
        "lnp": np.stack([np.concatenate([a[f"ln{h}_g"][l], a[f"ln{h}_b"][l]]) for l in range(DEPTH) for h in (1, 2)]),
        "routw": a["router_w"].reshape(DEPTH, DC, P, EXPERTS).transpose(0, 2, 1, 3),
        "pos": np.tile(np.stack([a["nsa_cmp_pos_k"][0].T, a["nsa_cmp_pos_v"][0].T], 1), (2, 1, 1)),
        "w2": np.tile(np.stack([a["nsa_cmp_k_w2"][0], a["nsa_cmp_v_w2"][0]], 1), (2, 1, 1)),
    }


def kernel(**inputs):
    import concourse.bacc as _bacc
    from concourse.bass_utils import run_bass_kernel_spmd as _run

    arrays = {k: np.ascontiguousarray(v) for k, v in _lay_out({k: np.asarray(v) for k, v in inputs.items()}).items()}
    nc = _bacc.Bacc("TRN2", target_bir_lowering=False, num_devices=1)
    args = {k: nc.dram_tensor(f"in_{k}", v.shape, mybir.dt.float32, kind="ExternalInput").ap() for k, v in arrays.items()}
    out = nc.dram_tensor("out_0_dram", (TOK, D), mybir.dt.float32, kind="ExternalOutput").ap()
    build(nc, out=out, **args)
    r = _run(nc, [{f"in_{k}": v for k, v in arrays.items()}], core_ids=[0])
    return r.results[0]["out_0_dram"].reshape(1, TOK, D)
```

```python
import math
from contextlib import ExitStack

import numpy as np

import concourse.bass as bass
from concourse import mybir

P = 128
TOK = 256
TT = TOK // P
D = 1024
DC = D // P
DEPTH = 2
ALPHA = (2 * DEPTH) ** 0.25
LN_EPS, RMS_EPS = 1e-5, 1e-6
NEG = -1e30

H_A, NOPE, ROPE, MLA_V = 12, 64, 32, 64
Q_LORA, KV_LORA = 256, 128
QK_A = NOPE + ROPE
HALF = ROPE // 2
H_B, HD = 12, 64
H_C, G_C, R_C = 8, 2, 4
H_D = 4
CMP_LEN, CMP_STRIDE = 32, 16
NC_BLK = (TOK - CMP_LEN) // CMP_STRIDE + 1
LAM_INIT = 0.8 - 0.6 * math.exp(-0.3 * 1)
BUCKETS = 32

EXPERTS, TOP_K, GROUPS, TOP_GROUPS = 64, 8, 8, 4
F_EXP = 256
ROUTED_SCALE = 2.5
SLOTS = 64
PASSES = TOK // SLOTS
EXTRA = TOK * TOP_K // SLOTS
QUADS = EXPERTS // 4
MAX_QUADS = QUADS + EXTRA // 4
VISITS = 4 * (MAX_QUADS + 1)

C_IN = Q_LORA + KV_LORA + ROPE
GU = DC * 2 * F_EXP
SLOT_W = GU + 2 * D
RING = 4
MIX_BLOCKS = 8
MIX_SIZE = [[DC * C_IN, DC * 768, DC * 768, DC * 768, 2 * 1152 + 1536, DC * 512, DC * 512],
            [DC * 536, DC * 768, DC * 512 + 2048, DC * 512 + 2048, DC * 512, DC * 512, DC * 512]]

SPAN = P + TOK - 1
BIAS_ROWS = 25
BIAS_OF = [(0, 13), (13, 12)]

CONST = {}
_at = 0
for _name, _n in (("ident", P), ("tri", P), ("ones", P), ("iota", SLOTS * (PASSES + 1)),
                  ("cos", TT * HALF), ("sin", TT * HALF), ("valid", TT * 16), ("gtri", 64),
                  ("kiota", EXTRA), ("thr", 3), ("ecode", 1), ("pcode", 3), ("base", EXPERTS), ("quad4", 8)):
    CONST[_name] = (_at, _n)
    _at += _n
N_CONST = _at
SMALL = {"qn": (0, 256), "kvn": (256, 128), "dn": (384, 128), "lam": (512, 256), "rb": (768, 128)}
N_SMALL = 896


def build(nc, x, xT_in, mixw, expw, const, tab, hot, mask, small, lnp, routw, pos, w2, out):
    F32, FR, I32 = mybir.dt.float32, mybir.dt.float32r, mybir.dt.int32
    ALU, ACT = mybir.AluOpType, mybir.ActivationFunctionType
    X = mybir.AxisListType.X
    scratch = nc.dram_tensor("bias_rows_dram", (BIAS_ROWS, SPAN), F32, kind="Internal").ap()

    with ExitStack() as ctx:
        def sb(name, shape, dt=F32):
            return ctx.enter_context(nc.sbuf_tensor(name, shape, dt))

        def sem(name):
            return ctx.enter_context(nc.semaphore(name))

        def per_layer(name):
            return [sem(f"{name}_{l}") for l in range(DEPTH)]

        bank = [ctx.enter_context(nc.psum_tensor(f"bank{i}", [P, 512], F32)) for i in range(8)]
        Ybank = [[bank[2 * t + hh] for hh in range(2)] for t in range(TT)]
        bA, bB, bC, bH = bank[4], bank[5], bank[6], bank[7]

        ring = sb("ring", [P, RING, SLOT_W])
        x_tok = sb("x_tok", [P, TT, D])

        def shared_space(name, words, *views):
            offset = nc.sbuf_base
            sb(name, [P, words])
            return [nc.alloc_sbuf_tensor_at(n, shape, dt, offset=offset + 4 * at) for n, shape, dt, at in views]

        xT = sb("xT", [P, DC, TOK])
        zb, x_high = shared_space("z_space", TT * 1152, ("zb", [P, TT * 1152], F32, 0), ("x_high", [P, TT, D], FR, 0))
        biasZ, x_low = shared_space("bias_space", 13 * TOK, ("biasZ", [P, 13, TOK], F32, 0), ("x_low", [P, TT, D], FR, 0))
        arena, Sel, y_high, y_low, selT = shared_space(
            "arena_space", 12288, ("arena", [P, 12288], F32, 0), ("Sel", [P, 2, TT, P], FR, 5632),
            ("y_high", [P, D], FR, 2048), ("y_low", [P, D], FR, 3072), ("selT", [P, 2, TOK], FR, 4096))
        probs = sb("probs", [P, 3, 3 * P])
        probsT = sb("probsT", [P, 2, 3 * P])
        tmp = sb("tmp", [P, 832])
        cst = sb("cst", [P, N_CONST])
        sml = sb("sml", [P, N_SMALL])
        rw = sb("rw", [P, DC, EXPERTS])
        posT = sb("posT", [P, 2, CMP_LEN])
        w2s = sb("w2s", [P, 2, HD])
        negmax = sb("negmax", [P, TT, 24])
        rowsum = sb("rowsum", [P, TT, 24])
        rinv = sb("rinv", [P, TT, 24])
        gates3 = sb("gates3", [P, TT, 24])
        wg = sb("wg", [P, TT, 24])
        st = sb("st", [P, 64])
        lam = sb("lam", [P, 8])
        visit = sb("visit", [1, 2, VISITS], I32)
        nquads = sb("nquads", [1, 4], I32)

        def area(at, *shape):
            n = int(np.prod(shape))
            ap = arena[:, at:at + n]
            if len(shape) > 1:
                names = "abcd"[:len(shape)]
                ap = ap.rearrange(f"p ({' '.join(names)}) -> p {' '.join(names)}",
                                  **{k: v for k, v in zip(names[1:], shape[1:])})
            return ap

        def zview(at, *shape):
            n = int(np.prod(shape))
            names = "abcd"[:len(shape)]
            return zb[:, at:at + n].rearrange(f"p ({' '.join(names)}) -> p {' '.join(names)}",
                                              **{k: v for k, v in zip(names[1:], shape[1:])})

        def c_(name, rows=P):
            at, n = CONST[name]
            return cst[0:rows, at:at + n]

        def halves_of(k, t):
            return 2 * TT * k + 2 * t + 2

        def s_(name):
            at, n = SMALL[name]
            return sml[:, at:at + n]

        ident = c_("ident")
        z = zview(0, TT, D)
        o_tok = z
        q_tok = zview(0, TT, 1152)
        ctok = zview(0, TT, C_IN)
        cn = zview(TT * C_IN, TT, 480)
        cT = probs[:, 0:2, :].rearrange("p a b -> p (a b)").rearrange("p (c t) -> p c t", c=3)
        oT = xT
        ob = xT[:, 0:4, :].rearrange("p c t -> p (c t)").rearrange("p (a n) -> p a n", a=TT)
        V0 = area(0, TT, 24 * HD)
        KTm = area(3072, H_A, TOK)
        QTd = area(6144, 6, TOK)
        KTd = area(7680, 6, TOK)
        QTm = area(9216, H_A, TOK)
        QTc = area(0, R_C, TOK)
        QTf = area(1024, H_D, TOK)
        KTc = area(2048, 4, TOK)
        KTf = area(3072, H_D, TOK)
        Vs = area(4096, TT, 2 * P)
        Vf = area(4608, TT, 512)
        Xw = area(5632, 2, CMP_LEN, NC_BLK)
        hid = area(6592, 2, 16)
        hid_t = area(6624, 4, 16)
        hid4 = area(6688, 4, 32)
        kcT = area(6816, 16)
        VBD = area(6832, G_C, 4, HD)
        ec = area(7344, TT, H_C, 32)
        ecT = area(7856, TT, G_C, P)
        cs = area(8368, 6, 16)
        xg = area(0, 2, DC, P)
        hT = area(4608, TOK)
        slot_gate = area(9800, 2)
        sil = area(5120, 2, F_EXP)
        Selg = area(6144, 2, TT, P)
        sils = area(6656, 2, TOK)
        hTs = area(7168, 2, TOK)
        r_sc, r_sel, r_m8, r_selm, r_rep, r_mask, r_gate, r_pos = (
            area(7680 + 128 * i, TT, EXPERTS) for i in range(8))
        r_gs, r_rank, r_gm, r_top = (area(8704 + 16 * i, TT, GROUPS) for i in range(4))
        hid_s = area(9288, 2, F_EXP)
        r_gt = area(8768, GROUPS, GROUPS)
        r_eq = area(8832, GROUPS, GROUPS)
        r_ov = area(8896, 4)
        r_ovp = area(8900, 4)
        r_idx = area(8904, 4)
        r_hot = area(8912, 3, EXTRA)
        r_list = area(9008, 2, EXTRA)
        r_den = area(9072, TT)
        r_q = area(9080, 8)
        visit_f = area(9088, 2, VISITS)
        lng = area(10240, 2, D)

        const_in, x_in, small_in, scratch_out, out_done = map(sem, (
            "const_in", "x_in", "small_in", "scratch_out", "out_done"))
        bias_ps, bias_sb = sem("bias_ps"), sem("bias_sb")
        bias_in = sem("bias_in")
        rw_in = sem("rw_in")
        ln_in = sem("ln_in")
        dn_loaded = [[sem(f"ring{k}_down_loaded_{l}") for k in range(RING)] for l in range(DEPTH)]
        half_loaded = [[sem(f"ring{k}_half_loaded_{l}") for k in range(RING)] for l in range(DEPTH)]
        loaded = [[sem(f"ring{k}_loaded_{l}") for k in range(RING)] for l in range(DEPTH)]
        proj_done, proj_taken = per_layer("proj_done"), per_layer("proj_taken")
        xT_in_1, w_in_1, warm = sem("xT_in_first_half"), sem("w_in_first_half"), sem("warm_operand")
        key_spread = sem("key_spread")
        rms_var, rms_std = sem("rms_var"), sem("rms_std")
        cn_ready, q_roped = sem("cn_ready"), sem("q_roped")
        scores_done = per_layer("scores_done")
        max_ready, probs_ready = per_layer("max_ready"), per_layer("probs_ready")
        pt_done, pt_taken, pv_done = per_layer("pt_done"), per_layer("pt_taken"), per_layer("pv_done")
        o_taken = per_layer("o_taken")
        comb_d, comb_w = sem("comb_d"), sem("comb_w")
        o_ready, oT_done, oT_taken = per_layer("o_ready"), per_layer("oT_done"), per_layer("oT_taken")
        y_done = per_layer("y_done")
        ln_var, ln_std = map(sem, ("ln_var", "ln_std"))
        x_new = sem("x_new")
        xT_done, xT_taken = sem("xT_done"), sem("xT_taken")
        logit_done, esig_ready = per_layer("logit_done"), per_layer("esig_ready")
        mask_ready, pos_done = per_layer("mask_ready"), per_layer("pos_done")
        over_ready, idx_done = per_layer("over_ready"), per_layer("idx_done")
        hot_ready, list_done, visits_ready = per_layer("hot_ready"), per_layer("list_done"), per_layer("visits_ready")
        sh_gu, sh_silu, sh_h = per_layer("sh_gu"), per_layer("sh_silu"), per_layer("sh_h")
        sh_down = per_layer("sh_down")
        sel_ready, gath_done, xgA_ready, xgB_ready = (per_layer(n) for n in (
            "sel_ready", "gath_done", "xgA_ready", "xgB_ready"))
        gu_done, silu_ready, h_ready = per_layer("gu_done"), per_layer("silu_ready"), per_layer("h_ready")
        turn_done, turn_ready = per_layer("turn_done"), per_layer("turn_ready")
        down_done, y_high_ready, y_low_ready = (per_layer(n) for n in ("down_done", "y_high_ready", "y_low_ready"))
        moe_done = per_layer("moe_done")
        gsum_done, gsum_taken = per_layer("gsum_done"), per_layer("gsum_taken")
        win_ready, hid_done, hid_z, hid_e, hid_ready = map(sem, ("win_ready", "hid_done", "hid_z", "hid_e", "hid_ready"))
        kv_done, kv_taken = sem("kv_done"), sem("kv_taken")
        cmp_s, cmp_c, cmp_e, cmp_p = map(sem, ("cmp_s", "cmp_c", "cmp_e", "cmp_p"))
        cmpT_done, cmpT_taken, cmp_o, cmp_taken = map(sem, ("cmpT_done", "cmpT_taken", "cmp_o", "cmp_taken"))
        high_ready, low_ready = sem("x_high_ready"), sem("x_low_ready")
        lam_s, lam_e = sem("lam_s"), sem("lam_e")
        dn_var, dn_std = sem("dn_var"), sem("dn_std")
        dve_step, act_step = sem("dve_step"), sem("act_step")

        def mm_group(pe, outap, pairs):
            for k, (l, r) in enumerate(pairs):
                last = pe.matmul(outap, l, r, start=(k == 0), stop=(k == len(pairs) - 1))
            return last

        def slot(block, at, chunks, cols):
            return ring[:, block % RING, at:at + chunks * cols].rearrange("p (c n) -> p c n", c=chunks)

        def tokens_out(w, t, lo, n, src=xT, chunks=DC):
            return lambda pe, b: mm_group(pe, b[:, 0:n], [(src[:, c, t * P:(t + 1) * P], w[:, c, lo:lo + n])
                                                          for c in range(chunks)])

        def two_T(w, cols, part=None):
            def go(pe, b):
                for k, lhs in enumerate(cols):
                    if part is not None:
                        hidden_part(pe, part + k)
                    m = mm_group(pe, b[:, k * TOK:(k + 1) * TOK], [(lhs(w, c), xT[:, c, :]) for c in range(DC)])
                return m
            return go

        def jobs0():
            wA, wq, wk, wv = (slot(k, 0, DC, n) for k, n in ((0, C_IN), (1, 768), (2, 768), (3, 768)))
            wuq = slot(4, 0, 2, 1152)
            wukv = ring[:, 0, 2304:2304 + 1536].rearrange("p (h a d) -> p h a d", h=H_A, a=2)
            jobs = []
            for t in range(TT):
                jobs.append((0, t == 1, [], None, [(ctok[:, t, :], (P, 0, C_IN))]))
            for blk, w, dst in ((1, wq, QTd), (2, wk, KTd)):
                for k in range(3):
                    cols = [lambda w, c, i=i: w[:, c, i * P:(i + 1) * P] for i in (2 * k, 2 * k + 1)]
                    jobs.append((blk, k == 2, [], two_T(w, cols),
                                 [(dst[:, 2 * k:2 * k + 2, :].rearrange("p a t -> p (a t)"), (P, 0, 512))]))
            for t in range(TT):
                for lo, n in ((0, 512), (512, 256)):
                    jobs.append((3, t == 1 and lo > 0, [], tokens_out(wv, t, lo, n),
                                 [(V0[:, t, lo:lo + n], (P, 0, n))]))

            def turn_q(pe, b):
                for c in range(2):
                    for t in range(TT):
                        m = pe.transpose(b[:, c * TOK + t * P:c * TOK + (t + 1) * P], cn[:, t, c * P:(c + 1) * P], ident)
                return m

            def turn_kv(pe, b):
                for t in range(TT):
                    pe.transpose(b[:, t * P:(t + 1) * P], cn[:, t, 2 * P:3 * P], ident)
                for t in range(TT):
                    m = pe.transpose(b[0:QK_A, TOK + t * P:TOK + (t + 1) * P], cn[:, t, 384:480], ident)
                return m

            jobs.append((None, False, [(cn_ready, 1)], turn_q,
                         [(cT[:, 0:2, :].rearrange("p a t -> p (a t)"), (P, 0, 512))]))
            jobs.append((None, False, [], turn_kv,
                         [(cT[:, 2, :], (P, 0, TOK)), ("rope key", None)]))
            n_cT = len(jobs)
            for t in range(TT):
                for k, (lo, n) in enumerate(((0, 512), (512, 512), (1024, 128))):
                    jobs.append((4, False, [(proj_taken[0], n_cT)] if t == 0 and k == 0 else [],
                                 tokens_out(wuq, t, lo, n, cT, 2), [(q_tok[:, t, lo:lo + n], (P, 0, n))]))
            n_q = len(jobs)
            for k in range(6):
                def nope(pe, b, k=k):
                    for i in range(2):
                        m = pe.matmul(b[0:NOPE, i * TOK:(i + 1) * TOK], wukv[:, 2 * k + i, 0, :], cT[:, 2, :],
                                      start=True, stop=True)
                    return m
                jobs.append((4, False, [], nope,
                             [(KTm[0:NOPE, 2 * k:2 * k + 2, :].rearrange("p a t -> p (a t)"), (NOPE, 0, 512))]))
            for t in range(TT):
                for h0, n in ((0, 8), (8, 4)):
                    def vals(pe, b, t=t, h0=h0, n=n):
                        return pe.matmul(b[:, 0:n * HD].rearrange("p (h d) -> p h d", h=n),
                                         cT[:, 2, t * P:(t + 1) * P], wukv[:, h0:h0 + n, 1, :], start=True, stop=True)
                    jobs.append((4, t == 1 and h0 > 0, [], vals,
                                 [(V0[:, t, 768 + h0 * HD:768 + (h0 + n) * HD], (P, 0, n * HD))]))
            for k in range(6):
                def turn(pe, b, k=k):
                    for i in range(2):
                        for t in range(TT):
                            m = pe.transpose(b[0:QK_A, i * TOK + t * P:i * TOK + (t + 1) * P],
                                             q_tok[:, t, (2 * k + i) * QK_A:(2 * k + i + 1) * QK_A], ident)
                    return m
                jobs.append((None, False, [(q_roped, TT)] if k == 0 else [], turn,
                             [(QTm[0:QK_A, 2 * k:2 * k + 2, :].rearrange("p a t -> p (a t)"), (QK_A, 0, 512))]))
            return jobs, n_cT, n_q

        def hidden_part(pe, n):
            kv, quarter = n // 4, n % 4
            if n == 0:
                pe.wait_ge(win_ready, 1)
            if quarter == 0:
                pe.wait_ge(loaded[1][2 + kv], 16)
            w1 = ring[:, 2 + kv, 4096:6144].rearrange("p (j h) -> p j h", j=CMP_LEN)
            for j in range(8 * quarter, 8 * quarter + 8):
                for g in range(G_C):
                    r = slice(64 * g, 64 * g + 64)
                    m = pe.matmul(bank[6 + g][r, kv * 16:kv * 16 + NC_BLK], w1[r, j, :], Xw[r, kv, j, :],
                                  start=(j == 0), stop=(j == CMP_LEN - 1))
            if n == 7:
                m.then_inc(hid_done, 1)

        def jobs1():
            wqc, wkv, wqd, wkd = slot(0, 0, DC, 536), slot(1, 0, DC, 768), slot(2, 0, DC, 512), slot(3, 0, DC, 512)
            wvd = slot(4, 0, DC, 512)
            jobs = []
            for k in range(2):
                cols = [lambda w, c, r=r: w[:, c, r * P:(r + 1) * P] for r in (2 * k, 2 * k + 1)]
                jobs.append((0, False, [], two_T(wqc, cols),
                             [(QTc[:, 2 * k:2 * k + 2, :].rearrange("p a t -> p (a t)"), (P, 0, 512))]))

            def gate_cols(pe, b):
                for t in range(TT):
                    m = mm_group(pe, b[:, t * 24:(t + 1) * 24],
                                 [(xT[:, c, t * P:(t + 1) * P], wqc[:, c, 512:536]) for c in range(DC)])
                return m
            jobs.append((0, True, [], gate_cols, [("gates", None)]))
            for k in range(2):
                cols = [lambda w, c, i=i: w[:, c, i * P:(i + 1) * P] for i in (2 * k, 2 * k + 1)]
                jobs.append((1, False, [], two_T(wkv, cols),
                             [(KTc[:, 2 * k:2 * k + 2, :].rearrange("p a t -> p (a t)"), (P, 0, 512))]))

            def vals(pe, b):
                for t in range(TT):
                    hidden_part(pe, t)
                    m = mm_group(pe, b[:, t * TOK:(t + 1) * TOK],
                                 [(xT[:, c, t * P:(t + 1) * P], wkv[:, c, 512:768]) for c in range(DC)])
                return m
            jobs.append((1, True, [], vals, [(Vs[:, :, :].rearrange("p a t -> p (a t)"), (P, 0, 512))]))
            for blk, w, dst in ((2, wqd, QTf), (3, wkd, KTf)):
                for k in range(2):
                    cols = [lambda w, c, i=i: w[:, c, i * P:(i + 1) * P] for i in (2 * k, 2 * k + 1)]
                    part = {(2, 0): 2, (2, 1): 4, (3, 0): 6}.get((blk, k))
                    jobs.append((blk, (blk, k) == (3, 1), [], two_T(w, cols, part),
                                 [(dst[:, 2 * k:2 * k + 2, :].rearrange("p a t -> p (a t)"), (P, 0, 512))]))
            return jobs, wvd

        JOBS0, N_KEY, N_Q = jobs0()
        JOBS1, w_vd = jobs1()
        JOBS = [JOBS0, JOBS1]
        for t in range(TT):
            JOBS1.append((4, t == 1, [], tokens_out(w_vd, t, 0, 512), [(Vf[:, t, :], (P, 0, 512))]))
        KCMP_JOB = 4
        HID_AFTER = 10

        def freed(l, k):
            if k in (5, 6):
                return y_done[l], k - 2
            if k == 7:
                return sh_down[l], 1
            if l == 1 and k == 2:
                return hid_done, 1
            return proj_done[l], 1 + next(n for n, job in enumerate(JOBS[l]) if job[0] == k and job[1])

        def item(l, n):
            if l == 0:
                if n < 12:
                    r = slice(64 * (n % 2), 64 * (n % 2) + 64)
                    return dict(q=QTd[r, n // 2, :], k=KTd[r, n // 2, :], v=lambda j, n=n: V0[:, j, n * HD:(n + 1) * HD],
                                bias=n, scale=HD ** -0.5, col=(n % 8) * HD, width=HD, stat=n)
                h = n - 12
                return dict(q=QTm[0:QK_A, h, :], k=KTm[0:QK_A, h, :], v=lambda j, n=n: V0[:, j, n * HD:(n + 1) * HD],
                            bias=12, scale=QK_A ** -0.5, col=(n % 8) * HD, width=HD, stat=n)
            if n >= 8:
                b, g, r = n // 8 - 1, n % 2, (n % 8) // 2
                h = g * R_C + r
                rows = slice(64 * g, 64 * g + 64)
                return dict(q=QTc[rows, r, :], k=KTc[rows, 2 + b, :],
                            v=lambda j, b=b, g=g: Vs[:, j, b * P + g * HD:b * P + (g + 1) * HD],
                            bias=h, scale=HD ** -0.5, col=h * HD, width=HD, stat=8 * b + h)
            hd, m = n // 2, n % 2
            rows = slice(64 * m, 64 * m + 64)
            return dict(q=QTf[rows, hd, :], k=KTf[rows, hd, :], v=lambda j, hd=hd: Vf[:, j, hd * P:(hd + 1) * P],
                        bias=8 + hd, scale=HD ** -0.5, col=(hd % 2) * 256 + m * P, width=P, stat=16 + 4 * m + hd)

        ITEMS = [[item(l, n) for n in range(24)] for l in range(DEPTH)]
        GROUP_END = [[8, 16, 24], [4, 8, 16, 24]]

        def group_of(l, n):
            return next(g for g, e in enumerate(GROUP_END[l]) if n < e)

        def o_bank(l, g, t):
            return bank[4 + 2 * (g % 2) + t]

        block = ctx.enter_context(nc.Block())

        @block.sync
        def _(sp):
            def ring_load(l, k, src, n):
                sp.dma_start(ring[:, k % RING, 0:n], src[:, 0:n]).then_inc(loaded[l][k % RING], 16)

            xT_halves = xT_in.rearrange("(c p) t -> p c t", p=P)
            for h, xs, ws in ((0, xT_in_1, w_in_1), (1, x_in, loaded[0][0])):
                cs_, ns = slice(h * DC // 2, (h + 1) * DC // 2), slice(h * MIX_SIZE[0][0] // 2, (h + 1) * MIX_SIZE[0][0] // 2)
                sp.dma_start(xT[:, cs_, :], xT_halves[:, cs_, :]).then_inc(xs, 16)
                sp.dma_start(ring[:, 0, ns], mixw[0, 0][:, ns]).then_inc(ws, 16)
            n = None
            for l in range(DEPTH):
                for k in range(MIX_BLOCKS):
                    if k >= RING:
                        sp.wait_ge(*freed(l, k - RING))
                    elif l and k == 0:
                        sp.wait_ge(down_done[0], n * 4)
                    if l == 0 and k == 0:
                        continue
                    if k < MIX_BLOCKS - 1:
                        ring_load(l, k, mixw[l, k], MIX_SIZE[l][k])
                    else:
                        ring_load(l, k, expw[l, EXPERTS], SLOT_W)
                    if l == 0 and k == RING - 1:
                        sp.dma_start(x_tok[:, :, :], x.rearrange("(t p) d -> p t d", p=P)).then_inc(x_in, 16)
                def step(i, a, known):
                    pair = (2 * a, 2 * a + 1)
                    e = known or [sp.value_load(visit[0:1, 0, bass.ds(i * 4 + j, 1)], min_val=0, max_val=EXPERTS - 1)
                                  for j in pair]
                    for part, arrived, lo, hi in ((0, half_loaded[l], 0, GU // 2), (1, loaded[l], GU // 2, GU),
                                                  (2, dn_loaded[l], GU, SLOT_W)):
                        if not known and part != 1:
                            sp.wait_ge(*((gu_done[l], i * 2 + (a - 1)) if part == 0 else (down_done[l], i * 4 + (2 * a - 2))))
                        for s, j in enumerate(pair):
                            if known and part == 0:
                                sp.wait_ge(*freed(l, MIX_BLOCKS - RING + j))
                            sp.dma_start(ring[:, j, lo:hi],
                                         (expw[l, e[s], :, lo:hi] if known else
                                          expw[l, bass.ds(e[s], 1), :, lo:hi].rearrange("o p n -> (o p) n")))\
                              .then_inc(arrived[j], 16)

                for a in range(2):
                    step(0, a, (2 * a, 2 * a + 1))
                sp.wait_ge(visits_ready[l], 1)
                n = sp.value_load(nquads[0:1, 0:1], min_val=QUADS, max_val=MAX_QUADS)

                with sp.Fori(1, n) as i:
                    for a in range(2):
                        step(i, a, None)
            for t in range(TT):
                for hh in range(2):
                    sp.wait_ge(x_new, halves_of(2 * DEPTH - 1, t) - 1 + hh)
                    cols = slice(hh * 512, (hh + 1) * 512)
                    sp.dma_start(out[t * P:(t + 1) * P, cols], x_tok[:, t, cols]).then_inc(out_done, 16)
            sp.wait_ge(out_done, 16 * 2 * TT)

        @block.gpsimd
        def _(pool):
            pool.wait_ge(loaded[0][1], 16)
            pool.dma_start(cst[:, :], const).then_inc(const_in, 16)
            pool.dma_start(tmp[0:BUCKETS, 0:BIAS_ROWS], tab).then_inc(const_in, 16)
            pool.dma_start(tmp[0:BUCKETS, 32:32 + SPAN], hot).then_inc(const_in, 16)
            pool.dma_start(tmp[0:BIAS_ROWS, 448:448 + SPAN], mask).then_inc(const_in, 16)
            pool.dma_start(sml[:, :], small.to_broadcast([P, N_SMALL])).then_inc(small_in, 16)
            pool.dma_start(posT[:, :, :], pos).then_inc(small_in, 16)
            pool.dma_start(w2s[:, :, :], w2).then_inc(small_in, 16)
            pool.dma_start(rw[:, :, :], routw[0]).then_inc(rw_in, 16)
            pool.wait_ge(bias_sb, 1)
            pool.dma_start(scratch, tmp[0:BIAS_ROWS, 448:448 + SPAN]).then_inc(scratch_out, 16)
            pool.wait_ge(scratch_out, 16)

            def bias_load(l):
                r0, n = BIAS_OF[l]
                src = bass.AP(scratch.tensor, r0 * SPAN, [(1, P), (SPAN, n), (1, TOK)])
                pool.dma_start(biasZ[:, 0:n, :], src).then_inc(bias_in, 16)

            bias_load(0)
            for l in range(DEPTH):
                for half in range(2):
                    k = 2 * l + half
                    if half == 0:
                        pool.wait_ge(scores_done[l], 24)
                    else:
                        pool.wait_ge(x_new, halves_of(k - 1, TT - 1))
                    pool.dma_start(lng[:, :, :].rearrange("p a d -> p (a d)"),
                                   lnp[k:k + 1, :].to_broadcast([P, 2 * D])).then_inc(ln_in, 16)
                    if half == 1:
                        if l == 0:
                            pool.wait_ge(logit_done[0], 1)
                            pool.dma_start(rw[:, :, :], routw[1]).then_inc(rw_in, 16)
                        pool.wait_ge(high_ready, l + 1)
                        pool.tensor_tensor(x_low[:, :, :], x_tok[:, :, :], x_high[:, :, :].bitcast(F32), ALU.subtract)\
                            .then_inc(low_ready, 1)
                        if l == 0:
                            pool.wait_ge(moe_done[0], 4)
                            bias_load(1)

        @block.tensor
        def _(pe):
            def bias_rows():
                pe.wait_ge(const_in, 64)
                pe.matmul(bank[7][0:BIAS_ROWS, 0:SPAN], tmp[0:BUCKETS, 0:BIAS_ROWS], tmp[0:BUCKETS, 32:32 + SPAN],
                          start=True, stop=True).then_inc(bias_ps, 1)

            def ring_in(l, k):
                pe.wait_ge(loaded[l][k % RING], 16 * (k // RING + 1))

            def projections(l, lo, hi):
                for n in range(lo, hi):
                    blk, _, waits, go, _ = JOBS[l][n]
                    if blk is not None:
                        ring_in(l, blk)
                    for s, v in waits:
                        pe.wait_ge(s, v)
                    if n >= 4:
                        pe.wait_ge(proj_taken[l], n - 3)
                    m = go(pe, bank[n % 4])
                    m.then_inc(proj_done[l], 1)

            def scores(l, n):
                if n >= 2:
                    pe.wait_ge(max_ready[l], n - 1)
                for qt, at in ((0, 0), (1, P)):
                    for k in (n, n + 1):
                        it = ITEMS[l][k]
                        m = pe.matmul(bank[k % 3][:, at:at + P * (qt + 1)], it["q"][:, qt * P:(qt + 1) * P],
                                      it["k"][:, 0:P * (qt + 1)], start=True, stop=True)
                        if qt:
                            m.then_inc(scores_done[l], 1)

            def turn_probs(l, n):
                pe.wait_ge(probs_ready[l], n + 1)
                if n >= 1:
                    pe.wait_ge(pt_taken[l], n)
                for j in range(3):
                    m = pe.transpose(bank[3][:, j * P:(j + 1) * P], probs[:, n % 3, j * P:(j + 1) * P], ident)
                m.then_inc(pt_done[l], 1)

            def values(l, n):
                it, g = ITEMS[l][n], group_of(l, n)
                pe.wait_ge(pt_taken[l], n + 1)
                if g >= 2:
                    pe.wait_ge(o_taken[l], g - 1)
                if l == 1 and g == 3:
                    pe.wait_ge(cmp_taken, 1)
                cols = slice(it["col"], it["col"] + it["width"])
                pe.matmul(o_bank(l, g, 0)[:, cols], probsT[:, n % 2, 0:P], it["v"](0), start=True, stop=True)
                pe.matmul(o_bank(l, g, 1)[:, cols], probsT[:, n % 2, P:2 * P], it["v"](0), start=True, stop=False)
                pe.matmul(o_bank(l, g, 1)[:, cols], probsT[:, n % 2, 2 * P:3 * P], it["v"](1), start=False, stop=True)\
                  .then_inc(pv_done[l], 1)

            def attention(l):
                pe.wait_ge(proj_taken[l], len(JOBS[l]))
                if l == 0:
                    pe.wait_ge(key_spread, 1)
                scores(l, 0)
                keep_clock(1, bank[4])
                for n in range(25):
                    if n < 22 and n % 2 == 0:
                        scores(l, n + 2)
                    if n < 24:
                        turn_probs(l, n)
                    if n >= 1:
                        values(l, n - 1)
                    if l == 1 and n in COMPRESSED:
                        COMPRESSED[n]()

            def output_projection(l):
                pe.wait_ge(o_ready[l], 1)
                for k in range(4):
                    for c in (2 * k, 2 * k + 1):
                        for t in range(TT):
                            m = pe.transpose(bank[k][:, (c % 2) * TOK + t * P:(c % 2) * TOK + (t + 1) * P],
                                             o_tok[:, t, c * P:(c + 1) * P], ident)
                    m.then_inc(oT_done[l], 1)
                pe.wait_ge(oT_taken[l], 4)
                ring_in(l, 5)
                ring_in(l, 6)
                for t in range(TT):
                    for hh in range(2):
                        if (t, hh) == (TT - 1, 1):
                            turn_x(2 * l, 0)
                        w = slot(5 + hh, 0, DC, 512)
                        m = mm_group(pe, Ybank[t][hh][:, :], [(oT[:, c, t * P:(t + 1) * P], w[:, c, :]) for c in range(DC)])
                        m.then_inc(y_done[l], 1)

            def turn_x(k, t):
                for q in range(2):
                    pe.wait_ge(x_new, halves_of(k, t) - 1 + q)
                    for cc in range(4):
                        c = 4 * q + cc
                        m = pe.transpose(bank[4 + 2 * t + q][:, cc * P:(cc + 1) * P],
                                         x_tok[:, t, c * P:(c + 1) * P], ident)
                    m.then_inc(xT_done, 1)

            def compressed_kv():
                pe.wait_ge(hid_ready, 1)
                pe.wait_ge(small_in, 48)
                for g in range(G_C):
                    r = slice(64 * g, 64 * g + 64)
                    pe.matmul(bank[6 + g][r, 64:64 + NC_BLK], w2s[r, 0, :], hid[r, 0, 0:NC_BLK], start=True, stop=True)
                    m = pe.matmul(bank[6 + g][:, 128:192], hid4[r, :, :].rearrange("p a c -> p (a c)"), w2s[r, 1, :],
                                  start=True, stop=True)
                m.then_inc(kv_done, 1)

            def compressed_scores():
                pe.wait_ge(kv_taken, 1)
                pe.wait_ge(o_taken[1], 2)
                for t in range(TT):
                    for r in range(R_C):
                        if r % 2 == 0:
                            keep_clock(1, bank[7], 256)
                        for g in range(G_C):
                            rows = slice(64 * g, 64 * g + 64)
                            at = (t * R_C + r) * 16
                            m = pe.matmul(bank[6 + g][:, at:at + NC_BLK], QTc[rows, r, t * P:(t + 1) * P],
                                          kcT[rows, 0:NC_BLK], start=True, stop=True)
                m.then_inc(cmp_s, 1)

            def compressed_turn():
                pe.wait_ge(cmp_p, 1)
                for t in range(TT):
                    for g in range(G_C):
                        m = pe.transpose(bank[6][:, (t * G_C + g) * P:(t * G_C + g + 1) * P],
                                         ec[:, t, 4 * g:4 * g + 4, :].rearrange("p h c -> p (h c)"), ident)
                m.then_inc(cmpT_done, 1)

            def compressed_values():
                pe.wait_ge(cmpT_taken, 1)
                for t in range(TT):
                    for g in range(G_C):
                        m = pe.matmul(bank[6 + t][:, g * 256:(g + 1) * 256], ecT[:, t, g, :],
                                      VBD[:, g, :, :].rearrange("p h d -> p (h d)"), start=True, stop=True)
                m.then_inc(cmp_o, 1)

            COMPRESSED = {10: compressed_scores, 13: compressed_turn, 15: compressed_values}

            def router(l):
                pe.wait_ge(rw_in, 16 * (l + 1))
                for t in range(TT):
                    m = mm_group(pe, bC[:, t * EXPERTS:(t + 1) * EXPERTS],
                                 [(xT[:, c, t * P:(t + 1) * P], rw[:, c, :]) for c in range(DC)])
                m.then_inc(logit_done[l], 1)

            def gate_up_shared(l, lo, hi):
                ring_in(l, 7)
                w = slot(3, 0, DC, 2 * F_EXP)
                for part in range(lo, hi):
                    b, f = (bA, bH)[part // 2], part % 2
                    m = mm_group(pe, b[:, f * TOK:(f + 1) * TOK],
                                 [(w[:, c, part * P:(part + 1) * P], xT[:, c, :]) for c in range(DC)])
                    if f:
                        m.then_inc(sh_gu[l], 1)

            def places(l):
                pe.wait_ge(mask_ready[l], 1)
                tri, ones = c_("tri"), c_("ones")
                mm_group(pe, bC[:, 0:EXPERTS], [(tri, r_mask[:, 0, :])])
                mm_group(pe, bC[:, EXPERTS:2 * EXPERTS], [(ones, r_mask[:, 0, :]), (tri, r_mask[:, 1, :])])
                mm_group(pe, bC[0:EXPERTS, 128:129], [(r_mask[:, t, :], ones[:, 0:1]) for t in range(TT)])\
                    .then_inc(pos_done[l], 1)

            def down_shared(l):
                pe.wait_ge(sh_h[l], 1)
                w = ring[:, 3, GU:SLOT_W].rearrange("p (f n) -> p f n", f=2)
                for t in range(TT):
                    for hh in range(2):
                        for f in range(2):
                            m = pe.matmul(Ybank[t][hh][:, :], hTs[:, f, t * P:(t + 1) * P],
                                          w[:, f, hh * 512:(hh + 1) * 512], start=(f == 0), stop=False,
                                          skip_group_check=True)
                m.then_inc(sh_down[l], 1)

            def keep_clock(n, b, lo=0):
                for _ in range(n):
                    pe.matmul(b[:, lo:512], ident, cst[:, 0:512 - lo], start=True, stop=True)

            def visit_places(l):
                pe.wait_ge(over_ready[l], 1)
                mm_group(pe, bC[0:64, 0:4], [(c_("tri", 64)[:, 0:64], r_ov[0:64, :]), (c_("ones", 64)[:, 0:64], r_ovp[0:64, :])])\
                    .then_inc(idx_done[l], 1)

            def visit_list(l):
                pe.wait_ge(hot_ready[l], 1)
                mm_group(pe, bC[0:1, 0:EXTRA], [(c_("ecode", 64), r_hot[0:64, p, :]) for p in range(3)])
                mm_group(pe, bC[0:1, EXTRA:2 * EXTRA], [(c_("pcode", 64)[:, p:p + 1], r_hot[0:64, p, :]) for p in range(3)])\
                    .then_inc(list_done[l], 1)

            def gather(l, a, pair):
                pe.wait_ge(sel_ready[l], pair + 1)
                for half, b in ((0, bA), (1, bB)):
                    for cc in range(4):
                        c = 4 * half + cc
                        m = mm_group(pe, b[:, cc * P:(cc + 1) * P],
                                     [(part[:, t, c * P:(c + 1) * P], Sel[:, a, t, :])
                                      for part in (x_high, x_low) for t in range(TT)])
                    m.then_inc(gath_done[l], 1)

            def scatter_half(a, t, hh):
                for part in (y_high, y_low):
                    m = pe.matmul(Ybank[t][hh][:, :], selT[:, a, t * P:(t + 1) * P],
                                  part[:, hh * 512:(hh + 1) * 512], start=False, stop=False, skip_group_check=True)
                return m

            def scatter(a):
                for t in range(TT):
                    for hh in range(2):
                        scatter_half(a, t, hh)

            def experts(l):
                pe.nop().then_inc(turn_done[l], 1)
                pe.wait_ge(visits_ready[l], 1)
                last = pe.value_load(nquads[0:1, 1:2], min_val=QUADS - 1, max_val=MAX_QUADS - 1)
                def pair(i, a, more):
                    pe.wait_ge(turn_ready[l], i * 2 + (a + 1))
                    m = mm_group(pe, bC[:, 0:1], [(Selg[:, a, t, :], c_("ones")[:, 0:1]) for t in range(TT)])
                    m.then_inc(gsum_done[l], 1)
                    pe.wait_ge(xgA_ready[l], i * 2 + (a + 1))
                    pe.wait_ge(xgB_ready[l], i * 2 + (a + 1))
                    pe.wait_ge(h_ready[l], i * 2 + (a + 1))
                    for c in range(DC):
                        for s in range(2):
                            if c == 0:
                                pe.wait_ge(half_loaded[l][2 * a + s], i * 16 + 16)
                            if c == DC // 2:
                                pe.wait_ge(loaded[l][2 * a + s], i * 16 + 48)
                            m = pe.matmul(bH[s * SLOTS:(s + 1) * SLOTS, :], xg[:, a, c, s * SLOTS:(s + 1) * SLOTS],
                                          ring[:, 2 * a + s, c * 512:(c + 1) * 512], start=(c == 0), stop=(c == DC - 1))
                    m.then_inc(gu_done[l], 1)
                    pe.wait_ge(y_low_ready[l], i * 4 + (2 * a + 2))
                    if more:
                        gather(l, 1 - a, i * 2 + (a + 1))
                    else:
                        scatter(1 - a)
                    pe.wait_ge(gsum_taken[l], i * 2 + (a + 1))
                    for t in range(TT):
                        pe.transpose(bC[:, t * P:(t + 1) * P], Sel[:, a, t, :].bitcast(F32), ident)
                    pe.wait_ge(h_ready[l], i * 2 + (a + 2))
                    for f in range(2):
                        m = pe.transpose(bC[:, (2 + f) * P:(3 + f) * P], hid_s[:, a, f * P:(f + 1) * P], ident)
                    m.then_inc(turn_done[l], 1)
                    if more:
                        scatter(1 - a)
                    pe.wait_ge(turn_ready[l], i * 2 + (a + 2))
                    if more:
                        pe.wait_ge(xgA_ready[l], i * 2 + (a + 2))
                        pe.wait_ge(xgB_ready[l], i * 2 + (a + 2))
                    for s in range(2):
                        pe.wait_ge(dn_loaded[l][2 * a + s], i * 16 + 16)
                    for hh, b in ((0, bA), (1, bB)):
                        for f in range(2):
                            for s in range(2):
                                at = f * P + s * SLOTS
                                m = pe.matmul(b[s * SLOTS:(s + 1) * SLOTS, :], hT[:, at:at + SLOTS],
                                              ring[:, 2 * a + s, GU + f * D + hh * 512:GU + f * D + (hh + 1) * 512],
                                              start=(f == 0), stop=(f == 1))
                        m.then_inc(down_done[l], 1)

                with pe.Fori(0, last) as i:
                    for a in range(2):
                        pair(i, a, True)
                for a in range(2):
                    pair(last, a, a == 0)
                pe.wait_ge(turn_ready[l], last * 2 + 3)
                for hh in range(2):
                    pe.wait_ge(y_low_ready[l], last * 4 + (5 + hh))
                    for t in range(TT):
                        scatter_half(1, t, hh).then_inc(moe_done[l], 1)

            def first_projection():
                w = slot(0, 0, DC, C_IN)
                for h, xs, ws in ((0, xT_in_1, w_in_1), (1, x_in, loaded[0][0])):
                    pe.wait_ge(xs, 16)
                    pe.wait_ge(ws, 16)
                    for t in range(TT):
                        for c in range(h * DC // 2, (h + 1) * DC // 2):
                            m = pe.matmul(bank[t][:, 0:C_IN], xT[:, c, t * P:(t + 1) * P], w[:, c, :],
                                          start=(c == 0), stop=(c == DC - 1))
                        if h:
                            m.then_inc(proj_done[0], 1)

            pe.wait_ge(warm, 1)
            for _ in range(4):
                pe.matmul(bank[7][:, 0:3 * P], probs[:, 0, 0:P], probs[:, 0, :], start=True, stop=True)
            for l in range(DEPTH):
                if l == 0:
                    first_projection()
                    projections(0, 2, 6)
                    bias_rows()
                    projections(0, 6, len(JOBS0))
                else:
                    projections(1, 0, len(JOBS1))
                    compressed_kv()
                attention(l)
                keep_clock(2, bank[0])
                output_projection(l)
                keep_clock(4, bank[6])
                turn_x(2 * l, 1)
                keep_clock(2, bank[0])
                pe.wait_ge(xT_taken, 4 * (2 * l + 1))
                router(l)
                gate_up_shared(l, 0, 3)
                places(l)
                gate_up_shared(l, 3, 4)
                visit_places(l)
                pe.wait_ge(low_ready, l + 1)
                pe.wait_ge(sh_silu[l], 1)
                gather(l, 0, 0)
                visit_list(l)
                down_shared(l)
                experts(l)
                if l + 1 < DEPTH:
                    for t in range(TT):
                        keep_clock(4, bH)
                        turn_x(2 * l + 1, t)
                    pe.wait_ge(xT_taken, 4 * (2 * l + 2))

        @block.scalar
        def _(act):
            steps = [0]

            def link(ins):
                steps[0] += 1
                ins.then_inc(act_step, 1)
                act.wait_ge(act_step, steps[0])

            def projections(l, lo, hi):
                for n in range(lo, hi):
                    b = bank[n % 4]
                    act.wait_ge(proj_done[l], n + 1)
                    for dst, src in JOBS[l][n][4]:
                        if isinstance(dst, str) and dst == "rope key":
                            m = act.copy(KTm[NOPE:QK_A, 0, :], b[NOPE:QK_A, TOK:2 * TOK])
                        elif isinstance(dst, str):
                            m = act.activation(gates3[:, :, :].rearrange("p t k -> p (t k)"), b[:, 0:48], ACT.Exp, scale=-1.0)
                        else:
                            rows, c0, n_ = src
                            m = act.copy(dst, b[0:rows, c0:c0 + n_])
                    m.then_inc(proj_taken[l], 1)
                    if l == 0 and n == 2:
                        act.wait_ge(rms_var, 1)
                        act.activation(st[:, 0:4], st[:, 0:4], ACT.Sqrt).then_inc(rms_std, 1)

            def attention(l):
                for n in range(25):
                    if l == 1 and n == 14:
                        act.wait_ge(cmp_c, 1)
                        act.activation(ec[:, :, :, 0:NC_BLK], ec[:, :, :, 0:NC_BLK], ACT.Exp, scale=HD ** -0.5)\
                           .then_inc(cmp_e, 1)
                    if n < 24:
                        it = ITEMS[l][n]
                        act.wait_ge(max_ready[l], n + 1)
                        for t, c0, w in ((0, 0, P), (1, P, 2 * P)):
                            m = act.activation(probs[:, n % 3, c0:c0 + w], probs[:, n % 3, c0:c0 + w], ACT.Exp,
                                               scale=-1.0, bias=negmax[:, t, it["stat"]:it["stat"] + 1],
                                               accum_out=rowsum[:, t, it["stat"]:it["stat"] + 1])
                        m.then_inc(probs_ready[l], 1)
                    if n >= 1:
                        act.wait_ge(pt_done[l], n)
                        if n >= 3:
                            act.wait_ge(pv_done[l], n - 2)
                        act.copy(probsT[:, (n - 1) % 2, :], bank[3][:, 0:3 * P]).then_inc(pt_taken[l], 1)
                    if l == 0 and n == 19:
                        act.wait_ge(comb_d, 1)
                        act.activation(wg[:, :, 0:12], wg[:, :, 0:12], ACT.Exp).then_inc(comb_w, 1)
                    if l == 1 and n == 14:
                        act.wait_ge(cmpT_done, 1)
                        act.copy(ecT[:, :, :, :].rearrange("p t g q -> p (t g q)"), bank[6][:, :]).then_inc(cmpT_taken, 1)
                    if l == 1 and n == 19:
                        act.wait_ge(dn_var, 1)
                        act.activation(st[:, 32:40], st[:, 32:40], ACT.Sqrt).then_inc(dn_std, 1)

            def output_projection(l):
                for k in range(4):
                    act.wait_ge(oT_done[l], k + 1)
                    act.copy(oT[:, 2 * k:2 * k + 2, :].rearrange("p a t -> p (a t)"), bank[k][:, :]).then_inc(oT_taken[l], 1)

            def norm(k):
                for t in range(TT):
                    act.wait_ge(ln_var, TT * k + t + 1)
                    act.activation(st[:, 16 + t:17 + t], st[:, 16 + t:17 + t], ACT.Sqrt).then_inc(ln_std, 1)
                    if k == 2 * DEPTH - 1:
                        continue
                    for q in range(2):
                        act.wait_ge(xT_done, 4 * k + 2 * t + q + 1)
                        act.copy(xT[:, 4 * q:4 * q + 4, t * P:(t + 1) * P],
                                 bank[4 + 2 * t + q][:, :].rearrange("p (c s) -> p c s", c=4)).then_inc(xT_taken, 1)

            def experts(l):
                act.wait_ge(gath_done[l], 1)
                act.copy(xg[:, 0, 0:4, :].rearrange("p c s -> p (c s)"), bA[:, :]).then_inc(xgA_ready[l], 1)
                act.wait_ge(visits_ready[l], 1)
                last = act.value_load(nquads[0:1, 1:2], min_val=QUADS - 1, max_val=MAX_QUADS - 1)
                def pair(i, a, more):
                    act.wait_ge(gu_done[l], i * 2 + (a + 1))
                    act.activation(sil[:, a, :], bH[:, 0:F_EXP], ACT.Silu).then_inc(silu_ready[l], 1)
                    if more:
                        act.wait_ge(gath_done[l], i * 4 + (2 * a + 3))
                        act.copy(xg[:, 1 - a, 0:4, :].rearrange("p c s -> p (c s)"), bA[:, :]).then_inc(xgA_ready[l], 1)
                    act.wait_ge(turn_done[l], i * 2 + (a + 2))
                    act.copy(selT[:, a, :], bC[:, 0:TOK])
                    act.copy(hT[:, :], bC[:, TOK:2 * TOK]).then_inc(turn_ready[l], 1)
                    for hh, b in ((0, bA), (1, bB)):
                        act.wait_ge(down_done[l], i * 4 + (2 * a + hh + 1))
                        act.copy(y_high[:, hh * 512:(hh + 1) * 512], b[:, :]).then_inc(y_high_ready[l], 1)

                with act.Fori(0, last) as i:
                    for a in range(2):
                        pair(i, a, True)
                for a in range(2):
                    pair(last, a, a == 0)

            for l in range(DEPTH):
                if l == 0:
                    projections(0, 0, len(JOBS0))
                else:
                    act.wait_ge(lam_s, 1)
                    act.activation(lam[:, 0:2], lam[:, 0:2], ACT.Exp).then_inc(lam_e, 1)
                    projections(1, 0, HID_AFTER)
                    act.wait_ge(hid_z, 1)
                    act.activation(hid_t[:, 2:4, :], hid_t[:, 2:4, :], ACT.Exp, scale=-1.0).then_inc(hid_e, 1)
                    projections(1, HID_AFTER, len(JOBS1))
                attention(l)
                output_projection(l)
                norm(2 * l)
                act.wait_ge(logit_done[l], 1)
                act.activation(r_sc[:, :, :].rearrange("p t e -> p (t e)"), bC[:, 0:2 * EXPERTS], ACT.Exp, scale=-1.0)\
                   .then_inc(esig_ready[l], 1)
                act.copy(x_high[:, :, :], x_tok[:, :, :]).then_inc(high_ready, 1)
                act.wait_ge(sh_gu[l], 1)
                act.activation(sils[:, :, :].rearrange("p f t -> p (f t)"), bA[:, :], ACT.Silu).then_inc(sh_silu[l], 1)
                experts(l)
                norm(2 * l + 1)

        @block.vector
        def _(dve):
            steps = [0]

            def link(ins):
                steps[0] += 1
                ins.then_inc(dve_step, 1)
                dve.wait_ge(dve_step, steps[0])

            TTen, TS, STT = dve.tensor_tensor, dve.tensor_scalar, dve.scalar_tensor_tensor

            def bias_rows():
                dve.wait_ge(bias_ps, 1)
                m = tmp[0:BIAS_ROWS, 448:448 + SPAN]
                STT(m, bank[7][0:BIAS_ROWS, 0:SPAN], 1.0 / HD ** -0.5, m, ALU.mult, ALU.add).then_inc(bias_sb, 1)

            def latent_norms():
                dve.wait_ge(small_in, 48)
                link(dve.memset(cn[:, :, 384:448], 0.0))
                dve.wait_ge(proj_taken[0], 2)
                for t in range(TT):
                    for k, (c0, n) in enumerate(((0, Q_LORA), (Q_LORA, KV_LORA))):
                        link(dve.tensor_tensor_reduce(tmp[:, 0:n], ctok[:, t, c0:c0 + n], ctok[:, t, c0:c0 + n],
                                                      1.0 / n, RMS_EPS, ALU.mult, ALU.add, st[:, 2 * t + k:2 * t + k + 1]))
                dve.nop().then_inc(rms_var, 1)
                dve.wait_ge(rms_std, 1)
                link(dve.reciprocal(st[:, 4:8], st[:, 0:4]))
                for t in range(TT):
                    for k, (c0, n, g) in enumerate(((0, Q_LORA, "qn"), (Q_LORA, KV_LORA, "kvn"))):
                        STT(cn[:, t, c0:c0 + n], ctok[:, t, c0:c0 + n], st[:, 4 + 2 * t + k:5 + 2 * t + k],
                            s_(g), ALU.mult, ALU.mult)
                    cos, sin = (c_(k).rearrange("p (t f) -> p t f", t=TT)[:, t, :] for k in ("cos", "sin"))
                    k1, k2 = ctok[:, t, 384:400], ctok[:, t, 400:416]
                    u = tmp[:, 256 + 64 * t:320 + 64 * t].rearrange("p (a f) -> p a f", a=4)
                    TTen(u[:, 0, :], k1, cos, ALU.mult)
                    TTen(u[:, 1, :], k2, sin, ALU.mult)
                    TTen(u[:, 2, :], k1, sin, ALU.mult)
                    link(TTen(u[:, 3, :], k2, cos, ALU.mult))
                    TTen(cn[:, t, 448:464], u[:, 0, :], u[:, 1, :], ALU.subtract)
                    m = TTen(cn[:, t, 464:480], u[:, 2, :], u[:, 3, :], ALU.add)
                m.then_inc(cn_ready, 1)

            def spread_key():
                dve.wait_ge(proj_taken[0], N_KEY)
                dve.tensor_copy(KTm[NOPE:QK_A, 1:H_A, :], KTm[NOPE:QK_A, 0:1, :].to_broadcast([ROPE, H_A - 1, TOK]))\
                   .then_inc(key_spread, 1)

            def rotate_queries():
                dve.wait_ge(scratch_out, 16)
                u = tmp[:, 0:768].rearrange("p (a h f) -> p a h f", a=4, h=H_A)
                for t in range(TT):
                    dve.wait_ge(proj_taken[0], N_Q - 3 * (1 - t))
                    cos, sin = (c_(k).rearrange("p (t f) -> p t f", t=TT)[:, t:t + 1, :].to_broadcast([P, H_A, HALF])
                                for k in ("cos", "sin"))
                    q = q_tok[:, t, :].rearrange("p (h e) -> p h e", h=H_A)
                    q1, q2 = q[:, :, NOPE:NOPE + HALF], q[:, :, NOPE + HALF:QK_A]
                    TTen(u[:, 0], q1, cos, ALU.mult)
                    TTen(u[:, 1], q2, sin, ALU.mult)
                    TTen(u[:, 2], q1, sin, ALU.mult)
                    link(TTen(u[:, 3], q2, cos, ALU.mult))
                    link(TTen(q1, u[:, 0], u[:, 1], ALU.subtract))
                    link(TTen(q2, u[:, 2], u[:, 3], ALU.add))
                    dve.nop().then_inc(q_roped, 1)

            def attention(l, first=0):
                dve.wait_ge(bias_in, 16 * (l + 1))
                for n in range(26):
                    if n < 24:
                        it, b = ITEMS[l][n], bank[n % 3]
                        dve.wait_ge(scores_done[l], n + 1)
                        if n >= 3:
                            dve.wait_ge(pt_done[l], n - 2)
                        for t, c0, w in ((0, 0, P), (1, P, 2 * P)):
                            m = dve.tensor_tensor_reduce(probs[:, n % 3, c0:c0 + w], b[:, c0:c0 + w],
                                                         biasZ[:, it["bias"], 0:w][:, ::-1], -it["scale"], 3e38,
                                                         ALU.add, ALU.min, negmax[:, t, it["stat"]:it["stat"] + 1])
                        m.then_inc(max_ready[l], 1)
                    for stage in BETWEEN[l].get(n, ()):
                        stage()

            def inverse_sums(a, b):
                link(dve.reciprocal(rinv[:, :, a:b], rowsum[:, :, a:b]))

            def heads(ap, n):
                return ap.rearrange("p (h d) -> p h d", h=n)

            def spread(ap, n, w=HD):
                return ap.unsqueeze(2).to_broadcast([P, n, w])

            def take_dilated01():
                dve.wait_ge(pv_done[0], GROUP_END[0][0])
                for t in range(TT):
                    m = dve.tensor_copy(ob[:, t, :], o_bank(0, 0, t)[:, :])
                m.then_inc(o_taken[0], 1)

            def group_maxima():
                nm = negmax
                link(TTen(wg[:, :, 12:16], nm[:, :, 0:4], nm[:, :, 4:8], ALU.min))
                link(TTen(wg[:, :, 12:16], wg[:, :, 12:16], nm[:, :, 8:12], ALU.min))
                for k in range(3):
                    m = TTen(wg[:, :, 4 * k:4 * k + 4], wg[:, :, 12:16], nm[:, :, 4 * k:4 * k + 4], ALU.subtract)
                m.then_inc(comb_d, 1)

            def take_mla0():
                dve.wait_ge(pv_done[0], GROUP_END[0][1])
                inverse_sums(12, 16)
                for t in range(TT):
                    TTen(heads(o_tok[:, t, 0:256], 4), heads(o_bank(0, 1, t)[:, 256:512], 4),
                         spread(rinv[:, t, 12:16], 4), ALU.mult)

            def group_weights():
                dve.wait_ge(comb_w, 1)
                u = tmp[:, 0:24].rearrange("p (t k) -> p t k", t=TT)
                link(TTen(u, wg[:, :, 0:12], rowsum[:, :, 0:12], ALU.mult))
                link(TTen(wg[:, :, 12:16], u[:, :, 0:4], u[:, :, 4:8], ALU.add))
                link(TTen(wg[:, :, 12:16], wg[:, :, 12:16], u[:, :, 8:12], ALU.add))
                link(dve.reciprocal(wg[:, :, 16:20], wg[:, :, 12:16]))
                for k in range(3):
                    m = TTen(rinv[:, :, 4 * k:4 * k + 4], wg[:, :, 4 * k:4 * k + 4], wg[:, :, 16:20], ALU.mult)
                link(m)

            def combine(t):
                o = heads(o_tok[:, t, 768:1024], 4)

                def weigh():
                    TTen(o, heads(o_bank(0, 1, t)[:, 0:256], 4), spread(rinv[:, t, 8:12], 4), ALU.mult)
                    link(TTen(heads(ob[:, t, :], 8), heads(ob[:, t, :], 8), spread(rinv[:, t, 0:8], 8), ALU.mult))

                def add():
                    link(TTen(o, o, heads(ob[:, t, 0:256], 4), ALU.add))
                    link(TTen(o, o, heads(ob[:, t, 256:512], 4), ALU.add))
                return weigh, add

            def take_mla1():
                dve.wait_ge(pv_done[0], GROUP_END[0][2])
                inverse_sums(16, 24)
                for t in range(TT):
                    m = TTen(heads(o_tok[:, t, 256:768], 8), heads(o_bank(0, 2, t)[:, :], 8),
                             spread(rinv[:, t, 16:24], 8), ALU.mult)
                m.then_inc(o_ready[0], 1)

            def take_differential(g, t):
                def go():
                    k = 2 * g
                    if t == 0:
                        dve.wait_ge(pv_done[1], GROUP_END[1][g])
                        inverse_sums(16 + k, 18 + k)
                        inverse_sums(20 + k, 22 + k)
                        link(TS(rinv[:, :, 20 + k:22 + k], rinv[:, :, 20 + k:22 + k], lam[:, 2:3], None, ALU.mult))
                    b = o_bank(1, g, t)[:, :].rearrange("p (h m d) -> p h m d", h=2, m=2)
                    o = heads(o_tok[:, t, 512 + k * P:512 + (k + 2) * P], 2)
                    u = heads(tmp[:, 0:256], 2)
                    TTen(o, b[:, :, 0, :], spread(rinv[:, t, 16 + k:18 + k], 2, P), ALU.mult)
                    link(TTen(u, b[:, :, 1, :], spread(rinv[:, t, 20 + k:22 + k], 2, P), ALU.mult))
                    link(TTen(o, o, u, ALU.add))
                    if t == TT - 1:
                        dve.nop().then_inc(o_taken[1], 1)
                return go

            def head_squares(t):
                def go():
                    od = o_tok[:, t, 512:1024]
                    link(TTen(tmp[:, 0:512], od, od, ALU.mult))
                    link(dve.tensor_reduce(st[:, 32 + 4 * t:36 + 4 * t], heads(tmp[:, 0:512], 4), X, ALU.add))
                    if t == TT - 1:
                        TS(st[:, 32:40], st[:, 32:40], 1.0 / P, RMS_EPS, ALU.mult, ALU.add).then_inc(dn_var, 1)
                return go

            def head_norm(t):
                def go():
                    if t == 0:
                        dve.wait_ge(dn_std, 1)
                        link(dve.reciprocal(st[:, 40:48], st[:, 32:40]))
                        link(TS(st[:, 40:48], st[:, 40:48], 1.0 - LAM_INIT, None, ALU.mult))
                    od = heads(o_tok[:, t, 512:1024], 4)
                    link(TTen(od, od, spread(st[:, 40 + 4 * t:44 + 4 * t], 4, P), ALU.mult))
                    link(TTen(od, od, s_("dn").unsqueeze(1).to_broadcast([P, 4, P]), ALU.mult))
                return go

            def take_branch(g, t):
                def go():
                    a, b = 8 * (g - 2), 8 * (g - 2) + 8
                    if t == 0:
                        dve.wait_ge(pv_done[1], GROUP_END[1][g])
                        inverse_sums(a, b)
                        link(TTen(rinv[:, :, a:b], rinv[:, :, a:b], gates3[:, :, a + 8:b + 8], ALU.mult))
                    link(TTen(heads(tmp[:, 0:512], 8), heads(o_bank(1, g, t)[:, :], 8), spread(rinv[:, t, a:b], 8), ALU.mult))
                    link(TTen(o_tok[:, t, 0:512], o_tok[:, t, 0:512], tmp[:, 0:512], ALU.add))
                    if g == 3 and t == TT - 1:
                        dve.nop().then_inc(o_ready[1], 1)
                return go

            def norm(k, y_sem, place):
                dve.wait_ge(x_in, 32)
                for t in range(TT):
                    mean, std = st[:, 20 + 2 * t:21 + 2 * t], st[:, 16 + t:17 + t]
                    for hh in range(2):
                        dve.wait_ge(y_sem, place(t, hh))
                        cols = slice(hh * 512, (hh + 1) * 512)
                        link(STT(z[:, t, cols], x_tok[:, t, cols], ALPHA, Ybank[t][hh][:, :], ALU.mult, ALU.add))
                        link(dve.bn_stats(st[:, 48 + 6 * hh:54 + 6 * hh], z[:, t, cols]))
                    link(dve.bn_aggr(st[:, 20 + 2 * t:22 + 2 * t], st[:, 48:60]))
                    TS(std, st[:, 21 + 2 * t:22 + 2 * t], LN_EPS, None, ALU.add).then_inc(ln_var, 1)
                    dve.wait_ge(ln_in, 16 * (k + 1))
                    STT(z[:, t, :], z[:, t, :], mean, lng[:, 0, :], ALU.subtract, ALU.mult)
                    dve.wait_ge(ln_std, TT * k + t + 1)
                    link(dve.reciprocal(st[:, 18 + t:19 + t], std))
                    for hh in range(2):
                        cols = slice(hh * 512, (hh + 1) * 512)
                        STT(x_tok[:, t, cols], z[:, t, cols], st[:, 18 + t:19 + t], lng[:, 1, cols], ALU.mult, ALU.add)\
                            .then_inc(x_new, 1)

            def router(l):
                dve.memset(y_high[:, :].bitcast(F32), 0.0)
                dve.memset(y_low[:, :].bitcast(F32), 0.0).then_inc(y_low_ready[l], 2)
                dve.memset(selT[:, 1, :].bitcast(F32), 0.0).then_inc(turn_ready[l], 1)
                dve.nop().then_inc(h_ready[l], 1)
                dve.wait_ge(esig_ready[l], 1)
                link(TS(r_sc, r_sc, 1.0, None, ALU.add))
                link(dve.reciprocal(r_sc, r_sc))
                rb = s_("rb").rearrange("p (l e) -> p l e", l=DEPTH)[:, l:l + 1, :].to_broadcast([P, TT, EXPERTS])
                link(TTen(r_sel, r_sc, rb, ALU.add))
                for t in range(TT):
                    for g in range(GROUPS):
                        m = dve.max(r_m8[:, t, 8 * g:8 * g + 8], r_sel[:, t, 8 * g:8 * g + 8])
                link(m)
                best = r_m8.rearrange("p t (g k) -> p t g k", g=GROUPS)
                link(TTen(r_gs, best[:, :, :, 0], best[:, :, :, 1], ALU.add))
                for t in range(TT):
                    other = r_gs[:, t:t + 1, :].to_broadcast([P, GROUPS, GROUPS])
                    own = r_gs[:, t, :].unsqueeze(2).to_broadcast([P, GROUPS, GROUPS])
                    TTen(r_gt, other, own, ALU.is_gt)
                    link(TTen(r_eq, other, own, ALU.is_equal))
                    link(TTen(r_eq, r_eq, c_("gtri").rearrange("p (a b) -> p a b", a=GROUPS), ALU.mult))
                    link(TTen(r_gt, r_gt, r_eq, ALU.add))
                    link(dve.tensor_reduce(r_rank[:, t, :], r_gt, X, ALU.add))
                link(TS(r_gm, r_rank, TOP_GROUPS - 0.5, None, ALU.is_lt))
                link(TS(r_rank, r_gm, 1.0, -NEG, ALU.subtract, ALU.mult))
                for t in range(TT):
                    sel, selm = (heads(r[:, t, :], GROUPS) for r in (r_sel, r_selm))
                    link(TTen(selm, sel, spread(r_gm[:, t, :], GROUPS, 8), ALU.mult))
                    link(TTen(selm, selm, spread(r_rank[:, t, :], GROUPS, 8), ALU.add))
                    link(dve.max(r_top[:, t, :], r_selm[:, t, :]))
                    link(dve.match_replace(r_rep[:, t, :], r_top[:, t, :], r_selm[:, t, :], -3e38))
                link(TS(r_mask, r_rep, -2e38, None, ALU.is_lt))
                dve.nop().then_inc(mask_ready[l], 1)
                link(TTen(r_gate, r_sc, r_mask, ALU.mult))
                link(dve.tensor_reduce(r_den, r_gate, X, ALU.add))
                link(dve.reciprocal(r_den, r_den))
                link(TS(r_den, r_den, ROUTED_SCALE, None, ALU.mult))
                link(TTen(r_gate, r_gate, r_den.unsqueeze(2).to_broadcast([P, TT, EXPERTS]), ALU.mult))
                dve.wait_ge(pos_done[l], 1)
                link(STT(r_pos, bC[:, 0:2 * EXPERTS].rearrange("p (t e) -> p t e", t=TT), 1.0, r_mask, ALU.add, ALU.mult))
                link(TS(r_pos, r_pos, -1.0, None, ALU.add))
                select(l, 0, None)
                dve.memset(r_ov[0:64, 3:4], 0.0)
                dve.memset(r_ovp[0:64, 0:1], 0.0)
                link(TTen(r_ov[0:64, 0:3], c_("thr", 64), bC[0:64, 128:129].to_broadcast([64, 3]), ALU.is_lt))
                link(dve.tensor_copy(r_ovp[0:64, 1:2], r_ov[0:64, 0:1]))
                link(TTen(r_ovp[0:64, 2:3], r_ovp[0:64, 1:2], r_ov[0:64, 1:2], ALU.add))
                link(TTen(r_ovp[0:64, 3:4], r_ovp[0:64, 2:3], r_ov[0:64, 2:3], ALU.add))
                dve.nop().then_inc(over_ready[l], 1)

            def shared_hidden(l):
                dve.wait_ge(sh_silu[l], 1)
                dve.wait_ge(sh_gu[l], 2)
                TTen(hTs[:, :, :].rearrange("p f t -> p (f t)"), sils[:, :, :].rearrange("p f t -> p (f t)"), bH[:, :],
                     ALU.mult).then_inc(sh_h[l], 1)

            def visit_list(l):
                dve.wait_ge(idx_done[l], 1)
                link(dve.tensor_copy(r_idx[0:64, :], bC[0:64, 0:4]))
                for p in range(3):
                    m = TS(r_hot[0:64, p, :], c_("kiota", 64), r_idx[0:64, p:p + 1], r_ov[0:64, p:p + 1],
                           ALU.is_equal, ALU.mult)
                m.then_inc(hot_ready[l], 1)
                shared_hidden(l)
                link(dve.memset(visit_f[0:1, 0, :], 0.0))
                link(dve.memset(visit_f[0:1, 1, :], float(SLOTS * PASSES)))
                dve.memset(visit_f[0:1, 1, 0:EXPERTS], 0.0)
                dve.tensor_copy(visit_f[0:1, 0, 0:EXPERTS], c_("base", 1))
                link(TS(r_q[0:1, :], c_("quad4", 1), r_idx[0:1, 3:4], None, ALU.is_lt))
                link(dve.tensor_reduce(r_den[0:1, 0:1], r_q[0:1, :], X, ALU.add))
                link(TS(r_den[0:1, 0:1], r_den[0:1, 0:1], float(QUADS), None, ALU.add))
                dve.tensor_copy(nquads[0:1, 0:1], r_den[0:1, 0:1])
                link(TS(r_den[0:1, 1:2], r_den[0:1, 0:1], -1.0, None, ALU.add))
                dve.tensor_copy(nquads[0:1, 1:2], r_den[0:1, 1:2])
                dve.wait_ge(gath_done[l], 2)
                dve.tensor_copy(xg[:, 0, 4:8, :].rearrange("p c s -> p (c s)"), bB[:, :]).then_inc(xgB_ready[l], 1)
                dve.wait_ge(list_done[l], 1)
                link(dve.tensor_copy(r_list[0:1, :, :].rearrange("p a k -> p (a k)"), bC[0:1, 0:2 * EXTRA]))
                link(TS(r_hot[0:1, 0, :], r_list[0:1, 1, :], 0.0, float(SLOTS * PASSES), ALU.is_equal, ALU.mult))
                TTen(visit_f[0:1, 1, EXPERTS:EXPERTS + EXTRA], r_list[0:1, 1, :], r_hot[0:1, 0, :], ALU.add)
                link(dve.tensor_copy(visit_f[0:1, 0, EXPERTS:EXPERTS + EXTRA], r_list[0:1, 0, :]))
                link(dve.tensor_copy(visit[0:1, :, :], visit_f[0:1, :, :]))
                dve.nop().then_inc(visits_ready[l], 1)

            def select(l, a, first):
                for s in range(2):
                    if first is None:
                        e, off = s, 0
                    else:
                        at = first + (2 * a + s)
                        e = dve.value_load(visit[0:1, 0, bass.ds(at, 1)], min_val=0, max_val=EXPERTS - 1)
                        off = dve.value_load(visit[0:1, 1, bass.ds(at, 1)], min_val=0, max_val=SLOTS * PASSES)
                    cols = slice(s * SLOTS, (s + 1) * SLOTS)
                    base = CONST["iota"][0]
                    for t in range(TT):
                        place = r_pos[:, t, bass.ds(e, 1)]
                        slot_no = cst[:, bass.ds(off + base, SLOTS)]
                        TS(Sel[:, a, t, cols], slot_no, place, None, ALU.is_equal)
                        m = TS(Selg[:, a, t, cols], slot_no, place, r_gate[:, t, bass.ds(e, 1)], ALU.is_equal, ALU.mult)
                m.then_inc(sel_ready[l], 1)

            def experts(l):
                last = dve.value_load(nquads[0:1, 1:2], min_val=QUADS - 1, max_val=MAX_QUADS - 1)
                def pair(i, a, more):
                    dve.wait_ge(gsum_done[l], i * 2 + (a + 1))
                    dve.tensor_copy(slot_gate[:, a:a + 1], bC[:, 0:1]).then_inc(gsum_taken[l], 1)
                    if more:
                        dve.wait_ge(gath_done[l], i * 4 + (2 * a + 2))
                        dve.wait_ge(turn_done[l], i * 2 + (a + 1))
                        select(l, 1 - a, i * 4 + (2 + 2) * a)
                    dve.wait_ge(silu_ready[l], i * 2 + (a + 1))
                    dve.wait_ge(gsum_taken[l], i * 2 + (a + 1))
                    STT(hid_s[:, a, :], sil[:, a, :], slot_gate[:, a:a + 1], bH[:, F_EXP:2 * F_EXP],
                        ALU.mult, ALU.mult).then_inc(h_ready[l], 1)
                    if more:
                        dve.wait_ge(gath_done[l], i * 4 + (2 * a + 4))
                        dve.tensor_copy(xg[:, 1 - a, 4:8, :].rearrange("p c s -> p (c s)"), bB[:, :])\
                           .then_inc(xgB_ready[l], 1)
                    for hh, b in ((0, bA), (1, bB)):
                        cols = slice(hh * 512, (hh + 1) * 512)
                        dve.wait_ge(y_high_ready[l], i * 4 + (2 * a + hh + 1))
                        TTen(y_low[:, cols], b[:, :], y_high[:, cols].bitcast(F32), ALU.subtract)\
                            .then_inc(y_low_ready[l], 1)

                with dve.Fori(0, last) as i:
                    for a in range(2):
                        pair(i, a, True)
                for a in range(2):
                    pair(last, a, a == 0)

            def compress():
                dve.wait_ge(proj_taken[1], KCMP_JOB)
                for kv in range(2):
                    src = KTc[:, kv, :]
                    win = bass.AP(src.tensor, src.offset, [src.ap[0], (1, CMP_LEN), (CMP_STRIDE, NC_BLK)])
                    m = TTen(Xw[:, kv, :, :], win, posT[:, kv, :].unsqueeze(2).to_broadcast([P, CMP_LEN, NC_BLK]), ALU.add)
                m.then_inc(win_ready, 1)
                dve.memset(hid4[:, :, :], 0.0)
                dve.memset(VBD[:, :, :, :], 0.0)
                link(dve.memset(ec[:, :, :, :], 0.0))
                dve.wait_ge(hid_done, 1)
                for g in range(G_C):
                    r = slice(64 * g, 64 * g + 64)
                    m = dve.tensor_copy(hid_t[r, 0:2, 0:NC_BLK],
                                        bank[6 + g][r, 0:32].rearrange("p (a c) -> p a c", a=2)[:, :, 0:NC_BLK])
                link(m)
                h, u = hid_t[:, 0:2, 0:NC_BLK], hid_t[:, 2:4, 0:NC_BLK]
                link(TTen(u, h, h, ALU.mult))
                link(TS(u, u, 0.044715, 1.0, ALU.mult, ALU.add))
                link(TTen(u, u, h, ALU.mult))
                link(TS(u, u, 2.0 * math.sqrt(2.0 / math.pi), None, ALU.mult))
                dve.nop().then_inc(hid_z, 1)
                dve.wait_ge(hid_e, 1)
                link(TS(u, u, 1.0, None, ALU.add))
                link(dve.reciprocal(u, u))
                link(TTen(hid[:, :, 0:NC_BLK], h, u, ALU.mult))
                link(dve.tensor_copy(hid4[:, :, 0:NC_BLK], hid[:, 1:2, 0:NC_BLK].to_broadcast([P, 4, NC_BLK])))
                dve.nop().then_inc(hid_ready, 1)
                dve.wait_ge(kv_done, 1)
                for g in range(G_C):
                    r = slice(64 * g, 64 * g + 64)
                    dve.tensor_copy(kcT[r, 0:NC_BLK], bank[6 + g][r, 64:64 + NC_BLK])
                    for h4 in range(4):
                        q = slice(32 * h4, 32 * h4 + 32)
                        m = dve.tensor_copy(VBD[q, g, h4, :], bank[6 + g][q, 128:192])
                m.then_inc(kv_taken, 1)

            def gates_and_lambda():
                l1 = s_("lam").rearrange("p (a d) -> p a d", a=4)
                dve.tensor_tensor_reduce(tmp[:, 0:64], l1[:, 0, :], l1[:, 1, :], 1.0, 0.0, ALU.mult, ALU.add, lam[:, 0:1])
                dve.tensor_tensor_reduce(tmp[:, 64:128], l1[:, 2, :], l1[:, 3, :], 1.0, 0.0, ALU.mult, ALU.add,
                                         lam[:, 1:2]).then_inc(lam_s, 1)
                dve.wait_ge(lam_e, 1)
                link(TTen(lam[:, 2:3], lam[:, 1:2], lam[:, 0:1], ALU.subtract))
                link(TS(lam[:, 2:3], lam[:, 2:3], -LAM_INIT, None, ALU.add))
                dve.wait_ge(proj_taken[1], 3)
                link(TS(gates3[:, :, :], gates3[:, :, :], 1.0, None, ALU.add))
                link(dve.reciprocal(gates3[:, :, :], gates3[:, :, :]))

            def compressed_maxima():
                dve.wait_ge(cmp_s, 1)
                seen = [7, NC_BLK]
                link(dve.memset(ec[:, 0, :, seen[0]:NC_BLK], NEG))
                for t in range(TT):
                    first = P * t + P - 1 - (CMP_LEN - 1)
                    for g in range(G_C):
                        n = seen[t]
                        zz = biasZ[:, 4 * g:4 * g + 4, :]
                        bias = bass.AP(zz.tensor, zz.offset + first, [zz.ap[0], (TOK, 4), (-CMP_STRIDE, n)])
                        s = bank[6 + g][:, t * 64:(t + 1) * 64].rearrange("p (r c) -> p r c", r=R_C)[:, :, 0:n]
                        m = TTen(ec[:, t, 4 * g:4 * g + 4, 0:n], s, bias, ALU.add)
                link(m)
                e = ec[:, :, :, 0:NC_BLK].rearrange("p t h c -> p (t h) c")
                cmax = cs[:, 0, :]
                link(dve.tensor_reduce(cmax, e, X, ALU.max))
                link(TTen(e, e, cmax.unsqueeze(2).to_broadcast([P, 16, NC_BLK]), ALU.subtract))
                dve.nop().then_inc(cmp_c, 1)

            def compressed_probs():
                e, csum = ec[:, :, :, 0:NC_BLK].rearrange("p t h c -> p (t h) c"), cs[:, 1, :]
                dve.wait_ge(cmp_e, 1)
                for t in range(TT):
                    v = c_("valid").rearrange("p (t c) -> p t c", t=TT)[:, t:t + 1, 0:NC_BLK].to_broadcast([P, H_C, NC_BLK])
                    m = TTen(ec[:, t, :, 0:NC_BLK], ec[:, t, :, 0:NC_BLK], v, ALU.mult)
                link(m)
                dve.nop().then_inc(cmp_p, 1)
                link(dve.tensor_reduce(csum, e, X, ALU.add))
                link(TS(csum, csum, 1e-30, None, ALU.max))
                link(dve.reciprocal(csum, csum))
                link(TTen(csum.rearrange("p (t h) -> p t h", t=TT), csum.rearrange("p (t h) -> p t h", t=TT),
                          gates3[:, :, 0:8], ALU.mult))

            def take_compressed():
                dve.wait_ge(cmp_o, 1)
                for t in range(TT):
                    m = TTen(heads(o_tok[:, t, 0:512], 8), heads(bank[6 + t][:, :], 8),
                             spread(cs[:, 1, 8 * t:8 * t + 8], 8), ALU.mult)
                link(m)
                dve.nop().then_inc(cmp_taken, 1)

            (weigh0, add0), (weigh1, add1) = combine(0), combine(1)
            BETWEEN = [{11: [take_dilated01], 17: [group_maxima], 18: [take_mla0], 19: [group_weights], 20: [weigh0],
                        21: [add0], 22: [weigh1], 23: [add1], 25: [take_mla1]},
                       {7: [take_differential(0, 0)], 8: [take_differential(0, 1)],
                        11: [take_differential(1, 0), take_differential(1, 1)],
                        13: [compressed_maxima], 14: [compressed_probs], 16: [head_squares(0)], 17: [take_compressed],
                        18: [head_squares(1)], 19: [take_branch(2, 0)], 20: [take_branch(2, 1)], 21: [head_norm(0)],
                        22: [head_norm(1)], 25: [take_branch(3, 0), take_branch(3, 1)]}]

            for l in range(DEPTH):
                if l == 0:
                    dve.memset(probs[:, 0, :], 0.0).then_inc(warm, 1)
                    bias_rows()
                    latent_norms()
                    spread_key()
                    rotate_queries()
                else:
                    gates_and_lambda()
                    compress()
                attention(l)
                norm(2 * l, y_done[l], lambda t, hh: 2 * t + hh + 1)
                router(l)
                visit_list(l)
                experts(l)
                norm(2 * l + 1, moe_done[l], lambda t, hh: TT * hh + t + 1)


def _constants():
    c = np.zeros((P, N_CONST), np.float32)

    def put(name, a):
        at, n = CONST[name]
        a = np.asarray(a, np.float32)
        c[:a.shape[0], at:at + n] = a.reshape(a.shape[0], n)

    p = np.arange(P)
    put("ident", np.eye(P))
    put("tri", p[:, None] < p[None, :])
    put("ones", np.ones((P, P)))
    put("iota", np.tile(np.arange(SLOTS * (PASSES + 1)), (P, 1)))
    freqs = np.float32(10000.0) ** (-np.arange(HALF, dtype=np.float32) / np.float32(HALF))
    ang = (np.arange(TOK, dtype=np.float32)[:, None] * freqs).astype(np.float32)
    for name, f in (("cos", np.cos), ("sin", np.sin)):
        put(name, f(ang).reshape(TT, P, HALF).transpose(1, 0, 2))
    tok = np.arange(TOK).reshape(TT, P).T
    put("valid", (tok[:, :, None] - (np.arange(16) * CMP_STRIDE + CMP_LEN - 1)) >= 0)
    g = np.arange(GROUPS)
    put("gtri", np.tile((g[None, :] < g[:, None]).reshape(1, -1), (P, 1)))
    put("kiota", np.tile(np.arange(EXTRA), (64, 1)))
    put("thr", np.tile(SLOTS * np.arange(1, PASSES), (64, 1)))
    put("ecode", np.arange(EXPERTS)[:, None])
    put("pcode", np.tile(SLOTS * np.arange(1, PASSES), (64, 1)))
    put("base", np.arange(EXPERTS)[None, :])
    put("quad4", 4 * np.arange(8)[None, :])

    d = np.arange(SPAN) - (P - 1)
    n = np.maximum(d, 0)
    ratio = (np.log(np.maximum(n, 1).astype(np.float32) / np.float32(16)) / np.float32(math.log(2048 / 16))).astype(np.float32)
    large = 16 + (ratio * np.float32(16)).astype(np.int32)
    bucket = np.where(n < 16, n, np.minimum(large, BUCKETS - 1))
    hot = (bucket[None, :] == np.arange(BUCKETS)[:, None]).astype(np.float32)
    mask = np.where(d < 0, NEG, 0.0)[None, :].repeat(BIAS_ROWS, 0)
    mask[0:4] = np.where((d < 0) | (d > 128), NEG, 0.0)
    mask[4:8] = np.where((d < 0) | (d % 4 != 0), NEG, 0.0)
    mask[8:12] = np.where((d < 0) | (d % 16 != 0), NEG, 0.0)
    return c, hot, mask.astype(np.float32)


def _chunks(w):
    r, n = w.shape
    return w.reshape(r // P, P, n).transpose(1, 0, 2).reshape(P, -1)


def _lay_out(a):
    f = np.float32
    mix = np.zeros((DEPTH, MIX_BLOCKS - 1, P, SLOT_W), f)

    def put(l, k, *parts):
        at = 0
        for p in parts:
            mix[l, k, :, at:at + p.shape[1]] = p
            at += p.shape[1]

    w = a["ab_w_in"][0]
    put(0, 0, _chunks(w[:, :C_IN]))
    for k in range(3):
        put(0, 1 + k, _chunks(w[:, C_IN + 768 * k:C_IN + 768 * (k + 1)]))
    put(0, 4, _chunks(a["mla_w_uq"][0]), a["mla_w_ukv"][0])
    w = a["cd_w_in"][0]
    qc = w[:, :512].reshape(D, G_C, R_C, HD).transpose(0, 2, 1, 3).reshape(D, 512)
    put(1, 0, _chunks(np.concatenate([qc, w[:, 1280:1304]], 1)))
    order = [0, 1, 2, 4, 3, 5]
    put(1, 1, _chunks(np.concatenate([w[:, 512 + P * i:512 + P * (i + 1)] for i in order], 1)))
    for k in range(2):
        w1 = a[("nsa_cmp_k_w1", "nsa_cmp_v_w1")[k]][0].reshape(CMP_LEN, HD, 64).transpose(1, 0, 2).reshape(HD, -1)
        put(1, 2 + k, _chunks(w[:, 1304 + 512 * k:1304 + 512 * (k + 1)]), np.concatenate([w1, w1], 0))
    put(1, 4, _chunks(w[:, 2328:2840]))
    for l, name in enumerate(("ab_w_out", "cd_w_out")):
        for hh in range(2):
            put(l, 5 + hh, _chunks(a[name][0][:, hh * 512:(hh + 1) * 512]))
    exp = np.empty((DEPTH, EXPERTS + 1, P, SLOT_W), f)
    gu = exp[..., :GU].reshape(DEPTH, EXPERTS + 1, P, DC, 2, F_EXP)
    dn = exp[..., GU:].reshape(DEPTH, EXPERTS + 1, P, 2, D)
    for l in range(DEPTH):
        for k, (r, s) in enumerate((("exp_w_gate", "sh_w_gate"), ("exp_w_up", "sh_w_up"))):
            gu[l, :EXPERTS, :, :, k] = a[r][l].reshape(EXPERTS, DC, P, F_EXP).transpose(0, 2, 1, 3)
            gu[l, EXPERTS, :, :, k] = a[s][l].reshape(DC, P, F_EXP).transpose(1, 0, 2)
        dn[l, :EXPERTS] = a["exp_w_down"][l].reshape(EXPERTS, 2, P, D).transpose(0, 2, 1, 3)
        dn[l, EXPERTS] = a["sh_w_down"][l].reshape(2, P, D).transpose(1, 0, 2)
    exp[..., :GU] = gu.reshape(DEPTH, EXPERTS + 1, P, GU)
    exp[..., GU:] = dn.reshape(DEPTH, EXPERTS + 1, P, 2 * D)
    const, hot, mask = _constants()
    x = a["x"][0]
    rel = a["rel_bias"]
    small = np.concatenate([a["mla_q_norm"][0], a["mla_kv_norm"][0], a["diff_norm"][0]]
                           + [a[f"diff_lambda_{n}"][0] for n in ("q1", "k1", "q2", "k2")]
                           + [a["router_b"].reshape(-1)])[None, :]
    return {
        "x": x, "xT_in": np.ascontiguousarray(x.T), "mixw": mix, "expw": exp, "const": const,
        "tab": np.concatenate([rel[:, :12], np.zeros((BUCKETS, 1), f), rel[:, 12:]], 1),
        "hot": hot, "mask": mask, "small": small,
        "lnp": np.stack([np.concatenate([a[f"ln{h}_g"][l], a[f"ln{h}_b"][l]]) for l in range(DEPTH) for h in (1, 2)]),
        "routw": a["router_w"].reshape(DEPTH, DC, P, EXPERTS).transpose(0, 2, 1, 3),
        "pos": np.tile(np.stack([a["nsa_cmp_pos_k"][0].T, a["nsa_cmp_pos_v"][0].T], 1), (2, 1, 1)),
        "w2": np.tile(np.stack([a["nsa_cmp_k_w2"][0], a["nsa_cmp_v_w2"][0]], 1), (2, 1, 1)),
    }


def kernel(**inputs):
    import concourse.bacc as _bacc
    from concourse.bass_utils import run_bass_kernel_spmd as _run

    arrays = {k: np.ascontiguousarray(v) for k, v in _lay_out({k: np.asarray(v) for k, v in inputs.items()}).items()}
    nc = _bacc.Bacc("TRN2", target_bir_lowering=False, num_devices=1)
    args = {k: nc.dram_tensor(f"in_{k}", v.shape, mybir.dt.float32, kind="ExternalInput").ap() for k, v in arrays.items()}
    out = nc.dram_tensor("out_0_dram", (TOK, D), mybir.dt.float32, kind="ExternalOutput").ap()
    build(nc, out=out, **args)
    r = _run(nc, [{f"in_{k}": v for k, v in arrays.items()}], core_ids=[0])
    return r.results[0]["out_0_dram"].reshape(1, TOK, D)
```
